# Optimizing a Trainium2 kernel written in Bass

```python
import math
import jax
import jax.numpy as jnp
from jax import lax
import numpy as np

D_MODEL = 2048
BATCH = 1
SEQ = 256
DEPTH = 2

CHUNK = 64
N_MIXERS = 4
DN_ALPHA = (2 * DEPTH) ** 0.25
DN_BETA = (8 * DEPTH) ** -0.25
LN_EPS = 1e-5

D_FF = int(math.ceil(8 * D_MODEL / 3 / 256)) * 256

RW_HEAD = 64
RW_HEADS = D_MODEL // RW_HEAD
RW_DECAY_LORA = max(32, int(round(1.8 * D_MODEL ** 0.5 / 32)) * 32)
RW_ICLR_LORA = RW_DECAY_LORA
RW_GATE_LORA = max(32, int(round(0.6 * D_MODEL ** 0.8 / 32)) * 32)
RW_GN_EPS = 64e-5

SSD_D_INNER = 2 * D_MODEL
SSD_HEAD = 64
SSD_HEADS = SSD_D_INNER // SSD_HEAD
SSD_GROUPS = 8
SSD_HPG = SSD_HEADS // SSD_GROUPS
SSD_STATE = 128
SSD_CONV = 4
SSD_CONV_DIM = SSD_D_INNER + 2 * SSD_GROUPS * SSD_STATE
SSD_IN_DIM = SSD_D_INNER + SSD_CONV_DIM + SSD_HEADS
SSD_NORM_GROUP = SSD_D_INNER // SSD_GROUPS

DIF_HEADS = 8
DIF_HEAD = D_MODEL // DIF_HEADS // 2
DIF_ROPE = DIF_HEAD // 4
ROPE_THETA = 500000.0
Q_BLOCK = 128
DIF_LAYER = 2
DIF_LAMBDA_INIT = 0.8 - 0.6 * math.exp(-0.3 * DIF_LAYER)

LRU_WIDTH = D_MODEL
LRU_BLOCKS = 16
LRU_BLOCK = LRU_WIDTH // LRU_BLOCKS
LRU_CONV = 4
LRU_C = 8.0

kernel_name = 'hybrid_chunk_causal_trunk'

def layer_norm(x, g, b):
    xf = x.astype(jnp.float32)
    mu = jnp.mean(xf, -1, keepdims=True)
    var = jnp.mean(jnp.square(xf - mu), -1, keepdims=True)
    return ((xf - mu) * lax.rsqrt(var + LN_EPS) * g + b).astype(x.dtype)

def rms_norm(x, g, eps):
    xf = x.astype(jnp.float32)
    return xf * lax.rsqrt(jnp.mean(xf * xf, -1, keepdims=True) + eps) * g

def causal_dwconv(x, w, b):
    k = w.shape[0]
    y = lax.conv_general_dilated(x, w[:, None, :].astype(x.dtype), window_strides=(1,),
                                 padding=[(k - 1, 0)], dimension_numbers=('NWC', 'WIO', 'NWC'),
                                 feature_group_count=x.shape[-1])
    return y + b

def rwkv7_mixer(x, mu, w_in, w0, w1, w2, a0, a1, a2, g1, g2, k_k, k_a, r_k, ln_g, ln_b, w_out):
    bsz, seq, d = x.shape
    xx = jnp.pad(x, ((0, 0), (1, 0), (0, 0)))[:, :-1] - x
    xr, xw, xk, xv, xa, xg = (x + xx * mu[j] for j in range(6))
    r = xr @ w_in[0]
    k = xk @ w_in[1]
    v = xv @ w_in[2]
    w = -jax.nn.softplus(-(w0 + jnp.tanh(xw @ w1) @ w2)) - 0.5
    a = jax.nn.sigmoid(a0 + (xa @ a1) @ a2)
    g = jax.nn.sigmoid(xg @ g1) @ g2
    heads = lambda t: t.reshape(bsz, seq, RW_HEADS, RW_HEAD).astype(jnp.float32)
    kk = heads(k * k_k)
    kk = kk / jnp.maximum(jnp.linalg.norm(kk, axis=-1, keepdims=True), 1e-12)
    k = heads(k * (1 + (a - 1) * k_a))
    r = heads(r)
    v = heads(v)
    a = heads(a)
    decay = jnp.exp(-jnp.exp(heads(w)))

    def step(state, inp):
        r_t, w_t, k_t, v_t, a_t, b_t = inp
        sa = jnp.einsum('bhij,bhj->bhi', state, a_t)
        state = (state * w_t[:, :, None, :] + sa[..., None] * b_t[:, :, None, :]
                 + v_t[..., None] * k_t[:, :, None, :])
        return state, jnp.einsum('bhij,bhj->bhi', state, r_t)

    seq_first = lambda t: jnp.swapaxes(t, 0, 1)
    s0 = jnp.zeros((bsz, RW_HEADS, RW_HEAD, RW_HEAD), jnp.float32)
    _, y = lax.scan(step, s0, tuple(seq_first(t) for t in (r, decay, k, v, -kk, kk * a)))
    y = seq_first(y)
    mu_y = jnp.mean(y, -1, keepdims=True)
    var_y = jnp.mean(jnp.square(y - mu_y), -1, keepdims=True)
    y = ((y - mu_y) * lax.rsqrt(var_y + RW_GN_EPS)).reshape(bsz, seq, d) * ln_g + ln_b
    bonus = jnp.sum(r * k * r_k, -1, keepdims=True) * v
    y = y + bonus.reshape(bsz, seq, d)
    return (y * g).astype(x.dtype) @ w_out

def ssd_mixer(x, w_in, conv_w, conv_b, dt_bias, a_log, d_skip, norm_g, w_out):
    bsz, seq, _ = x.shape
    zxbcdt = x @ w_in
    z = zxbcdt[..., :SSD_D_INNER]
    xbc = zxbcdt[..., SSD_D_INNER:SSD_D_INNER + SSD_CONV_DIM]
    dt = zxbcdt[..., SSD_D_INNER + SSD_CONV_DIM:]
    xbc = jax.nn.silu(causal_dwconv(xbc, conv_w, conv_b))
    gn = SSD_GROUPS * SSD_STATE
    xs = xbc[..., :SSD_D_INNER].reshape(bsz, seq, SSD_GROUPS, SSD_HPG, SSD_HEAD)
    bm = xbc[..., SSD_D_INNER:SSD_D_INNER + gn].reshape(bsz, seq, SSD_GROUPS, SSD_STATE).astype(jnp.float32)
    cm = xbc[..., SSD_D_INNER + gn:].reshape(bsz, seq, SSD_GROUPS, SSD_STATE).astype(jnp.float32)
    dt = jax.nn.softplus(dt.astype(jnp.float32) + dt_bias).reshape(bsz, seq, SSD_GROUPS, SSD_HPG)
    a_neg = -jnp.exp(a_log.astype(jnp.float32)).reshape(SSD_GROUPS, SSD_HPG)
    da = dt * a_neg
    xdt = xs.astype(jnp.float32) * dt[..., None]
    nc = seq // CHUNK
    to_chunks = lambda t: jnp.swapaxes(t.reshape((bsz, nc, CHUNK) + t.shape[2:]), 0, 1)
    tril = jnp.tril(jnp.ones((CHUNK, CHUNK), bool))[None, :, :, None, None]

    def step(state, inp):
        xdt_c, da_c, b_c, c_c = inp
        cs = jnp.cumsum(da_c, axis=1)
        seg = cs[:, :, None] - cs[:, None, :]
        decay = jnp.exp(jnp.where(tril, seg, -jnp.inf))
        cb = jnp.einsum('btgn,bsgn->btsg', c_c, b_c)
        y = jnp.einsum('btsg,btsgh,bsghp->btghp', cb, decay, xdt_c)
        y = y + jnp.einsum('btgn,bghpn->btghp', c_c, state) * jnp.exp(cs)[..., None]
        to_end = jnp.exp(cs[:, -1:] - cs)
        state = (state * jnp.exp(cs[:, -1])[..., None, None]
                 + jnp.einsum('bsgn,bsgh,bsghp->bghpn', b_c, to_end, xdt_c))
        return state, y

    s0 = jnp.zeros((bsz, SSD_GROUPS, SSD_HPG, SSD_HEAD, SSD_STATE), jnp.float32)
    _, y = lax.scan(step, s0, (to_chunks(xdt), to_chunks(da), to_chunks(bm), to_chunks(cm)))
    y = jnp.swapaxes(y, 0, 1).reshape(bsz, seq, SSD_GROUPS, SSD_HPG, SSD_HEAD)
    y = y + xs.astype(jnp.float32) * d_skip.reshape(SSD_GROUPS, SSD_HPG, 1)
    y = y.reshape(bsz, seq, SSD_D_INNER) * jax.nn.silu(z.astype(jnp.float32))
    y = rms_norm(y.reshape(bsz, seq, SSD_GROUPS, SSD_NORM_GROUP), norm_g.reshape(SSD_GROUPS, SSD_NORM_GROUP), 1e-5)
    return y.reshape(bsz, seq, SSD_D_INNER).astype(x.dtype) @ w_out

def partial_rotary(t, cos, sin):
    half = DIF_ROPE // 2
    t1 = t[..., :half]
    t2 = t[..., half:DIF_ROPE]
    return jnp.concatenate([t1 * cos - t2 * sin, t2 * cos + t1 * sin, t[..., DIF_ROPE:]], axis=-1)

def diff_attn_mixer(x, positions, w_in, lq1, lk1, lq2, lk2, subln_g, w_out):
    bsz, seq, d = x.shape
    qkv = x @ w_in
    q = qkv[..., :d].reshape(bsz, seq, 2 * DIF_HEADS, DIF_HEAD)
    k = qkv[..., d:2 * d].reshape(bsz, seq, 2 * DIF_HEADS, DIF_HEAD)
    v = qkv[..., 2 * d:].reshape(bsz, seq, DIF_HEADS, 2 * DIF_HEAD)
    inv_freq = ROPE_THETA ** (-jnp.arange(0, DIF_ROPE, 2, dtype=jnp.float32) / DIF_ROPE)
    ang = positions.astype(jnp.float32)[..., None] * inv_freq
    cos = jnp.cos(ang)[:, :, None, :].astype(x.dtype)
    sin = jnp.sin(ang)[:, :, None, :].astype(x.dtype)
    q = partial_rotary(q, cos, sin) * (DIF_HEAD ** -0.5)
    k = partial_rotary(k, cos, sin)
    lam = (jnp.exp(jnp.sum(lq1.astype(jnp.float32) * lk1)) - jnp.exp(jnp.sum(lq2.astype(jnp.float32) * lk2))
           + DIF_LAMBDA_INIT)
    nb = seq // Q_BLOCK
    qb = q.reshape(bsz, nb, Q_BLOCK, 2 * DIF_HEADS, DIF_HEAD).transpose(1, 0, 3, 2, 4)
    kt = k.transpose(0, 2, 1, 3)
    vt = v.transpose(0, 2, 1, 3)
    key_chunk = jnp.arange(seq) // CHUNK

    def block(args):
        q_blk, blk = args
        s = jnp.einsum('bhqd,bhkd->bhqk', q_blk, kt).astype(jnp.float32)
        q_chunk = (blk * Q_BLOCK + jnp.arange(Q_BLOCK)) // CHUNK
        s = jnp.where(key_chunk[None, :] <= q_chunk[:, None], s, -jnp.inf)
        p = jax.nn.softmax(s, axis=-1).reshape(bsz, DIF_HEADS, 2, Q_BLOCK, seq)
        attn = p[:, :, 0] - lam * p[:, :, 1]
        return jnp.einsum('bhqk,bhkd->bhqd', attn.astype(vt.dtype), vt)

    o = lax.map(block, (qb, jnp.arange(nb)))
    o = o.transpose(1, 0, 3, 2, 4).reshape(bsz, seq, DIF_HEADS, 2 * DIF_HEAD)
    o = rms_norm(o, subln_g, 1e-5) * (1.0 - DIF_LAMBDA_INIT)
    return o.reshape(bsz, seq, d).astype(x.dtype) @ w_out

def rglru_mixer(x, w_in, conv_w, conv_b, w_a, b_a, w_x, b_x, lam, w_out):
    bsz, seq, _ = x.shape
    gu = x @ w_in
    gate = jax.nn.gelu(gu[..., :LRU_WIDTH], approximate=True)
    u = causal_dwconv(gu[..., LRU_WIDTH:], conv_w, conv_b)
    ub = u.reshape(bsz, seq, LRU_BLOCKS, LRU_BLOCK)
    r = jax.nn.sigmoid(jnp.einsum('bshi,hij->bshj', ub, w_a).reshape(bsz, seq, LRU_WIDTH) + b_a)
    i = jax.nn.sigmoid(jnp.einsum('bshi,hij->bshj', ub, w_x).reshape(bsz, seq, LRU_WIDTH) + b_x)
    log_a = -LRU_C * r.astype(jnp.float32) * jax.nn.softplus(-lam.astype(jnp.float32))
    a = jnp.exp(log_a)
    b = jnp.sqrt(-jnp.expm1(2.0 * log_a)) * (i * u).astype(jnp.float32)

    def combine(left, right):
        a1, b1 = left
        a2, b2 = right
        return a1 * a2, a2 * b1 + b2

    _, h = lax.associative_scan(combine, (a, b), axis=1)
    return (gate * h.astype(x.dtype)) @ w_out

def swiglu_ffn(x, w_in, w_out):
    gu = x @ w_in
    return (jax.nn.silu(gu[..., :D_FF]) * gu[..., D_FF:]) @ w_out

def setup_inputs(seed: int = 0) -> dict:
    key = jax.random.key(seed)
    kit = iter(jax.random.split(key, 64))

    def nrm(shape, scale):
        return jax.random.normal(next(kit), shape, jnp.float32) * scale

    def uni(shape, lo, hi):
        return jax.random.uniform(next(kit), shape, jnp.float32, lo, hi)

    d = D_MODEL
    x = nrm((BATCH, SEQ, d), 1.0)
    offsets = jax.random.randint(next(kit), (BATCH, 1), 0, 1024) * CHUNK
    positions = (offsets + jnp.arange(SEQ)[None, :]).astype(jnp.int32)
    rwkv_mu = uni((6, d), 0.0, 1.0)
    rwkv_w_in = nrm((3, d, d), d ** -0.5)
    rwkv_w0 = uni((d,), -6.0, -1.0)
    rwkv_w1 = nrm((d, RW_DECAY_LORA), d ** -0.5)
    rwkv_w2 = nrm((RW_DECAY_LORA, d), 0.1 * RW_DECAY_LORA ** -0.5)
    rwkv_a0 = nrm((d,), 0.1)
    rwkv_a1 = nrm((d, RW_ICLR_LORA), d ** -0.5)
    rwkv_a2 = nrm((RW_ICLR_LORA, d), 0.1 * RW_ICLR_LORA ** -0.5)
    rwkv_g1 = nrm((d, RW_GATE_LORA), d ** -0.5)
    rwkv_g2 = nrm((RW_GATE_LORA, d), RW_GATE_LORA ** -0.5)
    rwkv_k_k = 0.85 + nrm((d,), 0.02)
    rwkv_k_a = 1.0 + nrm((d,), 0.02)
    rwkv_r_k = nrm((RW_HEADS, RW_HEAD), 0.1)
    rwkv_ln_g = 1.0 + nrm((d,), 0.02)
    rwkv_ln_b = nrm((d,), 0.02)
    rwkv_w_out = nrm((d, d), d ** -0.5 * DN_BETA)
    ssd_w_in = nrm((d, SSD_IN_DIM), d ** -0.5)
    ssd_conv_w = nrm((SSD_CONV, SSD_CONV_DIM), SSD_CONV ** -0.5)
    ssd_conv_b = nrm((SSD_CONV_DIM,), 0.02)
    dt0 = jnp.exp(uni((SSD_HEADS,), math.log(1e-3), math.log(1e-1)))
    ssd_dt_bias = dt0 + jnp.log(-jnp.expm1(-dt0))
    ssd_a_log = jnp.log(uni((SSD_HEADS,), 1.0, 16.0))
    ssd_d = 1.0 + nrm((SSD_HEADS,), 0.02)
    ssd_norm_g = 1.0 + nrm((SSD_D_INNER,), 0.02)
    ssd_w_out = nrm((SSD_D_INNER, d), SSD_D_INNER ** -0.5 * DN_BETA)
    dif_w_in = nrm((d, 3 * d), d ** -0.5)
    dif_lq1 = nrm((DIF_HEAD,), 0.1)
    dif_lk1 = nrm((DIF_HEAD,), 0.1)
    dif_lq2 = nrm((DIF_HEAD,), 0.1)
    dif_lk2 = nrm((DIF_HEAD,), 0.1)
    dif_subln_g = 1.0 + nrm((2 * DIF_HEAD,), 0.02)
    dif_w_out = nrm((d, d), d ** -0.5 * DN_BETA)
    lru_w_in = nrm((d, 2 * LRU_WIDTH), d ** -0.5)
    lru_conv_w = nrm((LRU_CONV, LRU_WIDTH), LRU_CONV ** -0.5)
    lru_conv_b = nrm((LRU_WIDTH,), 0.02)
    lru_w_a = nrm((LRU_BLOCKS, LRU_BLOCK, LRU_BLOCK), LRU_BLOCK ** -0.5)
    lru_b_a = nrm((LRU_WIDTH,), 0.02)
    lru_w_x = nrm((LRU_BLOCKS, LRU_BLOCK, LRU_BLOCK), LRU_BLOCK ** -0.5)
    lru_b_x = nrm((LRU_WIDTH,), 0.02)
    a_init = uni((LRU_WIDTH,), 0.9, 0.999)
    lru_lam = jnp.log(a_init) - jnp.log1p(-a_init)
    lru_w_out = nrm((LRU_WIDTH, d), LRU_WIDTH ** -0.5 * DN_BETA)
    ffn_w_in = nrm((DEPTH, d, 2 * D_FF), d ** -0.5)
    ffn_w_out = nrm((DEPTH, D_FF, d), D_FF ** -0.5 * DN_BETA)
    ln_g = 1.0 + nrm((DEPTH, 2, d), 0.02)
    ln_b = nrm((DEPTH, 2, d), 0.02)
    return {'x': x, 'positions': positions,
            'rwkv_mu': rwkv_mu, 'rwkv_w_in': rwkv_w_in, 'rwkv_w0': rwkv_w0, 'rwkv_w1': rwkv_w1,
            'rwkv_w2': rwkv_w2, 'rwkv_a0': rwkv_a0, 'rwkv_a1': rwkv_a1, 'rwkv_a2': rwkv_a2,
            'rwkv_g1': rwkv_g1, 'rwkv_g2': rwkv_g2, 'rwkv_k_k': rwkv_k_k, 'rwkv_k_a': rwkv_k_a,
            'rwkv_r_k': rwkv_r_k, 'rwkv_ln_g': rwkv_ln_g, 'rwkv_ln_b': rwkv_ln_b, 'rwkv_w_out': rwkv_w_out,
            'ssd_w_in': ssd_w_in, 'ssd_conv_w': ssd_conv_w, 'ssd_conv_b': ssd_conv_b,
            'ssd_dt_bias': ssd_dt_bias, 'ssd_a_log': ssd_a_log, 'ssd_d': ssd_d,
            'ssd_norm_g': ssd_norm_g, 'ssd_w_out': ssd_w_out,
            'dif_w_in': dif_w_in, 'dif_lq1': dif_lq1, 'dif_lk1': dif_lk1, 'dif_lq2': dif_lq2,
            'dif_lk2': dif_lk2, 'dif_subln_g': dif_subln_g, 'dif_w_out': dif_w_out,
            'lru_w_in': lru_w_in, 'lru_conv_w': lru_conv_w, 'lru_conv_b': lru_conv_b,
            'lru_w_a': lru_w_a, 'lru_b_a': lru_b_a, 'lru_w_x': lru_w_x, 'lru_b_x': lru_b_x,
            'lru_lam': lru_lam, 'lru_w_out': lru_w_out,
            'ffn_w_in': ffn_w_in, 'ffn_w_out': ffn_w_out, 'ln_g': ln_g, 'ln_b': ln_b}

def reference(x, positions,
              rwkv_mu, rwkv_w_in, rwkv_w0, rwkv_w1, rwkv_w2, rwkv_a0, rwkv_a1, rwkv_a2,
              rwkv_g1, rwkv_g2, rwkv_k_k, rwkv_k_a, rwkv_r_k, rwkv_ln_g, rwkv_ln_b, rwkv_w_out,
              ssd_w_in, ssd_conv_w, ssd_conv_b, ssd_dt_bias, ssd_a_log, ssd_d, ssd_norm_g, ssd_w_out,
              dif_w_in, dif_lq1, dif_lk1, dif_lq2, dif_lk2, dif_subln_g, dif_w_out,
              lru_w_in, lru_conv_w, lru_conv_b, lru_w_a, lru_b_a, lru_w_x, lru_b_x, lru_lam, lru_w_out,
              ffn_w_in, ffn_w_out, ln_g, ln_b):
    h = x
    for i in range(DEPTH):
        m = i % N_MIXERS
        if m == 0:
            y = rwkv7_mixer(h, rwkv_mu, rwkv_w_in, rwkv_w0, rwkv_w1, rwkv_w2, rwkv_a0, rwkv_a1, rwkv_a2,
                            rwkv_g1, rwkv_g2, rwkv_k_k, rwkv_k_a, rwkv_r_k, rwkv_ln_g, rwkv_ln_b, rwkv_w_out)
        elif m == 1:
            y = ssd_mixer(h, ssd_w_in, ssd_conv_w, ssd_conv_b, ssd_dt_bias, ssd_a_log, ssd_d,
                          ssd_norm_g, ssd_w_out)
        elif m == 2:
            y = diff_attn_mixer(h, positions, dif_w_in, dif_lq1, dif_lk1, dif_lq2, dif_lk2,
                                dif_subln_g, dif_w_out)
        else:
            y = rglru_mixer(h, lru_w_in, lru_conv_w, lru_conv_b, lru_w_a, lru_b_a, lru_w_x, lru_b_x,
                            lru_lam, lru_w_out)
        h = layer_norm(DN_ALPHA * h + y, ln_g[i, 0], ln_b[i, 0])
        h = layer_norm(DN_ALPHA * h + swiglu_ffn(h, ffn_w_in[i], ffn_w_out[i]), ln_g[i, 1], ln_b[i, 1])
    return h


_drawn_inputs = setup_inputs


def setup_inputs(seed=0):
    import zlib

    import numpy as np

    out = dict(_drawn_inputs(seed))
    spreads = {}
    factors = {'rwkv_w1': 8.0,
     'rwkv_w2': 8.0,
     'rwkv_a0': 6.073,
     'rwkv_a1': 6.459,
     'rwkv_a2': 6.473,
     'rwkv_k_k': 8.0,
     'rwkv_k_a': 8.0,
     'rwkv_ln_g': 8.0,
     'rwkv_ln_b': 8.0,
     'ssd_conv_b': 6.046,
     'ssd_d': 8.0,
     'ssd_norm_g': 8.0}
    for name, (base, spread) in spreads.items():
        noise = np.random.default_rng([zlib.crc32(name.encode()), seed]).standard_normal(out[name].shape)
        drawn = base * np.exp(spread * noise) if base else spread * noise
        out[name] = jnp.asarray(drawn.astype(out[name].dtype))
    for name, factor in factors.items():
        out[name] = (out[name] * factor).astype(out[name].dtype)
    return out
```

```python
import math
from contextlib import ExitStack

import concourse.bass as bass
from concourse import mybir

F32 = mybir.dt.float32
F32R = mybir.dt.float32r
ALU = mybir.AluOpType
ACT = mybir.ActivationFunctionType

P = 128
T = 256
D = 2048
KT = D // P
DEPTH = 2
ALPHA = (2 * DEPTH) ** 0.25
LN_EPS = 1e-5
GN_EPS = 64e-5
RMS_EPS = 1e-5
DECAY = math.exp(-0.5)
LORA = 96
NF = 44
NX = 32
HEADS = 64
GROUPS = 8
RAW, SPLIT = 4, 2

PARAM_TILES = [("mu", 6 * KT), ("w0", KT), ("a0", KT), ("k_k", KT), ("k_a", KT), ("r_k", KT), ("gn_g", KT),
               ("gn_b", KT), ("conv_w", 4 * 48), ("conv_b", 48), ("norm_g", NX), ("d_skip", NX), ("ln_g", 4 * KT),
               ("ln_b", 4 * KT), ("dt_bias", 1), ("a_log", 1)]
PARAM_AT = {}
NPARAM = 0
for _name, _n in PARAM_TILES:
    PARAM_AT[_name] = NPARAM
    NPARAM += _n

N_BASIC, N_SSD = 3 * P, 3 * P
CREDIT = 1
LEVELS = (2, 4, 8, 16, 32, 64)


def shape_constants():
    import numpy as np
    row, col = np.arange(P)[:, None], np.arange(P)[None, :]
    level = lambda m: ((row // m) % 2 == 1) & (col // m == row // m - 1)
    basic = [row == col, row // 64 == col // 64, row >= 0 * col]
    chunk = [row < col, row <= col, level(1), level(1).T] + [level(m) for m in LEVELS]
    ssd = [row <= col, row >= 0 * col, row <= col]
    wide = lambda parts: np.concatenate([np.broadcast_to(m, (P, P)).astype(np.float32) for m in parts], axis=1)
    return wide(basic), wide(chunk), wide(ssd)


class Phase:

    def __init__(self, name, src, outs, per, tiles, width, unroll):
        self.name, self.src, self.outs, self.per, self.tiles, self.width, self.unroll = (
            name, src, outs, per, tiles, width, unroll)
        self.slabs = outs * per
        self.cols = tiles * width
        self.slab0 = self.out0 = 0


def loop(eng, n, body):
    if n == 1:
        body(0)
    elif n > 1:
        with eng.Fori(0, n) as k:
            body(k)


def build(nc, inp, out, debug=None):
    ctx = ExitStack()
    with ctx:
        sems = {}

        def S(name):
            if name not in sems:
                sems[name] = ctx.enter_context(nc.semaphore(name))
            return sems[name]

        KB = 1024
        at = [16512]

        def place(nbytes):
            here = at[0]
            at[0] += nbytes
            return here

        def sb(name, shape, dt, offset):
            return nc.alloc_sbuf_tensor_at(name, shape, dt, offset=offset)

        basic = sb("basic", [P, N_BASIC], F32, place(4 * N_BASIC))
        par = sb("par", [P, NPARAM, 1], F32, place((4 * NPARAM + 31) // 32 * 32))
        omm = sb("omm", [P, 6 * KT, 1], F32, place(4 * 6 * KT))
        omka = sb("omka", [P, KT, 1], F32, place(4 * KT))
        eps = sb("eps", [P, 4, 1], F32, place(32))
        raw = sb("raw", [P, RAW, D], F32, place(RAW * 8 * KB))
        wsp = sb("wsp", [P, SPLIT, 2, D], F32R, place(SPLIT * 16 * KB))
        H = sb("H", [P, KT, T], F32, place(16 * KB))
        xs_at = place(32 * KB)
        big_at = place(88 * KB)
        tmp_at = place(3 * KB)
        assert at[0] <= 229344, at
        XS = sb("XS", [P, 2, KT, T], F32R, xs_at)
        tmp = sb("tmp", [P, 3, T], F32, tmp_at)
        ident, bones, ones = (basic[:, i * P:(i + 1) * P] for i in range(3))

        def param(name, i):
            return par[:, PARAM_AT[name] + i, :]

        R = sb("R", [P, KT, T], F32, big_at)
        K = sb("K", [P, KT, T], F32, big_at + 16 * KB)
        V = sb("V", [P, KT, T], F32, big_at + 32 * KB)
        XS2 = sb("XS2", [P, 2, KT, T], F32R, big_at + 48 * KB)
        lo_w = sb("lo_w", [P, T], F32, big_at + 80 * KB)
        lo_a = sb("lo_a", [P, T], F32, big_at + 81 * KB)
        lo_g = sb("lo_g", [P, 2, T], F32, big_at + 82 * KB)
        YR = sb("YR", [P, 2, KT, T], F32R, big_at)

        ct = [big_at + 48 * KB]

        def core(name, shape, dt=F32):
            n = 4
            for s in shape[1:]:
                n *= s
            here = ct[0]
            ct[0] += (n + 31) // 32 * 32
            return sb(name, shape, dt, here)

        LM1 = [core(f"LM1_{g}", [P, 4, 2 * P]) for g in range(2)]
        LM2 = [core(f"LM2_{g}", [P, 4, 2 * P]) for g in range(2)]
        XI = [core(f"XI_{g}", [P, 4, P]) for g in range(2)]
        TI = [core(f"TI_{g}", [P, 4, P]) for g in range(2)]
        UI = [core(f"UI_{g}", [P, 4, P]) for g in range(2)]
        S0 = [sb(f"S0_{g}", [P, 64], F32, tmp_at + 256 * (g + 1)) for g in range(2)]
        assert ct[0] <= big_at + 76 * KB, ct
        ct = [big_at + 84 * KB]
        RH = [core(f"RH_{g}", [P, 4, 64]) for g in range(2)]
        SA = [core(f"SA_{g}", [P, 4, 64]) for g in range(2)]
        assert ct[0] <= big_at + 88 * KB
        ct = [xs_at]
        LW, TOK, SG, K2, AA, BV, GG, SC, EE, EI, KK, YY, VS, YC, AR, BT, KW, SQ = ([] for _ in range(18))
        for g in range(2):
            LW.append(sb(f"LW_{g}", [P, 4, P], F32, ct[0]))
            TOK.append(core(f"TOK_{g}", [P, 4, P]))
            SG.append(sb(f"SG_{g}", [P, T], F32, ct[0]))
            K2.append(core(f"K2_{g}", [P, 2, P]))
            AA.append(sb(f"AA_{g}", [P, T], F32, ct[0]))
            BV.append(core(f"BV_{g}", [P, T]))
            GG.append(core(f"GG_{g}", [P, T]))
            SC.append(core(f"SC_{g}", [P, 2, P + 1]))
            EE.append(core(f"EE_{g}", [P, 2, P + 1]))
            EI.append(core(f"EI_{g}", [P, 2, P + 1]))
            KK.append(sb(f"KK_{g}", [P, 2, P], F32, ct[0]))
            YY.append(core(f"YY_{g}", [P, T]))
            VS.append(sb(f"VS_{g}", [P, T], F32, ct[0]))
            YC.append(core(f"YC_{g}", [P, T]))
            AR.append(core(f"AR_{g}", [P, 2, 2, P]))
            BT.append(core(f"BT_{g}", [P, 2, P]))
            KW.append(core(f"KW_{g}", [P, 2, P]))
            SQ.append(core(f"SQ_{g}", [P, 2, P]))
        assert ct[0] <= xs_at + 32 * KB, ct
        level_mask = sb("level_mask", [P, len(LEVELS), P], F32, big_at + 76 * KB)
        pair_mask = sb("pair_mask", [P, 2 * P], F32, tmp_at + KB)
        first_mask = sb("first_mask", [P, 2, P], F32, tmp_at + 2 * KB)
        kb = sb("kb", [P, 2, 2, 2], F32, tmp_at)
        dsc = sb("dsc", [P, 2, 1], F32, tmp_at + 64)

        HID = sb("HID", [P, 2, NF, T], F32R, big_at)

        XC = sb("XC", [P, NX, T], F32, big_at)
        Z = sb("Z", [P, NX, T], F32, big_at + 32 * KB)
        BC = sb("BC", [P, 2 * GROUPS, T], F32, big_at + 64 * KB)
        YS = sb("YS", [P, 2, NX, T], F32R, big_at)
        dtt = sb("dtt", [P, 2, HEADS, 1], F32, big_at + 80 * KB)
        ncs = sb("ncs", [P, 2, HEADS, 1], F32, big_at + 80 * KB + 512)
        dtc = sb("dtc", [HEADS, T], F32, big_at + 81 * KB)
        cs = sb("cs", [HEADS, T], F32, big_at + 82 * KB)
        dta = sb("dta", [HEADS, T], F32, big_at + 83 * KB)
        dtb = sb("dtb", [HEADS, T], F32, big_at + 84 * KB)
        aneg = sb("aneg", [HEADS, 2], F32, big_at + 85 * KB)
        smask = sb("smask", [P, N_SSD], F32, big_at + 86 * KB)
        ct = [xs_at]
        CSB = core("CSB", [P, 8, T])
        XST = core("XST", [P, 4, T])
        BST = core("BST", [P, T])
        CBM = core("CBM", [P, 3 * P])
        XDT = core("XDT", [P, 2, 8, 64])
        SEG = [core(f"SEG_{i}", [P, 3 * P]) for i in range(2)]
        GE = [core(f"GE_{i}", [P, 3 * P]) for i in range(2)]
        YG = core("YG", [P, 4, T])
        SQS = core("SQS", [P, T])
        RST = core("RST", [P, T])
        assert ct[0] <= xs_at + 32 * KB, (ct, xs_at)
        cs_dram = nc.dram_tensor("cs_scratch", (HEADS, T), F32, kind="Internal").ap()

        bank = [nc.alloc_psum_tensor(f"bank{i}", [P, 512], F32) for i in range(8)]
        phases = [
            Phase("r", inp["w_r"], 16, 1, 16, P, 4),
            Phase("w1", inp["w_w1"], 1, 1, 16, LORA, 4),
            Phase("k", inp["w_k"], 16, 1, 16, P, 4),
            Phase("a1", inp["w_a1"], 1, 1, 16, LORA, 4),
            Phase("v", inp["w_v"], 16, 1, 16, P, 4),
            Phase("g1", inp["w_g1"], 2, 1, 16, P, 4),
            Phase("wo", inp["w_ro"], 16, 1, 16, P, 4),
            Phase("up0", inp["w_up0"], 88, 1, 16, P, 4),
            Phase("down0", inp["w_down0"], 16, 4, 11, P, 2),
            Phase("x", inp["w_x"], NX, 1, 16, P, 4),
            Phase("bc", inp["w_bc"], 2 * GROUPS, 1, 16, P, 4),
            Phase("z", inp["w_z"], 32, 1, 16, P, 4),
            Phase("dt", inp["w_dt"], 1, 1, 16, HEADS, 4),
            Phase("so", inp["w_so"], 16, 2, 16, P, 4),
            Phase("up1", inp["w_up1"], 88, 1, 16, P, 4),
            Phase("down1", inp["w_down1"], 16, 4, 11, P, 2),
        ]
        by = {}
        s = o = 0
        for ph in phases:
            ph.slab0, ph.out0 = s, o
            s, o = s + ph.slabs, o + ph.outs
            by[ph.name] = ph
        n_slabs = s
        owner = [ph for ph in phases for _ in range(ph.slabs)]

        landed = [S(f"slab_landed{i}") for i in range(RAW)]
        high_ready, low_ready, slab_done = S("high_ready"), S("low_ready"), S("slab_done")
        bank_free = [S("bank0_free"), S("bank1_free")]

        def run_phase(eng, ph, prepare, take):
            turn = ph.unroll * ph.per
            n = max(0, (ph.slabs - 2) // turn)

            def body(k):
                for j in range(ph.unroll):
                    for q in range(ph.per):
                        prepare(ph, ph.slab0 + j * ph.per + q + 2, k, turn)
                    take(ph, j, k, ph.unroll)

            loop(eng, n, body)
            for j in range(n * ph.unroll, ph.outs):
                for q in range(ph.per):
                    s = ph.slab0 + j * ph.per + q + 2
                    if s < n_slabs:
                        prepare(owner[s], s, 0, 0)
                take(ph, j, 0, 0)

        def lands(s, k, turn):
            return landed[s % RAW], 16 * (s // RAW + 1) + k * (16 * turn // RAW)

        def out_wait(eng, ph, j, k, u):
            eng.wait_ge(slab_done, ph.slab0 + (j + 1) * ph.per + k * (u * ph.per))

        def out_bank(ph, j):
            return bank[(ph.out0 + j) % 2][:ph.width, 0:T]

        def free_sem(ph, j):
            return bank_free[(ph.out0 + j) % 2]

        def freed(ph, j, k, u):
            return (ph.out0 + j) // 2 + 1 + k * (u // 2) + CREDIT

        block = ctx.enter_context(nc.Block())

        SHIFT_MU = [0, 1, 2, 4, 3, 5]
        SHIFT_PH = ["r", "w1", "k", "a1", "v", "g1"]

        def shift_buf(i):
            return (XS, XS2)[i % 2]

        @block.sync
        def _(sp):
            def load(ph, s, k, turn):
                if s >= RAW:
                    sp.wait_ge(low_ready, s - RAW + 1 + k * turn)
                sem, _n = lands(s, k, turn)
                sp.dma_start(raw[:, s % RAW, 0:ph.cols], ph.src[s - ph.slab0 + k * turn]).then_inc(sem, 16)

            sp.dma_start(H[:, :, :], inp["x_cm"]).then_inc(S("x_landed"), 16)
            sp.dma_start(par[:, :, 0], inp["params"]).then_inc(S("par_landed"), 16)
            for s in range(RAW):
                load(owner[s], s, 0, 0)
            sp.dma_start(basic[:, :], inp["basic"]).then_inc(S("basic_landed"), 16)
            for ph in phases:
                first = ph.slab0 if ph.slab0 else RAW
                n = (ph.slab0 + ph.slabs - first) // 4

                def body(k):
                    for j in range(4):
                        load(ph, first + j, k, 4)

                loop(sp, n, body)
                for s in range(first + 4 * n, ph.slab0 + ph.slabs):
                    load(ph, s, 0, 0)
            for n in range(KT):
                sp.wait_ge(S("ln_affine"), 3 * KT + n + 1)
                sp.dma_start(out[:, n, :], H[:, n, :]).then_inc(S("out_stored"), 16)
            sp.wait_ge(S("out_stored"), 16 * KT)

        @block.scalar
        def _(act):
            def apart():
                act.wait_ge(S("par_landed"), 16)

            def prepare(ph, s, k, turn):
                act.wait_ge(*lands(s, k, turn))
                if s >= 2:
                    act.wait_ge(slab_done, s - 1 + k * turn)
                act.activation(wsp[:, s % 2, 0, 0:ph.cols], raw[:, s % RAW, 0:ph.cols],
                               ACT.Copy).then_inc(high_ready, 1)

            def shift_high(i):
                buf = shift_buf(i)
                if i >= 2:
                    last = by[SHIFT_PH[i - 2]]
                    act.wait_ge(slab_done, last.slab0 + last.slabs)

                def body(k):
                    for j in range(2):
                        act.wait_ge(S("mixed"), KT * i + j + 1 + 2 * k)
                        apart()
                        act.activation(buf[:, 0, 2 * k + j, :], tmp[:, j, :], ACT.Copy).then_inc(S("shift_high"), 1)

                loop(act, KT // 2, body)

            def take_copy(dst, func=ACT.Copy):
                def take(ph, j, k, u):
                    out_wait(act, ph, j, k, u)
                    apart()
                    act.activation(dst(j + k * u), out_bank(ph, j), func).then_inc(free_sem(ph, j), 1)
                return take

            def take_up(layer):
                def take(ph, j, k, u):
                    n = j // 2 + k * (u // 2)
                    if j % 2 == 0:
                        out_wait(act, ph, j, k, u)
                        act.wait_ge(free_sem(ph, 1), (ph.out0 + 1) // 2 + n + CREDIT)
                        act.activation(tmp[:, 0, :], out_bank(ph, j), ACT.Silu).then_inc(free_sem(ph, j), 1)
                    else:
                        act.wait_ge(free_sem(ph, 1), (ph.out0 + 1) // 2 + n + 1 + CREDIT)
                        apart()
                        act.activation(HID[:, 0, n, :], tmp[:, 1 + (j // 2) % 2, :], ACT.Copy).then_inc(S("hid_high"), 1)
                return take

            def nothing(ph, j, k, u):
                pass

            def layer_norm(i):
                for j in range(2):
                    act.wait_ge(S("ln_centred"), KT * i + j + 1)
                    apart()
                    act.activation(tmp[:, 1 + j, :], H[:, j, :], ACT.Square).then_inc(S("ln_sq"), 1)

                def rest(k):
                    for j in range(2):
                        act.wait_ge(S("ln_centred"), KT * i + 2 * k + j + 3)
                        act.wait_ge(S("ln_sqsum"), KT * i + 2 * k + j + 1)
                        apart()
                        act.activation(tmp[:, 1 + j, :], H[:, 2 * k + 2 + j, :], ACT.Square).then_inc(S("ln_sq"), 1)

                loop(act, KT // 2 - 1, rest)
                act.wait_ge(S("ln_sqsum"), KT * (i + 1))
                act.activation(tmp[:, 0, :], bank[3][:, 0:T], ACT.Sqrt, scale=1.0 / D,
                               bias=eps[:, 0, :]).then_inc(S("ln_std"), 1)

                def affine(n):
                    act.wait_ge(S("ln_scaled"), KT * i + n + 1)
                    apart()
                    act.activation(H[:, n, :], H[:, n, :], ACT.Identity, scale=param("ln_g", KT * i + n),
                                   bias=param("ln_b", KT * i + n)).then_inc(S("ln_affine"), 1)

                def high(n):
                    act.wait_ge(S("ln_affine"), KT * i + n + 1)
                    apart()
                    act.activation(XS[:, 0, n, :], H[:, n, :], ACT.Copy).then_inc(S("ln_high"), 1)

                affine(0)

                def body(k):
                    affine(k + 1)
                    if i < 3:
                        high(k)

                loop(act, KT - 1, body)
                if i < 3:
                    high(KT - 1)

            def take_conv(tile0, dst):
                def take(ph, j, k, u):
                    n = j + k * u
                    out_wait(act, ph, j, k, u)
                    apart()
                    act.activation(tmp[:, j % 2, :], out_bank(ph, j), ACT.Identity, scale=param("conv_w", 3 * 48 + tile0 + n),
                                   bias=param("conv_b", tile0 + n)).then_inc(S("conv_begun"), 1)
                    act.wait_ge(free_sem(ph, j), freed(ph, j, k, u))
                    apart()
                    act.activation(dst(n), tmp[:, j % 2, :], ACT.Silu).then_inc(S("conv_done"), 1)
                return take

            def take_dt(ph, j, k, u):
                out_wait(act, ph, j, k, u)
                act.activation(dta[:, :], out_bank(ph, j), ACT.Abs,
                               bias=par[0:HEADS, PARAM_AT["dt_bias"], :]).then_inc(S("dt_abs"), 1)
                act.activation(aneg[:, 0:1], par[0:HEADS, PARAM_AT["a_log"], :], ACT.Exp).then_inc(S("dt_rate"), 1)
                act.wait_ge(S("dt_abs"), 1)
                act.activation(dtb[:, :], dta[:, :], ACT.Exp, scale=-1.0).then_inc(S("dt_exp"), 1)
                act.wait_ge(S("dt_exp"), 1)
                act.activation(dtb[:, :], dtb[:, :], ACT.Ln, bias=eps[0:HEADS, 3, :]).then_inc(S("dt_ln"), 1)
                act.wait_ge(S("cs_ready"), 1)
                act.dma_start(cs_dram, cs[:, :]).then_inc(S("cs_stored"), 16)
                act.wait_ge(S("dt_turned"), 1)
                act.activation(dtt[:, :, :, 0], bank[2][:, 0:2 * HEADS].rearrange("p (c h) -> p c h", c=2),
                               ACT.Copy).then_inc(S("dt_tokens"), 1)
                act.activation(ncs[:, :, :, 0], bank[2][:, 2 * HEADS:4 * HEADS].rearrange("p (c h) -> p c h", c=2),
                               ACT.Copy, scale=-1.0).then_inc(S("dt_tokens"), 1)

            def delta_rule():
                act.wait_ge(slab_done, by["wo"].slab0)
                act.wait_ge(S("shift_low"), 6 * KT + CREDIT)
                act.dma_start(level_mask[:, :, :], inp["level_mask"]).then_inc(S("mask_landed"), 16)
                act.dma_start(pair_mask[:, :], inp["pair_mask"]).then_inc(S("mask_landed"), 16)
                act.dma_start(first_mask[:, :, :], inp["first_mask"]).then_inc(S("mask_landed"), 16)

                def body(k):
                    for g in range(2):
                        n = 2 * k + g
                        act.wait_ge(S("y_low"), 2 * k + CREDIT)
                        act.dma_start(LW[g][:, :, :], inp["lora2"][n]).then_inc(S(f"lora_landed{g}"), 16)
                        act.dma_start(VS[g][:, :], V[:, n, :]).then_inc(S(f"v_landed{g}"), 16)
                    for g in range(2):
                        n = 2 * k + g
                        apart()
                        act.activation(SQ[g][:, :, :].rearrange("p a b -> p (a b)"), K[:, n, :], ACT.Square,
                                       scale=param("k_k", n)).then_inc(S("key_sq"), 1)
                    for g in range(2):
                        act.wait_ge(S("norm_mm"), 2 * k + g + 1)
                        act.activation(SQ[g][:, :, :].rearrange("p a b -> p (a b)"), bank[4 * g + 2][:, 0:T],
                                       ACT.Sqrt).then_inc(S("norm_ready"), 1)
                    for g in range(2):
                        n = 2 * k + g
                        act.wait_ge(S("lora_mm"), 2 * k + g + 1)
                        apart()
                        act.activation(SG[g][:, :], bank[4 * g][:, 0:T], ACT.Sigmoid,
                                       bias=param("w0", n)).then_inc(S("decay_gate"), 1)
                        apart()
                        act.activation(AA[g][:, :], bank[4 * g][:, T:2 * T], ACT.Sigmoid,
                                       bias=param("a0", n)).then_inc(S("rate_gate"), 1)
                        act.activation(GG[g][:, :], bank[4 * g + 1][:, 0:T], ACT.Copy).then_inc(S("gate_ready"), 1)
                    for g in range(2):
                        act.wait_ge(S("mid_ready"), 4 * k + 2 * g + 2)
                        for c in range(2):
                            act.activation(EE[g][:, c, :], SC[g][:, c, :], ACT.Exp, scale=-DECAY,
                                           bias=kb[:, g, 0, c:c + 1]).then_inc(S("decayed"), 1)
                            act.activation(EI[g][:, c, :], SC[g][:, c, :], ACT.Exp, scale=DECAY,
                                           bias=kb[:, g, 1, c:c + 1]).then_inc(S("decayed"), 1)
                    for g in range(2):
                        act.wait_ge(S("turned"), 2 * k + g + 1)
                        act.activation(TOK[g][:, :, :].rearrange("p a b -> p (a b)"), bank[4 * g + 3][:, :],
                                       ACT.Copy).then_inc(S("token_major"), 1)
                    for c in range(2):
                        for g in range(2):
                            act.wait_ge(S("rhs_mm"), 4 * k + 2 * c + g + 1)
                            if c == 0:
                                act.activation(RH[g][:, 0:2, :], bank[4 * g + 3][:, 0:P].rearrange(
                                    "p (a b) -> p a b", a=2), ACT.Copy).then_inc(S("rhs_ready"), 1)
                            else:
                                for h in range(2):
                                    act.activation(RH[g][:, 2 + h, :], bank[4 * g + 3 - h][:, P + 64 * h:P + 64 * h + 64],
                                                   ACT.Copy).then_inc(S("rhs_ready"), 1)
                        for g in range(2):
                            act.wait_ge(S("sa_mm"), 4 * k + 2 * c + g + 1)
                            act.activation(SA[g][:, 2 * c:2 * c + 2, :], bank[4 * g][:, 128 * c:128 * c + 128].rearrange(
                                "p (a b) -> p a b", a=2), ACT.Copy).then_inc(S("sa_ready"), 1)
                    for g in range(2):
                        act.wait_ge(S("y_mm"), 4 * k + g + 3)
                        act.activation(YY[g][:, :], bank[4 * g + 1][:, 0:T], ACT.Copy).then_inc(S("y_ready"), 1)
                    for g in range(2):
                        act.wait_ge(S("y_centred"), 2 * k + g + 1)
                        act.activation(SQ[g][:, :, :].rearrange("p a b -> p (a b)"), YC[g][:, :],
                                       ACT.Square).then_inc(S("y_sq"), 1)
                    for g in range(2):
                        act.wait_ge(S("y_var_mm"), 2 * k + g + 1)
                        act.activation(YY[g][:, :], bank[4 * g][:, 0:T], ACT.Sqrt, scale=1.0 / 64,
                                       bias=eps[:, 1, :]).then_inc(S("y_std"), 1)
                    for g in range(2):
                        act.wait_ge(S("y_gated"), 2 * k + g + 1)
                        apart()
                        act.activation(YR[:, 0, 2 * k + g, :], YC[g][:, :], ACT.Copy).then_inc(S("y_high"), 1)

                loop(act, KT // 2, body)

            def ssd():
                act.wait_ge(slab_done, by["so"].slab0)
                act.wait_ge(S("cs_stored"), 16)

                def body(k):
                    act.wait_ge(S("ys_low"), 4 * k + CREDIT)
                    act.dma_start(CSB[:, :, :], cs_dram.rearrange("(g h) t -> g h t", h=8)[k].partition_broadcast(P)
                                  ).then_inc(S("csb_landed"), 16)
                    act.dma_start(XST[:, :, :].rearrange("p a b -> p (a b)"), XC[:, :, :].rearrange("p (g a) t -> p g (a t)", g=GROUPS)[:, k, :]).then_inc(
                        S("xst_landed"), 16)
                    act.dma_start(BST[:, :], BC[:, k, :]).then_inc(S("bst_landed"), 16)
                    for h in range(8):
                        act.wait_ge(S("seg_ready"), 16 * k + 2 * h + 2)
                        if h >= 2:
                            act.wait_ge(S("ssd_y_mm"), 8 * k + h - 1)
                        act.activation(GE[h % 2][:, :], SEG[h % 2][:, :], ACT.Exp).then_inc(S("ge_ready"), 1)
                    for t in range(4):
                        act.wait_ge(S("ys_gated"), 4 * k + t + 1)
                        if t:
                            act.wait_ge(S("ys_sq_mm"), 4 * k + t)
                        act.activation(SQS[:, :], YG[:, t, :], ACT.Square).then_inc(S("ys_sq"), 1)
                    act.wait_ge(S("ys_sq_mm"), 4 * k + 4)
                    act.activation(RST[:, :], bank[7][:, 0:T], ACT.Sqrt, scale=1.0 / 512,
                                   bias=eps[:, 2, :]).then_inc(S("ys_std"), 1)
                    for t in range(4):
                        act.wait_ge(S("ys_normed"), 4 * k + t + 1)
                        apart()
                        act.activation(YS[:, 0, 4 * k + t, :], YG[:, t, :], ACT.Copy).then_inc(S("ys_high"), 1)

                loop(act, GROUPS, body)

            act.wait_ge(S("par_landed"), 16)
            prepare(by["r"], 0, 0, 0)
            prepare(by["r"], 1, 0, 0)
            shift_high(0)
            shift_high(1)
            run_phase(act, by["r"], prepare, take_copy(lambda n: R[:, n, :]))
            shift_high(2)
            run_phase(act, by["w1"], prepare, take_copy(lambda n: lo_w[0:LORA, :], ACT.Tanh))
            shift_high(3)
            run_phase(act, by["k"], prepare, take_copy(lambda n: K[:, n, :]))
            shift_high(4)
            run_phase(act, by["a1"], prepare, take_copy(lambda n: lo_a[0:LORA, :]))
            shift_high(5)
            run_phase(act, by["v"], prepare, take_copy(lambda n: V[:, n, :]))
            run_phase(act, by["g1"], prepare, take_copy(lambda n: lo_g[:, n, :], ACT.Sigmoid))
            delta_rule()
            run_phase(act, by["wo"], prepare, nothing)
            layer_norm(0)
            run_phase(act, by["up0"], prepare, take_up(0))
            run_phase(act, by["down0"], prepare, nothing)
            layer_norm(1)
            act.dma_start(smask[:, :], inp["ssd_mask"]).then_inc(S("smask_landed"), 16)
            run_phase(act, by["x"], prepare, take_conv(0, lambda n: XC[:, n, :]))
            run_phase(act, by["bc"], prepare, take_conv(NX, lambda n: BC[:, n, :]))
            run_phase(act, by["z"], prepare, take_copy(lambda n: Z[:, n, :], ACT.Silu))
            run_phase(act, by["dt"], prepare, take_dt)
            ssd()
            run_phase(act, by["so"], prepare, nothing)
            layer_norm(2)
            run_phase(act, by["up1"], prepare, take_up(1))
            run_phase(act, by["down1"], prepare, nothing)
            layer_norm(3)

        @block.tensor
        def _(pe):
            def product(ph, acts):
                turn = ph.unroll * ph.per

                def output(j, k, u):
                    o = ph.out0 + j
                    pe.wait_ge(bank_free[o % 2], o // 2 + k * (u // 2) + CREDIT)
                    for q in range(ph.per):
                        s = ph.slab0 + j * ph.per + q
                        pe.wait_ge(low_ready, s + 1 + k * (u * ph.per))
                        w = wsp[:, s % 2, :, 0:ph.cols].rearrange("p a (t c) -> p a t c", t=ph.tiles)
                        for t in range(ph.tiles):
                            i = q * ph.tiles + t
                            first, last = i == 0, i == ph.per * ph.tiles - 1
                            pe.matmul(out_bank(ph, j), w[:, 0, t, :], acts[:, 0, i, :], start=first, stop=False)
                            pe.matmul(out_bank(ph, j), w[:, 0, t, :], acts[:, 1, i, :], start=False, stop=False)
                            mm = pe.matmul(out_bank(ph, j), w[:, 1, t, :], acts[:, 0, i, :], start=False, stop=last)
                        mm.then_inc(slab_done, 1)

                u = 2
                n = ph.outs // u

                def body(k):
                    for j in range(u):
                        output(j, k, u)

                loop(pe, n, body)
                for j in range(n * u, ph.outs):
                    output(j, 0, 0)

            def layer_norm(i):
                pe.wait_ge(S("ln_acc"), KT * (i + 1) + CREDIT)
                pe.matmul(bank[2][:, 0:T], ones, tmp[:, 0, :], start=True, stop=True).then_inc(S("ln_sum"), 1)
                for n in range(KT):
                    pe.wait_ge(S("ln_sq"), KT * i + n + 1)
                    pe.matmul(bank[3][:, 0:T], ones, tmp[:, 1 + n % 2, :], start=n == 0,
                              stop=n == KT - 1).then_inc(S("ln_sqsum"), 1)

            def flat(x):
                return x[:, :, :].rearrange("p a b -> p (a b)")

            def delta_rule():
                pe.wait_ge(bank_free[0], (by["wo"].out0 + 1) // 2 + CREDIT)
                pe.wait_ge(bank_free[1], by["wo"].out0 // 2 + CREDIT)

                def rows(x, h):
                    return x[64 * h:64 * h + 64]

                def body(k):
                    for g in range(2):
                        pe.wait_ge(S("key_sq"), 2 * k + g + 1)
                        pe.matmul(bank[4 * g + 2][:, 0:T], bones, flat(SQ[g]), start=True, stop=True).then_inc(S("norm_mm"), 1)
                    for g in range(2):
                        pe.wait_ge(S(f"lora_landed{g}"), 16 * k + 16)
                        pe.matmul(bank[4 * g][:, 0:T], LW[g][0:LORA, 0, :], lo_w[0:LORA, :], start=True, stop=True)
                        pe.matmul(bank[4 * g][:, T:2 * T], LW[g][0:LORA, 1, :], lo_a[0:LORA, :], start=True, stop=True)
                        pe.matmul(bank[4 * g + 1][:, 0:T], LW[g][:, 2, :], lo_g[:, 0, :], start=True, stop=False)
                        pe.matmul(bank[4 * g + 1][:, 0:T], LW[g][:, 3, :], lo_g[:, 1, :], start=False,
                                  stop=True).then_inc(S("lora_mm"), 1)
                    for g in range(2):
                        pe.wait_ge(S(f"v_landed{g}"), 16 * k + 16)
                        pe.wait_ge(S("k_tilde"), 2 * k + g + 1)
                        pe.wait_ge(S("b_tilde"), 2 * k + g + 1)
                        pe.transpose(bank[4 * g + 3][:, 0:P], VS[g][:, 0:P], ident)
                        pe.transpose(bank[4 * g + 3][:, P:2 * P], VS[g][:, P:2 * P], ident)
                        pe.transpose(bank[4 * g + 3][:, 2 * P:3 * P], BT[g][:, 0, :], ident)
                        pe.transpose(bank[4 * g + 3][:, 3 * P:4 * P], KW[g][:, 0, :], ident).then_inc(S("turned"), 1)
                    for g in range(2):
                        pe.wait_ge(S("bonus_in"), 2 * k + g + 1)
                        pe.matmul(bank[4 * g + 2][:, T:2 * T], bones, flat(SQ[g]), start=True, stop=True).then_inc(S("bonus_mm"), 1)
                    for g in range(2):
                        pe.wait_ge(S("r_tilde"), 2 * k + g + 1)
                        pe.wait_ge(S("gate_ready"), 2 * k + g + 1)
                        for c in range(2):
                            for h in range(2):
                                mm = pe.matmul(bank[4 * g + h][:, T * c:T * c + T], rows(BT[g], h)[:, c, :],
                                               rows(AR[g], h)[:, c, :, :].rearrange("p a b -> p (a b)"),
                                               start=True, stop=True)
                        mm.then_inc(S("attn_b"), 1)
                    for g in range(2):
                        pe.wait_ge(S("bonus_ready"), 2 * k + g + 1)
                        pe.wait_ge(S("token_major"), 2 * k + g + 1)
                        for c in range(2):
                            for h in range(2):
                                mm = pe.matmul(bank[4 * g + 2 + h][:, T * c:T * c + T], rows(KW[g], h)[:, c, :],
                                               rows(AR[g], h)[:, c, :, :].rearrange("p a b -> p (a b)"),
                                               start=True, stop=True)
                        mm.then_inc(S("attn_k"), 1)
                    for g in range(2):
                        pe.wait_ge(S("lm1_ready"), 4 * k + 2 * g + 2)
                        for c in range(2):
                            for h in range(2):
                                mm = pe.matmul(bank[4 * g + h][:, P * c:P * c + P], rows(AR[g], h)[:, c, 0, :],
                                               rows(BT[g], h)[:, c, :], start=True, stop=True)
                        mm.then_inc(S("attn_l"), 1)
                    for lev in range(len(LEVELS)):
                        for g in range(2):
                            pe.wait_ge(S("t_ready"), 12 * k + 2 * lev + g + 1)
                            for p in range(4):
                                mm = pe.matmul(bank[4 * g][:, P * p:P * p + P], LM1[g][:, p, 0:P], TI[g][:, p, :],
                                               start=True, stop=True)
                            mm.then_inc(S("x_mm"), 1)
                        for g in range(2):
                            pe.wait_ge(S("x_ready"), 12 * k + 2 * lev + g + 1)
                            pe.wait_ge(S("u_ready"), 14 * k + 2 * lev + g + 1)
                            if lev == 0:
                                pe.wait_ge(S("lm2_ready"), 4 * k + 2 * g + 2)
                            if lev < len(LEVELS) - 1:
                                for p in range(4):
                                    mm = pe.matmul(bank[4 * g + 2][:, P * p:P * p + P], UI[g][:, p, :], XI[g][:, p, :],
                                                   start=True, stop=True)
                                mm.then_inc(S("t_mm"), 1)
                            for p in range(4):
                                mm = pe.matmul(bank[4 * g + 1][:, P * p:P * p + P], XI[g][:, p, :], UI[g][:, p, :],
                                               start=True, stop=True)
                            mm.then_inc(S("u_mm"), 1)
                    for c in range(2):
                        for g in range(2):
                            if c == 0:
                                pe.wait_ge(S("lm2_ready"), 4 * k + 2 * g + 2)
                            else:
                                pe.wait_ge(S("state_ready"), 2 * k + g + 1)
                            for h in range(2):
                                to = bank[4 * g + 3 - c * h][:, P * c + 64 * h:P * c + 64 * h + 64]
                                if c:
                                    pe.matmul(to, rows(AR[g], h)[:, 1, 0, :], rows(S0[g], h)[:, :], start=True, stop=False)
                                mm = pe.matmul(to, LM2[g][:, 2 * h + c, 0:P], TOK[g][:, c, 64 * h:64 * h + 64],
                                               start=c == 0, stop=True)
                            mm.then_inc(S("rhs_mm"), 1)
                        for g in range(2):
                            pe.wait_ge(S("rhs_ready"), 6 * k + (2 * g + 4 if c else g + 1))
                            pe.wait_ge(S("u_ready"), 14 * k + 2 * len(LEVELS) + g + 1)
                            for h in range(2):
                                mm = pe.matmul(bank[4 * g][:, P * c + 64 * h:P * c + 64 * h + 64], UI[g][:, 2 * h + c, :],
                                               RH[g][:, 2 * c + h, :], start=True, stop=True)
                            mm.then_inc(S("sa_mm"), 1)
                        if c == 0:
                            for g in range(2):
                                pe.wait_ge(S("sa_ready"), 4 * k + g + 1)
                                for h in range(2):
                                    to = bank[4 * g + 2][64 * h:64 * h + 64, 0:64]
                                    pe.matmul(to, TOK[g][:, 2, 64 * h:64 * h + 64], SA[g][:, h, :], start=True, stop=False)
                                    mm = pe.matmul(to, TOK[g][:, 3, 64 * h:64 * h + 64], TOK[g][:, 0, 64 * h:64 * h + 64],
                                                   start=False, stop=True)
                                mm.then_inc(S("state_mm"), 1)
                        for g in range(2):
                            pe.wait_ge(S("sa_ready"), 4 * k + 2 * c + g + 1)
                            for h in range(2):
                                to = bank[4 * g + 1][64 * h:64 * h + 64, P * c:P * c + P]
                                p = 2 * h + c
                                pe.matmul(to, SA[g][:, 2 * c + h, :], LM1[g][:, p, P:2 * P], start=True, stop=False)
                                mm = pe.matmul(to, TOK[g][:, c, 64 * h:64 * h + 64], LM2[g][:, p, P:2 * P],
                                               start=False, stop=c == 0)
                                if c:
                                    mm = pe.matmul(to, rows(S0[g], h)[:, :], rows(AR[g], h)[:, 1, 1, :],
                                                   start=False, stop=True)
                            mm.then_inc(S("y_mm"), 1)
                    for g in range(2):
                        pe.wait_ge(S("y_ready"), 2 * k + g + 1)
                        pe.matmul(bank[4 * g + 3][:, 0:T], bones, YY[g][:, :], start=True, stop=True).then_inc(S("y_sum_mm"), 1)
                    for g in range(2):
                        pe.wait_ge(S("y_sq"), 2 * k + g + 1)
                        pe.matmul(bank[4 * g][:, 0:T], bones, flat(SQ[g]), start=True, stop=True).then_inc(S("y_var_mm"), 1)

                loop(pe, KT // 2, body)

            def turn_dt():
                pe.wait_ge(S("cs_ready"), 1)
                half = ident[0:HEADS, 0:HEADS]
                for c in range(2):
                    pe.transpose(bank[2][:, HEADS * c:HEADS * c + HEADS], dtc[:, P * c:P * c + P], half)
                for c in range(2):
                    mm = pe.transpose(bank[2][:, HEADS * (2 + c):HEADS * (3 + c)], cs[:, P * c:P * c + P], half)
                mm.then_inc(S("dt_turned"), 1)

            def ssd():
                pe.wait_ge(bank_free[0], (by["so"].out0 + 1) // 2 + CREDIT)
                pe.wait_ge(bank_free[1], by["so"].out0 // 2 + CREDIT)
                pe.wait_ge(S("dt_tokens"), 2)

                def body(k):
                    pe.wait_ge(S("bst_landed"), 16 * k + 16)
                    pe.matmul(bank[0][:, 0:T], BST[:, 0:P], BC[:, GROUPS + k, :], start=True, stop=True)
                    pe.matmul(bank[0][:, T:T + P], BST[:, P:T], BC[:, GROUPS + k, P:T], start=True,
                              stop=True).then_inc(S("cb_mm"), 1)
                    pe.wait_ge(S("xst_landed"), 16 * k + 16)
                    for c in range(2):
                        for t in range(4):
                            mm = pe.transpose(bank[1 + c][:, P * t:P * t + P], XST[:, t, P * c:P * c + P], ident)
                        mm.then_inc(S("x_turned"), 1)
                    pe.wait_ge(S("xdt_ready"), 2 * k + 2)
                    for h in range(8):
                        pe.wait_ge(S("g_ready"), 8 * k + h + 1)
                        half = 64 * (h % 2)
                        to = bank[3 + h // 2]
                        pe.matmul(to[half:half + 64, 0:T], XDT[:, 0, h, :], GE[h % 2][:, 0:T], start=True, stop=False)
                        pe.matmul(to[half:half + 64, P:T], XDT[:, 1, h, :], GE[h % 2][:, T:T + P], start=False,
                                  stop=True).then_inc(S("ssd_y_mm"), 1)
                    for t in range(4):
                        pe.wait_ge(S("ys_sq"), 4 * k + t + 1)
                        pe.matmul(bank[7][:, 0:T], ones, SQS[:, :], start=t == 0, stop=t == 3).then_inc(S("ys_sq_mm"), 1)

                loop(pe, GROUPS, body)

            pe.wait_ge(S("basic_landed"), 16)
            for i, name in enumerate(SHIFT_PH):
                pe.wait_ge(S("shift_low"), KT * (i + 1) + CREDIT)
                product(by[name], shift_buf(i))
            delta_rule()
            pe.wait_ge(S("y_low"), KT + CREDIT)
            product(by["wo"], YR)
            layer_norm(0)
            pe.wait_ge(S("ln_low"), KT)
            product(by["up0"], XS)
            pe.wait_ge(S("hid_low"), NF + CREDIT)
            product(by["down0"], HID)
            layer_norm(1)
            pe.wait_ge(S("ln_low"), 2 * KT)
            for name in ("x", "bc", "z", "dt"):
                product(by[name], XS)
            turn_dt()
            ssd()
            pe.wait_ge(S("ys_low"), NX + CREDIT)
            product(by["so"], YS)
            layer_norm(2)
            pe.wait_ge(S("ln_low"), 3 * KT)
            product(by["up1"], XS)
            pe.wait_ge(S("hid_low"), 2 * NF + CREDIT)
            product(by["down1"], HID)
            layer_norm(3)

        @block.vector
        def _(dve):
            def prepare(ph, s, k, turn):
                dve.wait_ge(high_ready, s + 1 + k * turn)
                dve.tensor_tensor(wsp[:, s % 2, 1, 0:ph.cols], raw[:, s % RAW, 0:ph.cols],
                                  wsp[:, s % 2, 0, 0:ph.cols].bitcast(F32), ALU.subtract).then_inc(low_ready, 1)

            def mix(i):
                mu = SHIFT_MU[i]

                def body(k):
                    for j in range(2):
                        n = 2 * k + j
                        dve.wait_ge(S("shift_low"), KT * i + 2 * k + CREDIT)
                        dve.tensor_scalar(tmp[:, j, :], H[:, n, :], omm[:, KT * mu + n, :], None,
                                          ALU.mult).then_inc(S("mix_begun"), 1)
                        dve.wait_ge(S("mix_begun"), KT * i + n + 1)
                        dve.scalar_tensor_tensor(out=tmp[:, j, 1:T], in0=H[:, n, 0:T - 1], scalar=param("mu", KT * mu + n),
                                                 in1=tmp[:, j, 1:T], op0=ALU.mult, op1=ALU.add).then_inc(S("mixed"), 1)

                loop(dve, KT // 2, body)

            def nothing(ph, j, k, u):
                pass

            def take_residual(ph, j, k, u):
                n = j + k * u
                out_wait(dve, ph, j, k, u)
                dve.scalar_tensor_tensor(out=H[:, n, :], in0=H[:, n, :], scalar=ALPHA, in1=out_bank(ph, j),
                                         op0=ALU.mult, op1=ALU.add).then_inc(free_sem(ph, j), 1)

            def take_up(layer):
                def take(ph, j, k, u):
                    if j % 2:
                        n = j // 2 + k * (u // 2)
                        out_wait(dve, ph, j, k, u)
                        dve.wait_ge(free_sem(ph, j - 1), freed(ph, j - 1, k, u))
                        dve.wait_ge(S("hid_low"), NF * layer + n + CREDIT)
                        dve.tensor_tensor(tmp[:, 1 + (j // 2) % 2, :], tmp[:, 0, :], out_bank(ph, j),
                                          ALU.mult).then_inc(free_sem(ph, j), 1)
                return take

            def layer_norm(i):
                dve.wait_ge(S("ln_sum"), i + 1)

                def centre(k):
                    for j in range(4):
                        n = 4 * k + j
                        dve.scalar_tensor_tensor(out=H[:, n, :], in0=bank[2][:, 0:T], scalar=-1.0 / D, in1=H[:, n, :],
                                                 op0=ALU.mult, op1=ALU.add).then_inc(S("ln_centred"), 1)

                loop(dve, KT // 4, centre)
                dve.wait_ge(S("ln_std"), i + 1)
                dve.reciprocal(tmp[:, 0, :], tmp[:, 0, :]).then_inc(S("ln_rstd"), 1)
                dve.wait_ge(S("ln_rstd"), i + 1)

                def scale(k):
                    for j in range(4):
                        n = 4 * k + j
                        dve.tensor_tensor(H[:, n, :], H[:, n, :], tmp[:, 0, :], ALU.mult).then_inc(S("ln_scaled"), 1)

                loop(dve, KT // 4, scale)

            def take_conv(tile0):
                def take(ph, j, k, u):
                    n = j + k * u
                    dve.wait_ge(S("conv_begun"), tile0 + n + 1)
                    for tap in (2, 1, 0):
                        lag = 3 - tap
                        d = tmp[:, j % 2, :]
                        if lag > 1:
                            dve.wait_ge(S("conv_tap"), 2 * (tile0 + n) + lag - 1)
                        i = dve.scalar_tensor_tensor(out=d[:, lag:T], in0=out_bank(ph, j)[:, 0:T - lag],
                                                     scalar=param("conv_w", tap * 48 + tile0 + n), in1=d[:, lag:T],
                                                     op0=ALU.mult, op1=ALU.add)
                        i.then_inc(S("conv_tap") if tap else free_sem(ph, j), 1)
                return take

            def take_dt(ph, j, k, u):
                bias = par[0:HEADS, PARAM_AT["dt_bias"], :]
                out_wait(dve, ph, j, k, u)
                dve.wait_ge(S("dt_abs"), 1)
                dve.tensor_scalar(dtc[:, :], out_bank(ph, j), bias, 0.0, ALU.add, ALU.max).then_inc(free_sem(ph, j), 1)
                dve.wait_ge(free_sem(ph, j), freed(ph, j, k, u))
                dve.wait_ge(S("dt_ln"), 1)
                dve.tensor_tensor(dtc[:, :], dtc[:, :], dtb[:, :], ALU.add).then_inc(S("dt_step"), 1)
                dve.wait_ge(S("dt_rate"), 1)
                dve.wait_ge(S("dt_step"), 1)
                dve.tensor_scalar(dta[:, :], dtc[:, :], aneg[:, 0:1], -1.0, ALU.mult, ALU.mult).then_inc(S("dt_step"), 1)
                dve.wait_ge(S("dt_step"), 2)
                for c in range(2):
                    dve.tensor_tensor_scan(cs[:, P * c:P * c + P], ones[0:HEADS, :], dta[:, P * c:P * c + P], 0.0,
                                           ALU.mult, ALU.add).then_inc(S("dt_step"), 1)
                dve.wait_ge(S("dt_step"), 4)
                dve.tensor_copy(aneg[:, 1:2], cs[:, P - 1:P]).then_inc(S("dt_step"), 1)
                dve.wait_ge(S("dt_step"), 5)
                dve.tensor_scalar(cs[:, 0:P], cs[:, 0:P], aneg[:, 1:2], None, ALU.subtract).then_inc(S("cs_ready"), 1)

            def delta_rule():
                dve.wait_ge(S("mask_landed"), 48)
                dve.wait_ge(S("shift_low"), 6 * KT + CREDIT)
                for g in range(2):
                    dve.memset(SC[g][:, :, 0:1], 0.0).then_inc(S("scan_zeroed"), 1)
                dve.wait_ge(S("scan_zeroed"), 2)

                def bc(m, n):
                    return m.unsqueeze(1).broadcast_to([P, n, m.shape[-1]])

                def body(k):
                    each = [(g, 2 * k + g) for g in range(2)]
                    flat = lambda x: x[:, :, :].rearrange("p a b -> p (a b)")
                    two = lambda x: x.rearrange("p (a b) -> p a b", a=2)
                    for g, n in each:
                        dve.wait_ge(S("y_low"), 2 * k + CREDIT)
                        dve.tensor_scalar(flat(KK[g]), K[:, n, :], param("k_k", n), None, ALU.mult).then_inc(S("key_scaled"), 1)
                    for g, n in each:
                        dve.wait_ge(S("norm_ready"), n + 1)
                        dve.tensor_scalar(flat(SQ[g]), flat(SQ[g]), 1e-12, None, ALU.max).then_inc(S("norm_floor"), 1)
                    for g, n in each:
                        dve.wait_ge(S("norm_floor"), n + 1)
                        dve.reciprocal(flat(SQ[g]), flat(SQ[g])).then_inc(S("norm_inv"), 1)
                    for g, n in each:
                        dve.wait_ge(S("norm_inv"), n + 1)
                        dve.wait_ge(S("key_scaled"), n + 1)
                        dve.tensor_tensor(flat(KK[g]), flat(KK[g]), flat(SQ[g]), ALU.mult).then_inc(S("kk_ready"), 1)
                    for g, n in each:
                        dve.wait_ge(S("decay_gate"), n + 1)
                        for c in range(2):
                            dve.tensor_tensor_scan(SC[g][:, c, 1:P + 1], ones, SG[g][:, P * c:P * c + P], 0.0,
                                                   ALU.mult, ALU.add).then_inc(S("scanned"), 1)
                    for g, n in each:
                        dve.wait_ge(S("scanned"), 4 * k + 2 * g + 2)
                        for i, sign in enumerate((DECAY, -DECAY)):
                            dve.tensor_scalar(kb[:, g, i, :], SC[g][:, :, 64], sign, None, ALU.mult).then_inc(S("mid_ready"), 1)
                    for g, n in each:
                        dve.wait_ge(S("rate_gate"), n + 1)
                        dve.wait_ge(S("kk_ready"), n + 1)
                        dve.tensor_tensor(flat(SQ[g]), flat(KK[g]), AA[g][:, :], ALU.mult).then_inc(S("kka_ready"), 1)
                        dve.wait_ge(S("kka_ready"), n + 1)
                        dve.tensor_scalar(AA[g][:, :], AA[g][:, :], param("k_a", n), omka[:, n, :], ALU.mult,
                                          ALU.add).then_inc(S("rate_factor"), 1)
                    for g, n in each:
                        dve.wait_ge(S("rate_factor"), n + 1)
                        dve.wait_ge(S("scanned"), 4 * k + 2 * g + 2)
                        dve.tensor_tensor(flat(K2[g]), K[:, n, :], AA[g][:, :], ALU.mult).then_inc(S("key_ready"), 1)
                    for g, n in each:
                        dve.wait_ge(S("decayed"), 8 * k + 4 * g + 4)
                        dve.tensor_tensor(BT[g][:, :, :], SQ[g][:, :, :], EI[g][:, :, 1:P + 1], ALU.mult).then_inc(S("b_tilde"), 1)
                        dve.wait_ge(S("key_ready"), n + 1)
                        dve.tensor_tensor(KW[g][:, :, :], K2[g][:, :, :], EI[g][:, :, 1:P + 1], ALU.mult).then_inc(S("k_tilde"), 1)
                    for g, n in each:
                        dve.wait_ge(S("b_tilde"), n + 1)
                        dve.scalar_tensor_tensor(out=flat(SQ[g]), in0=R[:, n, :], scalar=param("r_k", n), in1=flat(K2[g]),
                                                 op0=ALU.mult, op1=ALU.mult).then_inc(S("bonus_in"), 1)
                    for g, n in each:
                        dve.scalar_tensor_tensor(out=AR[g][:, :, 0, :], in0=KK[g][:, :, :], scalar=-1.0,
                                                 in1=EE[g][:, :, 0:P], op0=ALU.mult, op1=ALU.mult).then_inc(S("a_tilde"), 1)
                        dve.tensor_tensor(AR[g][:, :, 1, :], two(R[:, n, :]), EE[g][:, :, 1:P + 1],
                                          ALU.mult).then_inc(S("r_tilde"), 1)
                        dve.tensor_tensor(dsc[:, g, :], EE[g][:, 0, P:P + 1], EI[g][:, 1, 0:1], ALU.mult).then_inc(S("carry"), 1)
                    for g, n in each:
                        dve.wait_ge(S("bonus_mm"), n + 1)
                        dve.wait_ge(S("v_landed%d" % g), 16 * k + 16)
                        dve.tensor_tensor(BV[g][:, :], bank[4 * g + 2][:, T:2 * T], VS[g][:, :], ALU.mult).then_inc(S("bonus_ready"), 1)
                    pairs = bc(pair_mask[:, :], 2)
                    for g, n in each:
                        dve.wait_ge(S("attn_b"), n + 1)
                        for h in range(2):
                            dve.tensor_tensor(LM1[g][:, 2 * h:2 * h + 2, :], two(bank[4 * g + h][:, :]), pairs,
                                              ALU.mult).then_inc(S("lm1_ready"), 1)
                    for g, n in each:
                        dve.wait_ge(S("lm1_ready"), 4 * k + 2 * g + 2)
                        dve.tensor_tensor(UI[g][:, :, :], LM1[g][:, :, 0:P], bc(first_mask[:, 1, :], 4), ALU.mult).then_inc(S("u_begun"), 1)
                        dve.wait_ge(S("u_begun"), n + 1)
                        dve.tensor_tensor(UI[g][:, :, :], UI[g][:, :, :], bc(ident, 4), ALU.add).then_inc(S("u_ready"), 1)
                    four = lambda x: x.rearrange("p (a b) -> p a b", a=4)
                    for g, n in each:
                        dve.wait_ge(S("attn_l"), n + 1)
                        for h in range(2):
                            dve.tensor_tensor(TI[g][:, 2 * h:2 * h + 2, :], two(bank[4 * g + h][:, 0:2 * P]),
                                              bc(first_mask[:, 0, :], 2), ALU.mult).then_inc(S("t_begun"), 1)
                        dve.wait_ge(S("t_begun"), 2 * n + 2)
                        dve.tensor_tensor(TI[g][:, :, :], TI[g][:, :, :], bc(ident, 4), ALU.add).then_inc(S("t_ready"), 1)
                    for g, n in each:
                        dve.wait_ge(S("attn_k"), n + 1)
                        for h in range(2):
                            dve.tensor_tensor(LM2[g][:, 2 * h:2 * h + 2, :], two(bank[4 * g + 2 + h][:, :]), pairs,
                                              ALU.mult).then_inc(S("lm2_ready"), 1)
                    for lev in range(len(LEVELS)):
                        for g, n in each:
                            dve.wait_ge(S("x_mm"), 12 * k + 2 * lev + g + 1)
                            dve.tensor_tensor(XI[g][:, :, :], four(bank[4 * g][:, :]), bc(level_mask[:, lev, :], 4),
                                              ALU.mult).then_inc(S("x_ready"), 1)
                        if lev < len(LEVELS) - 1:
                            for g, n in each:
                                dve.wait_ge(S("t_mm"), 10 * k + 2 * lev + g + 1)
                                dve.tensor_tensor(TI[g][:, :, :], TI[g][:, :, :], four(bank[4 * g + 2][:, :]),
                                                  ALU.add).then_inc(S("t_ready"), 1)
                        for g, n in each:
                            dve.wait_ge(S("u_mm"), 12 * k + 2 * lev + g + 1)
                            dve.tensor_tensor(UI[g][:, :, :], UI[g][:, :, :], four(bank[4 * g + 1][:, :]),
                                              ALU.add).then_inc(S("u_ready"), 1)
                    for g, n in each:
                        dve.wait_ge(S("state_mm"), n + 1)
                        dve.wait_ge(S("carry"), n + 1)
                        dve.tensor_scalar(S0[g][:, :], bank[4 * g + 2][:, 0:64], dsc[:, g, :], None, ALU.mult).then_inc(S("state_ready"), 1)
                    for g, n in each:
                        dve.wait_ge(S("y_sum_mm"), n + 1)
                        dve.scalar_tensor_tensor(out=YC[g][:, :], in0=bank[4 * g + 3][:, 0:T], scalar=-1.0 / 64, in1=YY[g][:, :],
                                                 op0=ALU.mult, op1=ALU.add).then_inc(S("y_centred"), 1)
                    for g, n in each:
                        dve.wait_ge(S("y_std"), n + 1)
                        dve.reciprocal(YY[g][:, :], YY[g][:, :]).then_inc(S("y_rstd"), 1)
                    for g, n in each:
                        dve.wait_ge(S("y_rstd"), n + 1)
                        dve.tensor_tensor(YC[g][:, :], YC[g][:, :], YY[g][:, :], ALU.mult).then_inc(S("y_normed"), 1)
                    for g, n in each:
                        dve.wait_ge(S("y_normed"), n + 1)
                        dve.tensor_scalar(YC[g][:, :], YC[g][:, :], param("gn_g", n), param("gn_b", n), ALU.mult,
                                          ALU.add).then_inc(S("y_affine"), 1)
                    for g, n in each:
                        dve.wait_ge(S("y_affine"), n + 1)
                        dve.tensor_tensor(YC[g][:, :], YC[g][:, :], BV[g][:, :], ALU.add).then_inc(S("y_bonus"), 1)
                    for g, n in each:
                        dve.wait_ge(S("y_bonus"), n + 1)
                        dve.tensor_tensor(YC[g][:, :], YC[g][:, :], GG[g][:, :], ALU.mult).then_inc(S("y_gated"), 1)

                loop(dve, KT // 2, body)

            def ssd():
                dve.wait_ge(S("smask_landed"), 16)
                dve.wait_ge(S("dt_tokens"), 2)

                def body(k):
                    dve.wait_ge(S("cb_mm"), k + 1)
                    dve.tensor_tensor(CBM[:, :], bank[0][:, 0:3 * P], smask[:, :], ALU.mult).then_inc(S("cbm_ready"), 1)
                    for c in range(2):
                        dve.wait_ge(S("x_turned"), 2 * k + c + 1)
                        dve.tensor_tensor(XDT[:, c, :, :], bank[1 + c][:, :].rearrange("p (h d) -> p h d", h=8),
                                          dtt[:, c, :, :].rearrange("p (g h) o -> p g h o", g=GROUPS)[:, k, :, :].broadcast_to([P, 8, 64]),
                                          ALU.mult).then_inc(S("xdt_ready"), 1)

                    def seg(h):
                        if h >= 2:
                            dve.wait_ge(S("ge_ready"), 8 * k + h - 1)
                        head = 8 * k + h
                        dve.tensor_scalar(SEG[h % 2][:, 0:T], CSB[:, h, :], ncs[:, 0, head, :], 0.0, ALU.add,
                                          ALU.min).then_inc(S("seg_ready"), 1)
                        dve.tensor_scalar(SEG[h % 2][:, T:T + P], CSB[:, h, P:T], ncs[:, 1, head, :], 0.0, ALU.add,
                                          ALU.min).then_inc(S("seg_ready"), 1)

                    dve.wait_ge(S("csb_landed"), 16 * k + 16)
                    dve.wait_ge(S("cbm_ready"), k + 1)
                    seg(0)
                    for h in range(8):
                        if h < 7:
                            seg(h + 1)
                        dve.wait_ge(S("ge_ready"), 8 * k + h + 1)
                        dve.tensor_tensor(GE[h % 2][:, :], GE[h % 2][:, :], CBM[:, :], ALU.mult).then_inc(S("g_ready"), 1)
                    for t in range(4):
                        n = 4 * k + t
                        dve.wait_ge(S("ssd_y_mm"), 8 * k + 2 * t + 2)
                        dve.wait_ge(S("xst_landed"), 16 * k + 16)
                        dve.scalar_tensor_tensor(out=YG[:, t, :], in0=XST[:, t, :], scalar=param("d_skip", n),
                                                 in1=bank[3 + t][:, 0:T], op0=ALU.mult, op1=ALU.add).then_inc(S("ys_skip"), 1)
                        dve.wait_ge(S("ys_skip"), n + 1)
                        dve.tensor_tensor(YG[:, t, :], YG[:, t, :], Z[:, n, :], ALU.mult).then_inc(S("ys_gated"), 1)
                    dve.wait_ge(S("ys_std"), k + 1)
                    dve.reciprocal(RST[:, :], RST[:, :]).then_inc(S("ys_rstd"), 1)
                    dve.wait_ge(S("ys_rstd"), k + 1)
                    for t in range(4):
                        n = 4 * k + t
                        dve.scalar_tensor_tensor(out=YG[:, t, :], in0=YG[:, t, :], scalar=param("norm_g", n), in1=RST[:, :],
                                                 op0=ALU.mult, op1=ALU.mult).then_inc(S("ys_normed"), 1)

                loop(dve, GROUPS, body)

            for i, e in enumerate((LN_EPS, GN_EPS, RMS_EPS, 1.0)):
                dve.memset(eps[:, i, :], e).then_inc(S("eps_set"), 1)
            dve.wait_ge(S("par_landed"), 16)
            for dst, name, n in ((omm, "mu", 6 * KT), (omka, "k_a", KT)):
                dve.tensor_scalar(dst[:, :, 0], par[:, PARAM_AT[name]:PARAM_AT[name] + n, 0], -1.0, 1.0, ALU.mult,
                                  ALU.add).then_inc(S("one_minus"), 1)
            dve.wait_ge(S("one_minus"), 2)
            dve.wait_ge(S("eps_set"), 4)
            dve.wait_ge(S("x_landed"), 16)
            dve.wait_ge(S("basic_landed"), 16)
            mix(0)
            prepare(by["r"], 0, 0, 0)
            prepare(by["r"], 1, 0, 0)
            mix(1)
            run_phase(dve, by["r"], prepare, nothing)
            mix(2)
            run_phase(dve, by["w1"], prepare, nothing)
            mix(3)
            run_phase(dve, by["k"], prepare, nothing)
            mix(4)
            run_phase(dve, by["a1"], prepare, nothing)
            mix(5)
            run_phase(dve, by["v"], prepare, nothing)
            run_phase(dve, by["g1"], prepare, nothing)
            delta_rule()
            run_phase(dve, by["wo"], prepare, take_residual)
            layer_norm(0)
            run_phase(dve, by["up0"], prepare, take_up(0))
            run_phase(dve, by["down0"], prepare, take_residual)
            layer_norm(1)
            run_phase(dve, by["x"], prepare, take_conv(0))
            run_phase(dve, by["bc"], prepare, take_conv(NX))
            run_phase(dve, by["z"], prepare, nothing)
            run_phase(dve, by["dt"], prepare, take_dt)
            ssd()
            run_phase(dve, by["so"], prepare, take_residual)
            layer_norm(2)
            run_phase(dve, by["up1"], prepare, take_up(1))
            run_phase(dve, by["down1"], prepare, take_residual)
            layer_norm(3)

        @block.gpsimd
        def _(pool):
            def apart():
                pool.wait_ge(S("par_landed"), 16)

            def shift_low(i):
                buf = shift_buf(i)

                def body(k):
                    for j in range(2):
                        n = 2 * k + j
                        pool.wait_ge(S("shift_high"), KT * i + n + 1)
                        apart()
                        pool.tensor_tensor(buf[:, 1, n, :], tmp[:, j, :], buf[:, 0, n, :].bitcast(F32),
                                           ALU.subtract).then_inc(S("shift_low"), 1)

                loop(pool, KT // 2, body)

            def add_up(ph, i):
                pool.wait_ge(slab_done, ph.slab0)
                pool.memset(tmp[:, 0, :], 0.0).then_inc(S("acc_zeroed"), 1)
                pool.wait_ge(S("acc_zeroed"), i + 1)

                def body(k):
                    for j in range(2):
                        n = 2 * k + j
                        pool.wait_ge(free_sem(ph, j), freed(ph, j, k, 2))
                        pool.wait_ge(S("ln_acc"), KT * i + n + CREDIT)
                        apart()
                        pool.tensor_tensor(tmp[:, 0, :], tmp[:, 0, :], H[:, n, :], ALU.add).then_inc(S("ln_acc"), 1)

                loop(pool, KT // 2, body)

            def low_of_norm(i):
                def body(k):
                    pool.wait_ge(S("ln_high"), KT * i + k + 1)
                    apart()
                    pool.tensor_tensor(XS[:, 1, k, :], H[:, k, :], XS[:, 0, k, :].bitcast(F32),
                                       ALU.subtract).then_inc(S("ln_low"), 1)

                loop(pool, KT, body)

            def low_of_hidden(layer):
                def body(k):
                    for j in range(2):
                        n = 2 * k + j
                        pool.wait_ge(S("hid_high"), NF * layer + n + 1)
                        apart()
                        pool.tensor_tensor(HID[:, 1, n, :], tmp[:, 1 + j, :], HID[:, 0, n, :].bitcast(F32),
                                           ALU.subtract).then_inc(S("hid_low"), 1)

                loop(pool, NF // 2, body)

            def low_of_delta():
                def body(k):
                    for g in range(2):
                        n = 2 * k + g
                        pool.wait_ge(S("y_high"), n + 1)
                        apart()
                        pool.tensor_tensor(YR[:, 1, n, :], YC[g][:, :], YR[:, 0, n, :].bitcast(F32),
                                           ALU.subtract).then_inc(S("y_low"), 1)

                loop(pool, KT // 2, body)

            def low_of_ssd():
                def body(k):
                    for t in range(4):
                        n = 4 * k + t
                        pool.wait_ge(S("ys_high"), n + 1)
                        apart()
                        pool.tensor_tensor(YS[:, 1, n, :], YG[:, t, :], YS[:, 0, n, :].bitcast(F32),
                                           ALU.subtract).then_inc(S("ys_low"), 1)

                loop(pool, GROUPS, body)

            for sem in (*bank_free, *map(S, ("y_low", "ys_low", "shift_low", "ln_acc", "hid_low"))):
                pool.sem_inc(sem, CREDIT)
            for i in range(6):
                shift_low(i)
            low_of_delta()
            add_up(by["wo"], 0)
            low_of_norm(0)
            low_of_hidden(0)
            add_up(by["down0"], 1)
            low_of_norm(1)
            low_of_ssd()
            add_up(by["so"], 2)
            low_of_norm(2)
            low_of_hidden(1)
            add_up(by["down1"], 3)


def kernel(**inputs):
    import numpy as np
    import concourse.bacc as bacc
    from concourse.bass_utils import run_bass_kernel_spmd as run

    a = {name: np.asarray(v) for name, v in inputs.items()}

    def slabs(w, per=1, width=P):
        rows, cols = w.shape
        tiles = rows // P // per
        v = w.reshape(per, tiles, P, cols // width, width)
        return np.ascontiguousarray(v.transpose(3, 0, 2, 1, 4)).reshape(-1, P, tiles * width)

    def cols(v):
        return v.reshape(-1, P).T

    def interleaved(w):
        half = w.shape[1] // 2 // P
        return w.reshape(D, 2, half, P).transpose(0, 2, 1, 3).reshape(D, -1)

    basic, chunk, ssd_mask = shape_constants()
    pad = np.zeros(P - HEADS, np.float32)
    lora2 = np.zeros((KT, P, 4, P), np.float32)
    lora2[:, :LORA, 0] = a["rwkv_w2"].reshape(LORA, KT, P).transpose(1, 0, 2)
    lora2[:, :LORA, 1] = a["rwkv_a2"].reshape(LORA, KT, P).transpose(1, 0, 2)
    lora2[:, :, 2:] = a["rwkv_g2"].reshape(2, P, KT, P).transpose(2, 1, 0, 3)
    params = np.concatenate([
        cols(a["rwkv_mu"]), cols(a["rwkv_w0"]), cols(a["rwkv_a0"]), cols(a["rwkv_k_k"]), cols(a["rwkv_k_a"]),
        cols(a["rwkv_r_k"]), cols(a["rwkv_ln_g"]), cols(a["rwkv_ln_b"]), cols(a["ssd_conv_w"]), cols(a["ssd_conv_b"]),
        cols(a["ssd_norm_g"]), cols(np.repeat(a["ssd_d"], 64)), cols(a["ln_g"]), cols(a["ln_b"]),
        cols(np.concatenate([a["ssd_dt_bias"], pad])), cols(np.concatenate([a["ssd_a_log"], pad]))], axis=1)
    w_ssd = a["ssd_w_in"]
    n_inner = NX * P
    arrays = {
        "x_cm": a["x"][0].T.reshape(KT, P, T).transpose(1, 0, 2),
        "params": params, "basic": basic, "pair_mask": chunk[:, :2 * P],
        "first_mask": chunk[:, 2 * P:4 * P].reshape(P, 2, P), "level_mask": chunk[:, 4 * P:].reshape(P, -1, P),
        "ssd_mask": ssd_mask, "lora2": lora2,
        "w_r": slabs(a["rwkv_w_in"][0]), "w_k": slabs(a["rwkv_w_in"][1]), "w_v": slabs(a["rwkv_w_in"][2]),
        "w_w1": slabs(a["rwkv_w1"], width=LORA), "w_a1": slabs(a["rwkv_a1"], width=LORA), "w_g1": slabs(a["rwkv_g1"]),
        "w_ro": slabs(a["rwkv_w_out"]),
        "w_z": slabs(w_ssd[:, :n_inner]), "w_x": slabs(w_ssd[:, n_inner:2 * n_inner]),
        "w_bc": slabs(w_ssd[:, 2 * n_inner:-HEADS]), "w_dt": slabs(w_ssd[:, -HEADS:], width=HEADS),
        "w_so": slabs(a["ssd_w_out"], per=2),
    }
    for layer in range(DEPTH):
        arrays[f"w_up{layer}"] = slabs(interleaved(a["ffn_w_in"][layer]))
        arrays[f"w_down{layer}"] = slabs(a["ffn_w_out"][layer], per=4)
    arrays = {name: np.ascontiguousarray(v) for name, v in arrays.items()}

    nc = bacc.Bacc("TRN2", target_bir_lowering=False, num_devices=1)
    inp = {name: nc.dram_tensor(name, v.shape, F32, kind="ExternalInput").ap() for name, v in arrays.items()}
    out = nc.dram_tensor("out", (P, KT, T), F32, kind="ExternalOutput").ap()
    build(nc, inp, out)
    r = run(nc, [arrays], core_ids=[0])
    return r.results[0]["out"].transpose(1, 0, 2).reshape(D, T).T.reshape(1, T, D)
```

```python
import math
from contextlib import ExitStack

import concourse.bass as bass
from concourse import mybir

F32 = mybir.dt.float32
F32R = mybir.dt.float32r
ALU = mybir.AluOpType
ACT = mybir.ActivationFunctionType

P = 128
T = 256
D = 2048
KT = D // P
DEPTH = 2
ALPHA = (2 * DEPTH) ** 0.25
LN_EPS = 1e-5
GN_EPS = 64e-5
RMS_EPS = 1e-5
DECAY = math.exp(-0.5)
LORA = 96
NF = 44
NX = 32
HEADS = 64
GROUPS = 8
PAIRS = KT // 2
RAW, SPLIT = 4, 2

PARAM_TILES = [("mu", 6 * KT), ("w0", KT), ("a0", KT), ("k_k", KT), ("k_a", KT), ("r_k", KT), ("gn_g", KT),
               ("gn_b", KT), ("conv_w", 4 * 48), ("conv_b", 48), ("norm_g", NX), ("d_skip", NX), ("ln_g", 4 * KT),
               ("ln_b", 4 * KT), ("dt_bias", 1), ("a_log", 1)]
PARAM_AT = {}
NPARAM = 0
for _name, _n in PARAM_TILES:
    PARAM_AT[_name] = NPARAM
    NPARAM += _n

N_BASIC, N_SSD = 3 * P, 3 * P
CREDIT = 1
LEVELS = (2, 4, 8, 16, 32, 64)


def shape_constants():
    import numpy as np
    row, col = np.arange(P)[:, None], np.arange(P)[None, :]
    level = lambda m: ((row // m) % 2 == 1) & (col // m == row // m - 1)
    basic = [row == col, row // 64 == col // 64, row >= 0 * col]
    chunk = [row < col, row <= col, level(1).T] + [level(m) for m in LEVELS]
    ssd = [row <= col, row >= 0 * col, row <= col]
    wide = lambda parts: np.concatenate([np.broadcast_to(m, (P, P)).astype(np.float32) for m in parts], axis=1)
    sel = np.concatenate([np.arange(4)[None, :] == 2 * g + row // 64 for g in range(2)], axis=1).astype(np.float32)
    sel_t = np.concatenate([sel[:, 4 * g:4 * g + 4].T for g in range(2)], axis=1)
    return wide(basic), wide(chunk), wide(ssd), sel, sel_t


class Phase:

    def __init__(self, name, src, outs, per, tiles, width, unroll):
        self.name, self.src, self.outs, self.per, self.tiles, self.width, self.unroll = (
            name, src, outs, per, tiles, width, unroll)
        self.slabs = outs * per
        self.cols = tiles * width
        self.slab0 = self.out0 = 0


def loop(eng, n, body):
    if n == 1:
        body(0)
    elif n > 1:
        with eng.Fori(0, n) as k:
            body(k)


def beyond(m, n):
    return not isinstance(m, int) or m >= n


def pair_turns(eng, turn):
    turn(0, 0, False, True)

    def body(q):
        turn(2 * q + 1, 1, True, True)
        turn(2 * q + 2, 0, True, True)

    loop(eng, PAIRS // 2 - 1, body)
    turn(PAIRS - 1, 1, True, False)


def build(nc, inp, out, debug=None):
    ctx = ExitStack()
    with ctx:
        sems = {}

        def S(name):
            if name not in sems:
                sems[name] = ctx.enter_context(nc.semaphore(name))
            return sems[name]

        KB = 1024
        at = [16512]

        def place(nbytes):
            here = at[0]
            at[0] += nbytes
            return here

        def sb(name, shape, dt, offset):
            return nc.alloc_sbuf_tensor_at(name, shape, dt, offset=offset)

        basic = sb("basic", [P, N_BASIC], F32, place(4 * N_BASIC))
        par = sb("par", [P, NPARAM, 1], F32, place((4 * NPARAM + 31) // 32 * 32))
        omm = sb("omm", [P, 6 * KT, 1], F32, place(4 * 6 * KT))
        omka = sb("omka", [P, KT, 1], F32, place(4 * KT))
        eps = sb("eps", [P, 4, 1], F32, place(32))
        raw = sb("raw", [P, RAW, D], F32, place(RAW * 8 * KB))
        wsp_at = place(SPLIT * 16 * KB)
        wsp = sb("wsp", [P, SPLIT, 2, D], F32R, wsp_at)
        H = sb("H", [P, KT, T], F32, place(16 * KB))
        xs_at = place(32 * KB)
        big_at = place(88 * KB)
        tmp_at = place(3 * KB)
        assert at[0] <= 229344, at
        XS = sb("XS", [P, 2, KT, T], F32R, xs_at)
        tmp = sb("tmp", [P, 3, T], F32, tmp_at)
        LSQ = sb("LSQ", [P, KT, T], F32, xs_at + 16 * KB)
        ident, bones, ones = (basic[:, i * P:(i + 1) * P] for i in range(3))

        def param(name, i):
            return par[:, PARAM_AT[name] + i, :]

        R = sb("R", [P, KT, T], F32, big_at)
        K = sb("K", [P, KT, T], F32, big_at + 16 * KB)
        V = sb("V", [P, KT, T], F32, big_at + 32 * KB)
        XS2 = sb("XS2", [P, 2, KT, T], F32R, big_at + 48 * KB)
        XS3 = sb("XS3", [P, 2, KT, T], F32R, big_at + 16 * KB)
        lo_w = sb("lo_w", [P, T], F32, big_at + 80 * KB)
        lo_a = sb("lo_a", [P, T], F32, big_at + 81 * KB)
        lo_g = sb("lo_g", [P, 2, T], F32, big_at + 82 * KB)
        YR = sb("YR", [P, 2, KT, T], F32R, big_at)

        ct = [big_at + 48 * KB]

        def core(name, shape, dt=F32):
            n = 4
            for s in shape[1:]:
                n *= s
            here = ct[0]
            ct[0] += (n + 31) // 32 * 32
            return sb(name, shape, dt, here)

        LM1 = [core(f"LM1_{g}", [P, 4, 2 * P]) for g in range(2)]
        LM2 = [core(f"LM2_{g}", [P, 4, 2 * P]) for g in range(2)]
        XI = [core(f"XI_{g}", [P, 4, P]) for g in range(2)]
        TI = [core(f"TI_{g}", [P, 4, P]) for g in range(2)]
        UI = [core(f"UI_{g}", [P, 4, P]) for g in range(2)]
        S0 = [sb(f"S0_{g}", [P, 64], F32, tmp_at + 256 * (g + 1)) for g in range(2)]
        assert ct[0] <= big_at + 76 * KB, ct
        ct = [big_at + 84 * KB]
        RH = [core(f"RH_{g}", [P, 4, 64]) for g in range(2)]
        SA = [core(f"SA_{g}", [P, 4, 64]) for g in range(2)]
        assert ct[0] <= big_at + 88 * KB
        ct = [xs_at]
        LW = [core(f"LW_{g}", [P, 4, P]) for g in range(2)]
        SG, AA, SC, EE, EI, KK, VS, BT, KW, SQ = ([] for _ in range(10))
        for g in range(2):
            SG.append(core(f"SG_{g}", [P, 2, P]))
            AA.append(core(f"AA_{g}", [P, T]))
            SC.append(core(f"SC_{g}", [P, 2, P + 1]))
            EE.append(core(f"EE_{g}", [P, 2, P + 1]))
            EI.append(core(f"EI_{g}", [P, 2, P + 1]))
            KK.append(core(f"KK_{g}", [P, 2, P]))
            VS.append(core(f"VS_{g}", [P, T]))
            BT.append(core(f"BT_{g}", [P, 2, P]))
            KW.append(core(f"KW_{g}", [P, 2, P]))
            SQ.append(core(f"SQ_{g}", [P, 2, P]))
        AR, TOK, BV, GG = [[], []], [[], []], [[], []], [[], []]
        AR[0] = [core(f"AR_0{g}", [P, 2, 2, P]) for g in range(2)]
        GG[0] = [core(f"GG_0{g}", [P, T]) for g in range(2)]
        assert ct[0] <= xs_at + 32 * KB, ct
        ct = [wsp_at]
        AR[1] = [core(f"AR_1{g}", [P, 2, 2, P]) for g in range(2)]
        for side in range(2):
            TOK[side] = [core(f"TOK_{side}{g}", [P, 4, P]) for g in range(2)]
        assert ct[0] <= wsp_at + 16 * KB, ct
        ct = [wsp_at + 16 * KB]
        GG[1] = [core(f"GG_1{g}", [P, T]) for g in range(2)]
        for side in range(2):
            BV[side] = [core(f"BV_{side}{g}", [P, T]) for g in range(2)]
        YY = [core(f"YY_{g}", [P, T]) for g in range(2)]
        YC = [core(f"YC_{g}", [P, T]) for g in range(2)]
        SY = [core(f"SY_{g}", [P, T]) for g in range(2)]
        NR = core("NR", [4, T])
        YV = core("YV", [4, T])
        assert ct[0] <= wsp_at + 32 * KB, ct
        level_mask = sb("level_mask", [P, len(LEVELS), P], F32, big_at + 76 * KB)
        pair_mask = sb("pair_mask", [P, 2 * P], F32, tmp_at + KB)
        first_mask = sb("first_mask", [P, P], F32, tmp_at + 2 * KB)
        sel = sb("sel", [P, 8], F32, tmp_at + 3 * KB // 4)
        sel_t = sb("sel_t", [4, 2 * P], F32, big_at + 79 * KB)
        kb = sb("kb", [P, 2, 2, 2], F32, tmp_at)
        dsc = sb("dsc", [P, 4, 1], F32, tmp_at + 64)

        HID = sb("HID", [P, 2, NF, T], F32R, big_at)

        XC = sb("XC", [P, NX, T], F32, big_at)
        Z = sb("Z", [P, NX, T], F32, big_at + 32 * KB)
        BC = sb("BC", [P, 2 * GROUPS, T], F32, big_at + 64 * KB)
        YS = sb("YS", [P, 2, NX, T], F32R, big_at)
        dtt = sb("dtt", [P, 2, HEADS, 1], F32, big_at + 80 * KB)
        ncs = sb("ncs", [P, 2, HEADS, 1], F32, big_at + 80 * KB + 512)
        dtc = sb("dtc", [HEADS, T], F32, big_at + 81 * KB)
        cs = sb("cs", [HEADS, T], F32, big_at + 82 * KB)
        dta = sb("dta", [HEADS, T], F32, big_at + 83 * KB)
        dtb = sb("dtb", [HEADS, T], F32, big_at + 84 * KB)
        aneg = sb("aneg", [HEADS, 2], F32, big_at + 85 * KB)
        smask = sb("smask", [P, N_SSD], F32, big_at + 86 * KB)
        ct = [xs_at]
        CSB = core("CSB", [P, 8, T])
        XST = core("XST", [P, 4, T])
        BST = core("BST", [P, T])
        CBM = core("CBM", [P, 3 * P])
        XDT = core("XDT", [P, 2, 8, 64])
        SEG = [core(f"SEG_{i}", [P, 3 * P]) for i in range(2)]
        GE = [core(f"GE_{i}", [P, 3 * P]) for i in range(2)]
        YG = core("YG", [P, 4, T])
        SQS = [x[:, 0:T] for x in (*SEG, *GE)]
        RST = core("RST", [P, T])
        assert ct[0] <= xs_at + 32 * KB, (ct, xs_at)
        cs_dram = nc.dram_tensor("cs_scratch", (HEADS, T), F32, kind="Internal").ap()

        bank = [nc.alloc_psum_tensor(f"bank{i}", [P, 512], F32) for i in range(8)]
        phases = [
            Phase("r", inp["w_r"], 16, 1, 16, P, 4),
            Phase("w1", inp["w_w1"], 1, 1, 16, LORA, 4),
            Phase("k", inp["w_k"], 16, 1, 16, P, 4),
            Phase("v", inp["w_v"], 16, 1, 16, P, 4),
            Phase("a1", inp["w_a1"], 1, 1, 16, LORA, 4),
            Phase("g1", inp["w_g1"], 2, 1, 16, P, 4),
            Phase("wo", inp["w_ro"], 16, 1, 16, P, 4),
            Phase("up0", inp["w_up0"], 88, 1, 16, P, 4),
            Phase("down0", inp["w_down0"], 16, 4, 11, P, 2),
            Phase("x", inp["w_x"], NX, 1, 16, P, 4),
            Phase("bc", inp["w_bc"], 2 * GROUPS, 1, 16, P, 4),
            Phase("z", inp["w_z"], 32, 1, 16, P, 4),
            Phase("dt", inp["w_dt"], 1, 1, 16, HEADS, 4),
            Phase("so", inp["w_so"], 16, 2, 16, P, 4),
            Phase("up1", inp["w_up1"], 88, 1, 16, P, 4),
            Phase("down1", inp["w_down1"], 16, 4, 11, P, 2),
        ]
        by = {}
        s = o = 0
        for ph in phases:
            ph.slab0, ph.out0 = s, o
            s, o = s + ph.slabs, o + ph.outs
            by[ph.name] = ph
        n_slabs = s
        owner = [ph for ph in phases for _ in range(ph.slabs)]

        landed = [S(f"slab_landed{i}") for i in range(RAW)]
        high_ready, low_ready, slab_done = S("high_ready"), S("low_ready"), S("slab_done")
        bank_free = [S("bank0_free"), S("bank1_free")]

        def run_phase(eng, ph, prepare, take, before=None, peel=0, until=None):
            turn = ph.unroll * ph.per
            n = max(0, (ph.slabs - 2) // turn)

            def single(j):
                if before:
                    before(ph, j, 0, 0)
                for q in range(ph.per):
                    s = ph.slab0 + j * ph.per + q + 2
                    if s < (until or n_slabs):
                        prepare(owner[s], s, 0, 0)
                take(ph, j, 0, 0)

            def body(k):
                for i in range(ph.unroll):
                    j = peel * ph.unroll + i
                    if before:
                        before(ph, j, k, ph.unroll)
                    for q in range(ph.per):
                        prepare(ph, ph.slab0 + j * ph.per + q + 2, k, turn)
                    take(ph, j, k, ph.unroll)

            for j in range(peel * ph.unroll):
                single(j)
            loop(eng, n - peel, body)
            for j in range(n * ph.unroll, ph.outs):
                single(j)

        def lands(s, k, turn):
            return landed[s % RAW], 16 * (s // RAW + 1) + k * (16 * turn // RAW)

        def out_wait(eng, ph, j, k, u):
            eng.wait_ge(slab_done, ph.slab0 + (j + 1) * ph.per + k * (u * ph.per))

        def out_bank(ph, j):
            return bank[(ph.out0 + j) % 2][:ph.width, 0:T]

        def free_sem(ph, j):
            return bank_free[(ph.out0 + j) % 2]

        def freed(ph, j, k, u):
            return (ph.out0 + j) // 2 + 1 + k * (u // 2) + CREDIT

        block = ctx.enter_context(nc.Block())

        MU = {"r": 0, "w1": 1, "k": 2, "v": 3, "a1": 4, "g1": 5}
        MIXED = {"r": XS, "w1": XS3, "k": XS2, "v": XS, "a1": XS2, "g1": XS}

        @block.sync
        def _(sp):
            def load(ph, s, k, turn):
                if s >= RAW:
                    sp.wait_ge(low_ready, s - RAW + 1 + k * turn)
                sem, _n = lands(s, k, turn)
                sp.dma_start(raw[:, s % RAW, 0:ph.cols], ph.src[s - ph.slab0 + k * turn]).then_inc(sem, 16)

            sp.dma_start(H[:, :, :], inp["x_cm"]).then_inc(S("x_landed"), 16)
            sp.dma_start(par[:, :, 0], inp["params"]).then_inc(S("par_landed"), 16)
            for s in range(RAW):
                load(owner[s], s, 0, 0)
            sp.dma_start(basic[:, :], inp["basic"]).then_inc(S("basic_landed"), 16)
            for ph in phases:
                first = ph.slab0 if ph.slab0 else RAW
                n = (ph.slab0 + ph.slabs - first) // 4

                def body(k):
                    for j in range(4):
                        load(ph, first + j, k, 4)

                loop(sp, n, body)
                for s in range(first + 4 * n, ph.slab0 + ph.slabs):
                    load(ph, s, 0, 0)
            for n in range(KT):
                sp.wait_ge(S("ln_affine"), 3 * KT + n + 1)
                sp.dma_start(out[:, n, :], H[:, n, :]).then_inc(S("out_stored"), 16)
            sp.wait_ge(S("out_stored"), 16 * KT)

        @block.scalar
        def _(act):
            def apart():
                act.wait_ge(S("par_landed"), 16)

            def prepare(ph, s, k, turn):
                act.wait_ge(*lands(s, k, turn))
                if s >= 2:
                    act.wait_ge(slab_done, s - 1 + k * turn)
                act.activation(wsp[:, s % 2, 0, 0:ph.cols], raw[:, s % RAW, 0:ph.cols],
                               ACT.Copy).then_inc(high_ready, 1)

            def mix_high(name, n, buf):
                act.wait_ge(S("mixed_" + name), n + 1)
                apart()
                act.activation(MIXED[name][:, 0, n, :], tmp[:, buf, :], ACT.Copy).then_inc(S("mix_high_" + name), 1)

            def mix_all_high(name):
                def body(k):
                    for j in range(2):
                        mix_high(name, 2 * k + j, j)

                loop(act, KT // 2, body)

            def take_and_mix(dst, names):
                def take(ph, j, k, u):
                    out_wait(act, ph, j, k, u)
                    apart()
                    act.activation(dst(j + k * u), out_bank(ph, j), ACT.Copy).then_inc(free_sem(ph, j), 1)
                    for i, name in enumerate(names):
                        mix_high(name, j + k * u, i)
                return take

            def take_copy(dst, func=ACT.Copy):
                def take(ph, j, k, u):
                    out_wait(act, ph, j, k, u)
                    apart()
                    act.activation(dst(j + k * u), out_bank(ph, j), func).then_inc(free_sem(ph, j), 1)
                return take

            def take_up(layer):
                def take(ph, j, k, u):
                    n = j // 2 + k * (u // 2)
                    if j % 2 == 0:
                        out_wait(act, ph, j, k, u)
                        act.wait_ge(free_sem(ph, 1), (ph.out0 + 1) // 2 + n + CREDIT)
                        act.activation(tmp[:, 0, :], out_bank(ph, j), ACT.Silu).then_inc(free_sem(ph, j), 1)
                    else:
                        act.wait_ge(free_sem(ph, 1), (ph.out0 + 1) // 2 + n + 1 + CREDIT)
                        apart()
                        act.activation(HID[:, 0, n, :], tmp[:, 1 + (j // 2) % 2, :], ACT.Copy).then_inc(S("hid_high"), 1)
                return take

            def nothing(ph, j, k, u):
                pass

            def layer_norm(i):
                def squares(k):
                    for j in range(2):
                        act.wait_ge(S("ln_centred"), KT * i + 2 * k + j + 1)
                        apart()
                        act.activation(LSQ[:, 2 * k + j, :], H[:, 2 * k + j, :], ACT.Square).then_inc(S("ln_sq"), 1)

                loop(act, KT // 2, squares)
                act.wait_ge(S("ln_sqsum"), KT * (i + 1))
                act.activation(tmp[:, 0, :], bank[3][:, 0:T], ACT.Sqrt, scale=1.0 / D,
                               bias=eps[:, 0, :]).then_inc(S("ln_std"), 1)

                def affine(n):
                    act.wait_ge(S("ln_scaled"), KT * i + n + 1)
                    apart()
                    act.activation(H[:, n, :], H[:, n, :], ACT.Identity, scale=param("ln_g", KT * i + n),
                                   bias=param("ln_b", KT * i + n)).then_inc(S("ln_affine"), 1)

                def high(n):
                    act.wait_ge(S("ln_affine"), KT * i + n + 1)
                    apart()
                    act.activation(XS[:, 0, n, :], H[:, n, :], ACT.Copy).then_inc(S("ln_high"), 1)

                affine(0)

                def body(k):
                    affine(k + 1)
                    if i < 3:
                        high(k)

                loop(act, KT - 1, body)
                if i < 3:
                    high(KT - 1)

            def take_conv(tile0, dst):
                def silu(ph, j, k, u):
                    act.wait_ge(free_sem(ph, j), freed(ph, j, k, u))
                    apart()
                    act.activation(dst(j + k * u), tmp[:, j % 2, :], ACT.Silu).then_inc(S("conv_done"), 1)

                def take(ph, j, k, u):
                    n = j + k * u
                    if tile0 + j >= 2:
                        act.wait_ge(S("conv_done"), tile0 + n - 1)
                    out_wait(act, ph, j, k, u)
                    apart()
                    act.activation(tmp[:, j % 2, :], out_bank(ph, j), ACT.Identity, scale=param("conv_w", 3 * 48 + tile0 + n),
                                   bias=param("conv_b", tile0 + n)).then_inc(S("conv_begun"), 1)
                    if j:
                        silu(ph, j - 1, k, u)
                    if j == ph.outs - 1:
                        silu(ph, j, k, u)
                return take

            def take_dt(ph, j, k, u):
                out_wait(act, ph, j, k, u)
                act.activation(dta[:, :], out_bank(ph, j), ACT.Abs,
                               bias=par[0:HEADS, PARAM_AT["dt_bias"], :]).then_inc(S("dt_abs"), 1)
                act.activation(aneg[:, 0:1], par[0:HEADS, PARAM_AT["a_log"], :], ACT.Exp).then_inc(S("dt_rate"), 1)
                act.wait_ge(S("dt_abs"), 1)
                act.activation(dtb[:, :], dta[:, :], ACT.Exp, scale=-1.0).then_inc(S("dt_exp"), 1)
                act.wait_ge(S("dt_exp"), 1)
                act.activation(dtb[:, :], dtb[:, :], ACT.Ln, bias=eps[0:HEADS, 3, :]).then_inc(S("dt_ln"), 1)
                act.wait_ge(S("cs_ready"), 1)
                act.dma_start(cs_dram, cs[:, :]).then_inc(S("cs_stored"), 16)
                act.wait_ge(S("dt_turned"), 1)
                act.activation(dtt[:, :, :, 0], bank[2][:, 0:2 * HEADS].rearrange("p (c h) -> p c h", c=2),
                               ACT.Copy).then_inc(S("dt_tokens"), 1)
                act.activation(ncs[:, :, :, 0], bank[2][:, 2 * HEADS:4 * HEADS].rearrange("p (c h) -> p c h", c=2),
                               ACT.Copy, scale=-1.0).then_inc(S("dt_tokens"), 1)

            def delta_rule():
                act.wait_ge(slab_done, by["wo"].slab0)
                act.wait_ge(S("mix_low_g1"), KT + CREDIT)
                act.dma_start(level_mask[:, :, :], inp["level_mask"]).then_inc(S("mask_landed"), 16)
                act.dma_start(pair_mask[:, :], inp["pair_mask"]).then_inc(S("mask_landed"), 16)
                act.dma_start(first_mask[:, :], inp["first_mask"]).then_inc(S("mask_landed"), 16)
                act.dma_start(sel[:, :], inp["sel"]).then_inc(S("mask_landed"), 16)
                act.dma_start(sel_t[:, :], inp["sel_t"]).then_inc(S("mask_landed"), 16)

                def flat(x):
                    return x[:, :, :].rearrange("p a b -> p (a b)")

                def keys(m):
                    for g in range(2):
                        if beyond(m, 1):
                            act.wait_ge(S("bonus_ready"), 2 * m)
                        act.dma_start(LW[g][:, :, :], inp["lora2"][2 * m + g]).then_inc(S(f"lora_landed{g}"), 16)
                        act.dma_start(VS[g][:, :], V[:, 2 * m + g, :]).then_inc(S(f"v_landed{g}"), 16)
                    for g in range(2):
                        if beyond(m, 1):
                            act.wait_ge(S("bonus_mm"), 2 * m)
                        apart()
                        act.activation(flat(SQ[g]), K[:, 2 * m + g, :], ACT.Square,
                                       scale=param("k_k", 2 * m + g)).then_inc(S("key_sq"), 1)

                def norms(m):
                    act.wait_ge(S("norm_mm"), m + 1)
                    act.activation(NR[:, :], bank[3][0:4, 0:T], ACT.Sqrt).then_inc(S("norm_ready"), 1)

                def gates(m):
                    for g in range(2):
                        act.wait_ge(S("lora_mm"), 2 * m + g + 1)
                        apart()
                        act.activation(flat(SG[g]), bank[4 * g + 3][:, 0:T], ACT.Sigmoid,
                                       bias=param("w0", 2 * m + g)).then_inc(S("decay_gate"), 1)
                        apart()
                        act.activation(AA[g][:, :], bank[4 * g + 3][:, T:2 * T], ACT.Sigmoid,
                                       bias=param("a0", 2 * m + g)).then_inc(S("rate_gate"), 1)

                def decays(m, g):
                    act.wait_ge(S("mid_ready"), 4 * m + 2 * g + 2)
                    if beyond(m, 1):
                        act.wait_ge(S("a_tilde"), 2 * m)
                        act.wait_ge(S("r_tilde"), 2 * m)
                    for c in range(2):
                        act.activation(EE[g][:, c, :], SC[g][:, c, :], ACT.Exp, scale=-DECAY,
                                       bias=kb[:, g, 0, c:c + 1]).then_inc(S("decayed"), 1)
                        act.activation(EI[g][:, c, :], SC[g][:, c, :], ACT.Exp, scale=DECAY,
                                       bias=kb[:, g, 1, c:c + 1]).then_inc(S("decayed"), 1)

                def output_gate(m, side):
                    for g in range(2):
                        act.wait_ge(S("gate_mm"), 2 * m + g + 1)
                        act.activation(GG[side][g][:, :], bank[4 * g + 3][:, 0:T], ACT.Copy).then_inc(S("gate_ready"), 1)

                def token_major(m, side):
                    for g in range(2):
                        act.wait_ge(S("turned"), 2 * m + g + 1)
                        act.activation(flat(TOK[side][g]), bank[4 * g + 3][:, :], ACT.Copy).then_inc(S("token_major"), 1)

                def inverse_begun(m):
                    for g in range(2):
                        act.wait_ge(S("t_mm"), 12 * m + g + 1)
                        act.activation(flat(TI[g]), bank[4 * g + 1][:, :], ACT.Copy).then_inc(S("t_copied"), 1)

                def output(k):
                    for g in range(2):
                        act.wait_ge(S("y_mm"), 4 * k + g + 3)
                        act.activation(YY[g][:, :], bank[4 * g + 1][:, 0:T], ACT.Copy).then_inc(S("y_ready"), 1)
                    for g in range(2):
                        act.wait_ge(S("y_centred"), 2 * k + g + 1)
                        act.activation(SY[g][:, :], YC[g][:, :], ACT.Square).then_inc(S("y_sq"), 1)
                    act.wait_ge(S("y_var_mm"), 2 * k + 2)
                    act.activation(YV[:, :], bank[0][0:4, 0:T], ACT.Sqrt, scale=1.0 / 64,
                                   bias=eps[0:4, 1, :]).then_inc(S("y_std"), 1)

                def output_high(k):
                    for g in range(2):
                        act.wait_ge(S("y_gated"), 2 * k + g + 1)
                        apart()
                        act.activation(YR[:, 0, 2 * k + g, :], YC[g][:, :], ACT.Copy).then_inc(S("y_high"), 1)

                def turn(k, side, post, pre):
                    if pre:
                        keys(k + 1)
                    for lev in range(len(LEVELS)):
                        if lev < len(LEVELS) - 1:
                            for g in range(2):
                                act.wait_ge(S("t_mm"), 12 * k + 2 * lev + g + 3)
                                act.activation(flat(TI[g]), bank[4 * g + 2][:, :], ACT.Copy).then_inc(S("t_copied"), 1)
                        if lev == 3 and post:
                            output_high(k - 1)
                        if pre:
                            if lev == 0:
                                norms(k + 1)
                            elif lev == 1:
                                gates(k + 1)
                            elif lev == 2:
                                decays(k + 1, 0)
                            elif lev == 3:
                                decays(k + 1, 1)
                                output_gate(k + 1, 1 - side)
                            elif lev == 4:
                                token_major(k + 1, 1 - side)
                    for c in range(2):
                        for g in range(2):
                            act.wait_ge(S("rhs_mm"), 4 * k + 2 * c + g + 1)
                            if c == 0:
                                act.activation(RH[g][:, 0:2, :], bank[4 * g + 3][:, 0:P].rearrange(
                                    "p (a b) -> p a b", a=2), ACT.Copy).then_inc(S("rhs_ready"), 1)
                            else:
                                for h in range(2):
                                    act.activation(RH[g][:, 2 + h, :], bank[4 * g + 3 - h][:, P + 64 * h:P + 64 * h + 64],
                                                   ACT.Copy).then_inc(S("rhs_ready"), 1)
                        for g in range(2):
                            act.wait_ge(S("sa_mm"), 4 * k + 2 * c + g + 1)
                            act.activation(SA[g][:, 2 * c:2 * c + 2, :], bank[4 * g][:, 128 * c:128 * c + 128].rearrange(
                                "p (a b) -> p a b", a=2), ACT.Copy).then_inc(S("sa_ready"), 1)
                    output(k)
                    if pre:
                        inverse_begun(k + 1)

                keys(0)
                norms(0)
                gates(0)
                decays(0, 0)
                decays(0, 1)
                output_gate(0, 0)
                token_major(0, 0)
                inverse_begun(0)
                pair_turns(act, turn)
                output_high(PAIRS - 1)

            def ssd():
                act.wait_ge(slab_done, by["so"].slab0)
                act.wait_ge(S("cs_stored"), 16)

                def load_bc(k):
                    act.dma_start(CSB[:, :, :], cs_dram.rearrange("(g h) t -> g h t", h=8)[k].partition_broadcast(P)
                                  ).then_inc(S("csb_landed"), 16)
                    act.dma_start(BST[:, :], BC[:, k, :]).then_inc(S("bst_landed"), 16)

                def load_x(k):
                    groups = XC[:, :, :].rearrange("p (g a) t -> p g (a t)", g=GROUPS)
                    act.dma_start(XST[:, :, :].rearrange("p a b -> p (a b)"), groups[:, k, :]).then_inc(
                        S("xst_landed"), 16)

                def body(k, last=False):
                    for h in range(8):
                        act.wait_ge(S("seg_ready"), 16 * k + 2 * h + 2)
                        if h >= 2:
                            act.wait_ge(S("ssd_y_mm"), 8 * k + h - 1)
                        act.activation(GE[h % 2][:, :], SEG[h % 2][:, :], ACT.Exp).then_inc(S("ge_ready"), 1)
                    if not last:
                        load_bc(k + 1)
                    for t in range(4):
                        act.wait_ge(S("ys_gated"), 4 * k + t + 1)
                        if t >= 2:
                            act.wait_ge(S("ssd_y_mm"), 8 * k + t + 5)
                        act.activation(SQS[t], YG[:, t, :], ACT.Square).then_inc(S("ys_sq"), 1)
                    if not last:
                        load_x(k + 1)
                    act.wait_ge(S("ys_sq_mm"), 4 * k + 4)
                    act.activation(RST[:, :], bank[7][:, 0:T], ACT.Sqrt, scale=1.0 / 512,
                                   bias=eps[:, 2, :]).then_inc(S("ys_std"), 1)
                    for t in range(4):
                        act.wait_ge(S("ys_normed"), 4 * k + t + 1)
                        apart()
                        act.activation(YS[:, 0, 4 * k + t, :], YG[:, t, :], ACT.Copy).then_inc(S("ys_high"), 1)

                load_bc(0)
                load_x(0)
                loop(act, GROUPS - 1, body)
                body(GROUPS - 1, last=True)

            act.wait_ge(S("par_landed"), 16)
            prepare(by["r"], 0, 0, 0)
            prepare(by["r"], 1, 0, 0)
            mix_all_high("r")
            run_phase(act, by["r"], prepare, take_and_mix(lambda n: R[:, n, :], ["k", "w1"]))
            run_phase(act, by["w1"], prepare, take_copy(lambda n: lo_w[0:LORA, :], ACT.Tanh))
            run_phase(act, by["k"], prepare, take_and_mix(lambda n: K[:, n, :], ["v"]))
            run_phase(act, by["v"], prepare, take_and_mix(lambda n: V[:, n, :], ["a1"]))
            mix_all_high("g1")
            run_phase(act, by["a1"], prepare, take_copy(lambda n: lo_a[0:LORA, :]))
            run_phase(act, by["g1"], prepare, take_copy(lambda n: lo_g[:, n, :], ACT.Sigmoid), until=by["wo"].slab0)
            delta_rule()
            for i in range(SPLIT):
                prepare(by["wo"], by["wo"].slab0 + i, 0, 0)
            run_phase(act, by["wo"], prepare, nothing)
            layer_norm(0)
            run_phase(act, by["up0"], prepare, take_up(0))
            run_phase(act, by["down0"], prepare, nothing)
            layer_norm(1)
            act.dma_start(smask[:, :], inp["ssd_mask"]).then_inc(S("smask_landed"), 16)
            run_phase(act, by["x"], prepare, take_conv(0, lambda n: XC[:, n, :]), peel=1)
            run_phase(act, by["bc"], prepare, take_conv(NX, lambda n: BC[:, n, :]), peel=1)
            run_phase(act, by["z"], prepare, take_copy(lambda n: Z[:, n, :], ACT.Silu))
            run_phase(act, by["dt"], prepare, take_dt)
            ssd()
            run_phase(act, by["so"], prepare, nothing)
            layer_norm(2)
            run_phase(act, by["up1"], prepare, take_up(1))
            run_phase(act, by["down1"], prepare, nothing)
            layer_norm(3)

        @block.tensor
        def _(pe):
            def product(ph, acts, ready):
                turn = ph.unroll * ph.per

                def output(j, k, u, ready=None):
                    o = ph.out0 + j
                    pe.wait_ge(bank_free[o % 2], o // 2 + k * (u // 2) + CREDIT)
                    for q in range(ph.per):
                        s = ph.slab0 + j * ph.per + q
                        pe.wait_ge(low_ready, s + 1 + k * (u * ph.per))
                        w = wsp[:, s % 2, :, 0:ph.cols].rearrange("p a (t c) -> p a t c", t=ph.tiles)
                        for t in range(ph.tiles):
                            i = q * ph.tiles + t
                            first, last = i == 0, i == ph.per * ph.tiles - 1
                            if ready:
                                pe.wait_ge(ready[0], ready[1] + i + 1)
                            pe.matmul(out_bank(ph, j), w[:, 0, t, :], acts[:, 0, i, :], start=first, stop=False)
                            pe.matmul(out_bank(ph, j), w[:, 0, t, :], acts[:, 1, i, :], start=False, stop=False)
                            mm = pe.matmul(out_bank(ph, j), w[:, 1, t, :], acts[:, 0, i, :], start=False, stop=last)
                        mm.then_inc(slab_done, 1)

                output(0, 0, 0, ready)
                u = 2
                n = (ph.outs - 1) // u

                def body(k):
                    for j in range(u):
                        output(1 + j, k, u)

                loop(pe, n, body)
                for j in range(1 + n * u, ph.outs):
                    output(j, 0, 0)

            def layer_norm(i):
                pe.wait_ge(S("ln_acc"), KT * (i + 1) + CREDIT)
                pe.matmul(bank[2][:, 0:T], ones, tmp[:, 0, :], start=True, stop=True).then_inc(S("ln_sum"), 1)
                for n in range(KT):
                    pe.wait_ge(S("ln_sq"), KT * i + n + 1)
                    pe.matmul(bank[3][:, 0:T], ones, LSQ[:, n, :], start=n == 0,
                              stop=n == KT - 1).then_inc(S("ln_sqsum"), 1)

            def flat(x):
                return x[:, :, :].rearrange("p a b -> p (a b)")

            def delta_rule():
                pe.wait_ge(bank_free[0], (by["wo"].out0 + 1) // 2 + CREDIT)
                pe.wait_ge(bank_free[1], by["wo"].out0 // 2 + CREDIT)
                pe.wait_ge(S("mask_landed"), 80)

                def rows(x, h):
                    return x[64 * h:64 * h + 64]

                def norm_sums(m):
                    for g in range(2):
                        pe.wait_ge(S("key_sq"), 2 * m + g + 1)
                        mm = pe.matmul(bank[3][0:4, 0:T], sel[:, 4 * g:4 * g + 4], flat(SQ[g]), start=g == 0, stop=g == 1)
                    mm.then_inc(S("norm_mm"), 1)

                def lora(m):
                    pe.wait_ge(S("norm_ready"), m + 1)
                    for g in range(2):
                        pe.wait_ge(S(f"lora_landed{g}"), 16 * m + 16)
                        pe.matmul(bank[4 * g + 3][:, 0:T], LW[g][0:LORA, 0, :], lo_w[0:LORA, :], start=True, stop=True)
                        pe.matmul(bank[4 * g + 3][:, T:2 * T], LW[g][0:LORA, 1, :], lo_a[0:LORA, :], start=True,
                                  stop=True).then_inc(S("lora_mm"), 1)

                def norm_spread(m):
                    pe.wait_ge(S("norm_inv"), m + 1)
                    for g in range(2):
                        pe.wait_ge(S("rate_gate"), 2 * m + g + 1)
                        pe.matmul(bank[4 * g + 3][:, 0:T], sel_t[:, P * g:P * g + P], NR[:, :], start=True,
                                  stop=True).then_inc(S("norm_spread"), 1)

                def output_gate(m):
                    for g in range(2):
                        pe.wait_ge(S("kk_ready"), 2 * m + g + 1)
                        pe.matmul(bank[4 * g + 3][:, 0:T], LW[g][:, 2, :], lo_g[:, 0, :], start=True, stop=False)
                        pe.matmul(bank[4 * g + 3][:, 0:T], LW[g][:, 3, :], lo_g[:, 1, :], start=False,
                                  stop=True).then_inc(S("gate_mm"), 1)

                def token_major(m):
                    for g in range(2):
                        pe.wait_ge(S("gate_ready"), 2 * m + g + 1)
                        pe.wait_ge(S(f"v_landed{g}"), 16 * m + 16)
                        pe.transpose(bank[4 * g + 3][:, 0:P], VS[g][:, 0:P], ident)
                        pe.transpose(bank[4 * g + 3][:, P:2 * P], VS[g][:, P:2 * P], ident)
                        pe.wait_ge(S("b_tilde"), 2 * m + g + 1)
                        pe.transpose(bank[4 * g + 3][:, 2 * P:3 * P], BT[g][:, 0, :], ident)
                        pe.wait_ge(S("k_tilde"), 2 * m + g + 1)
                        pe.transpose(bank[4 * g + 3][:, 3 * P:4 * P], KW[g][:, 0, :], ident).then_inc(S("turned"), 1)

                def bonus(m):
                    for g in range(2):
                        pe.wait_ge(S("bonus_in"), 2 * m + g + 1)
                        pe.matmul(bank[4 * g + 2][:, T:2 * T], bones, flat(SQ[g]), start=True, stop=True).then_inc(S("bonus_mm"), 1)

                def mean(k, g):
                    pe.wait_ge(S("y_ready"), 2 * k + g + 1)
                    pe.matmul(bank[4 * g + 3][:, 0:T], bones, YY[g][:, :], start=True, stop=True).then_inc(S("y_sum_mm"), 1)

                def variance(k):
                    for g in range(2):
                        pe.wait_ge(S("y_sq"), 2 * k + g + 1)
                        pe.matmul(bank[0][0:4, 0:T], sel[:, 4 * g:4 * g + 4], SY[g][:, :], start=g == 0,
                                  stop=g == 1).then_inc(S("y_var_mm"), 1)

                def output_spread(k):
                    pe.wait_ge(S("y_rstd"), k + 1)
                    for g in range(2):
                        pe.matmul(bank[4 * g + 3][:, 0:T], sel_t[:, P * g:P * g + P], YV[:, :], start=True,
                                  stop=True).then_inc(S("y_spread"), 1)

                def pair_products(m, side, k=None):
                    for g in range(2):
                        if k is not None:
                            pe.wait_ge(S("y_ready"), 2 * k + g + 1)
                        pe.wait_ge(S("a_tilde"), 2 * m + g + 1)
                        pe.wait_ge(S("r_tilde"), 2 * m + g + 1)
                        for c in range(2):
                            for h in range(2):
                                mm = pe.matmul(bank[4 * g + h][:, T * c:T * c + T], rows(BT[g], h)[:, c, :],
                                               rows(AR[side][g], h)[:, c, :, :].rearrange("p a b -> p (a b)"),
                                               start=True, stop=True)
                        mm.then_inc(S("attn_b"), 1)
                        if k is not None:
                            mean(k, g)
                    for g in range(2):
                        pe.wait_ge(S("bonus_ready"), 2 * m + g + 1)
                        pe.wait_ge(S("token_major"), 2 * m + g + 1)
                        if k is not None:
                            pe.wait_ge(S("y_centred"), 2 * k + g + 1)
                        for c in range(2):
                            for h in range(2):
                                mm = pe.matmul(bank[4 * g + 2 + h][:, T * c:T * c + T], rows(KW[g], h)[:, c, :],
                                               rows(AR[side][g], h)[:, c, :, :].rearrange("p a b -> p (a b)"),
                                               start=True, stop=True)
                        mm.then_inc(S("attn_k"), 1)
                    if k is not None:
                        pe.wait_ge(S("lm1_ready"), 4 * m + 2)
                        variance(k)
                    for g in range(2):
                        pe.wait_ge(S("u_ready"), 14 * m + g + 1)
                        for p in range(4):
                            mm = pe.transpose(bank[4 * g + 1][:, P * p:P * p + P], UI[g][:, p, :], ident)
                        mm.then_inc(S("t_mm"), 1)

                def turn(k, side, post, pre):
                    m = k + 1
                    tok, ar = TOK[side], AR[side]
                    for lev in range(len(LEVELS)):
                        if lev == 0 and post:
                            pe.wait_ge(S("y_std"), k)
                        for g in range(2):
                            pe.wait_ge(S("t_copied"), 12 * k + 2 * lev + g + 1)
                            for p in range(4):
                                mm = pe.matmul(bank[4 * g][:, P * p:P * p + P], LM1[g][:, p, 0:P], TI[g][:, p, :],
                                               start=True, stop=True)
                            mm.then_inc(S("x_mm"), 1)
                        if lev == 1 and post:
                            if pre:
                                pe.wait_ge(S("norm_ready"), m + 1)
                            output_spread(k - 1)
                        if lev == 5 and pre:
                            token_major(m)
                        for g in range(2):
                            pe.wait_ge(S("x_ready"), 12 * k + 2 * lev + g + 1)
                            pe.wait_ge(S("u_ready"), 14 * k + 2 * lev + g + 1)
                            if lev == 0:
                                pe.wait_ge(S("lm2_ready"), 4 * k + 2 * g + 2)
                            for p in range(4):
                                mm = pe.matmul(bank[4 * g + 1][:, P * p:P * p + P], XI[g][:, p, :], UI[g][:, p, :],
                                               start=True, stop=True)
                            mm.then_inc(S("u_mm"), 1)
                        for g in range(2):
                            if lev < len(LEVELS) - 1:
                                pe.wait_ge(S("u_ready"), 14 * k + 2 * lev + g + 3)
                                for p in range(4):
                                    mm = pe.transpose(bank[4 * g + 2][:, P * p:P * p + P], UI[g][:, p, :], ident)
                                mm.then_inc(S("t_mm"), 1)
                        if pre:
                            if lev == 0:
                                norm_sums(m)
                            elif lev == 1:
                                if post:
                                    pe.wait_ge(S("y_normed"), 2 * k)
                                lora(m)
                            elif lev == 2:
                                norm_spread(m)
                            elif lev == 3:
                                output_gate(m)
                            elif lev == 5:
                                bonus(m)
                    for c in range(2):
                        for g in range(2):
                            if c:
                                pe.wait_ge(S("state_ready"), 2 * k + g + 1)
                            elif pre:
                                pe.wait_ge(S("token_major"), 2 * m + g + 1)
                            else:
                                pe.wait_ge(S("y_normed"), 2 * k)
                            for h in range(2):
                                to = bank[4 * g + 3 - c * h][:, P * c + 64 * h:P * c + 64 * h + 64]
                                if c:
                                    pe.matmul(to, rows(ar[g], h)[:, 1, 0, :], rows(S0[g], h)[:, :], start=True, stop=False)
                                mm = pe.matmul(to, LM2[g][:, 2 * h + c, 0:P], tok[g][:, c, 64 * h:64 * h + 64],
                                               start=c == 0, stop=True)
                            mm.then_inc(S("rhs_mm"), 1)
                        for g in range(2):
                            pe.wait_ge(S("rhs_ready"), 6 * k + (2 * g + 4 if c else g + 1))
                            pe.wait_ge(S("u_ready"), 14 * k + 2 * len(LEVELS) + g + 1)
                            for h in range(2):
                                mm = pe.matmul(bank[4 * g][:, P * c + 64 * h:P * c + 64 * h + 64], UI[g][:, 2 * h + c, :],
                                               RH[g][:, 2 * c + h, :], start=True, stop=True)
                            mm.then_inc(S("sa_mm"), 1)
                        if c == 0:
                            for g in range(2):
                                pe.wait_ge(S("sa_ready"), 4 * k + g + 1)
                                if pre:
                                    pe.wait_ge(S("bonus_ready"), 2 * m + g + 1)
                                for h in range(2):
                                    to = bank[4 * g + 2][64 * h:64 * h + 64, 0:64]
                                    pe.matmul(to, tok[g][:, 2, 64 * h:64 * h + 64], SA[g][:, h, :], start=True, stop=False)
                                    mm = pe.matmul(to, tok[g][:, 3, 64 * h:64 * h + 64], tok[g][:, 0, 64 * h:64 * h + 64],
                                                   start=False, stop=True)
                                mm.then_inc(S("state_mm"), 1)
                        for g in range(2):
                            pe.wait_ge(S("sa_ready"), 4 * k + 2 * c + g + 1)
                            for h in range(2):
                                to = bank[4 * g + 1][64 * h:64 * h + 64, P * c:P * c + P]
                                p = 2 * h + c
                                pe.matmul(to, SA[g][:, 2 * c + h, :], LM1[g][:, p, P:2 * P], start=True, stop=False)
                                mm = pe.matmul(to, tok[g][:, c, 64 * h:64 * h + 64], LM2[g][:, p, P:2 * P],
                                               start=False, stop=c == 0)
                                if c:
                                    mm = pe.matmul(to, rows(S0[g], h)[:, :], rows(ar[g], h)[:, 1, 1, :],
                                                   start=False, stop=True)
                            mm.then_inc(S("y_mm"), 1)
                    if pre:
                        pair_products(m, 1 - side, k)
                    else:
                        mean(k, 0)
                        mean(k, 1)
                        variance(k)
                        output_spread(k)

                norm_sums(0)
                lora(0)
                norm_spread(0)
                output_gate(0)
                token_major(0)
                bonus(0)
                pair_products(0, 0)
                pair_turns(pe, turn)

            def turn_dt():
                pe.wait_ge(S("cs_ready"), 1)
                half = ident[0:HEADS, 0:HEADS]
                for c in range(2):
                    pe.transpose(bank[2][:, HEADS * c:HEADS * c + HEADS], dtc[:, P * c:P * c + P], half)
                for c in range(2):
                    mm = pe.transpose(bank[2][:, HEADS * (2 + c):HEADS * (3 + c)], cs[:, P * c:P * c + P], half)
                mm.then_inc(S("dt_turned"), 1)

            def ssd():
                pe.wait_ge(bank_free[0], (by["so"].out0 + 1) // 2 + CREDIT)
                pe.wait_ge(bank_free[1], by["so"].out0 // 2 + CREDIT)
                pe.wait_ge(S("dt_tokens"), 2)

                def body(k):
                    pe.wait_ge(S("bst_landed"), 16 * k + 16)
                    pe.matmul(bank[0][:, 0:T], BST[:, 0:P], BC[:, GROUPS + k, :], start=True, stop=True)
                    pe.matmul(bank[0][:, T:T + P], BST[:, P:T], BC[:, GROUPS + k, P:T], start=True,
                              stop=True).then_inc(S("cb_mm"), 1)
                    pe.wait_ge(S("xst_landed"), 16 * k + 16)
                    for c in range(2):
                        for t in range(4):
                            mm = pe.transpose(bank[1 + c][:, P * t:P * t + P], XST[:, t, P * c:P * c + P], ident)
                        mm.then_inc(S("x_turned"), 1)
                    pe.wait_ge(S("xdt_ready"), 2 * k + 2)
                    for h in range(8):
                        pe.wait_ge(S("g_ready"), 8 * k + h + 1)
                        half = 64 * (h % 2)
                        to = bank[3 + h // 2]
                        pe.matmul(to[half:half + 64, 0:T], XDT[:, 0, h, :], GE[h % 2][:, 0:T], start=True, stop=False)
                        pe.matmul(to[half:half + 64, P:T], XDT[:, 1, h, :], GE[h % 2][:, T:T + P], start=False,
                                  stop=True).then_inc(S("ssd_y_mm"), 1)
                    for t in range(4):
                        pe.wait_ge(S("ys_sq"), 4 * k + t + 1)
                        pe.matmul(bank[7][:, 0:T], ones, SQS[t], start=t == 0, stop=t == 3).then_inc(S("ys_sq_mm"), 1)

                loop(pe, GROUPS, body)

            pe.wait_ge(S("basic_landed"), 16)
            for name in ("r", "w1", "k", "v", "a1", "g1"):
                product(by[name], MIXED[name], (S("mix_low_" + name), CREDIT))
            delta_rule()
            pe.wait_ge(S("y_normed"), KT)
            product(by["wo"], YR, (S("y_low"), 0))
            layer_norm(0)
            product(by["up0"], XS, (S("ln_low"), 0))
            product(by["down0"], HID, (S("hid_low"), CREDIT))
            layer_norm(1)
            for name in ("x", "bc", "z", "dt"):
                product(by[name], XS, (S("ln_low"), KT) if name == "x" else None)
            turn_dt()
            ssd()
            product(by["so"], YS, (S("ys_low"), CREDIT))
            layer_norm(2)
            product(by["up1"], XS, (S("ln_low"), 2 * KT))
            product(by["down1"], HID, (S("hid_low"), NF + CREDIT))
            layer_norm(3)

        @block.vector
        def _(dve):
            def prepare(ph, s, k, turn):
                dve.wait_ge(high_ready, s + 1 + k * turn)
                dve.tensor_tensor(wsp[:, s % 2, 1, 0:ph.cols], raw[:, s % RAW, 0:ph.cols],
                                  wsp[:, s % 2, 0, 0:ph.cols].bitcast(F32), ALU.subtract).then_inc(low_ready, 1)

            def mix(name, n, buf, after=None):
                mu = KT * MU[name] + n
                if after is not None:
                    dve.wait_ge(S("mix_low_" + name), after)
                dve.tensor_scalar(tmp[:, buf, :], H[:, n, :], omm[:, mu, :], None, ALU.mult).then_inc(S("mix_begun_" + name), 1)
                dve.wait_ge(S("mix_begun_" + name), n + 1)
                dve.scalar_tensor_tensor(out=tmp[:, buf, 1:T], in0=H[:, n, 0:T - 1], scalar=param("mu", mu),
                                         in1=tmp[:, buf, 1:T], op0=ALU.mult, op1=ALU.add).then_inc(S("mixed_" + name), 1)

            def mix_low(name, n, buf):
                dve.wait_ge(S("mix_high_" + name), n + 1)
                dve.tensor_tensor(MIXED[name][:, 1, n, :], tmp[:, buf, :], MIXED[name][:, 0, n, :].bitcast(F32),
                                  ALU.subtract).then_inc(S("mix_low_" + name), 1)

            def mix_all(name):
                mix(name, 0, 0)
                mix(name, 1, 1)
                mix_low(name, 0, 0)

                def body(k):
                    for j in range(2):
                        mix(name, 2 * k + j + 2, j, after=2 * k + j + 1 + CREDIT)
                        mix_low(name, 2 * k + j + 1, 1 - j)

                loop(dve, KT // 2 - 1, body)
                mix_low(name, KT - 1, 1)

            def mixing(names):
                def before(ph, j, k, u):
                    for i, name in enumerate(names):
                        mix(name, j + k * u, i, after=j + k * u + CREDIT)

                def take(ph, j, k, u):
                    for i, name in enumerate(names):
                        mix_low(name, j + k * u, i)
                return before, take

            def nothing(ph, j, k, u):
                pass

            def take_residual(ph, j, k, u):
                n = j + k * u
                out_wait(dve, ph, j, k, u)
                dve.scalar_tensor_tensor(out=H[:, n, :], in0=H[:, n, :], scalar=ALPHA, in1=out_bank(ph, j),
                                         op0=ALU.mult, op1=ALU.add).then_inc(free_sem(ph, j), 1)

            def take_up(layer):
                def take(ph, j, k, u):
                    if j % 2:
                        n = j // 2 + k * (u // 2)
                        out_wait(dve, ph, j, k, u)
                        dve.wait_ge(free_sem(ph, j - 1), freed(ph, j - 1, k, u))
                        dve.wait_ge(S("hid_low"), NF * layer + n + CREDIT)
                        dve.tensor_tensor(tmp[:, 1 + (j // 2) % 2, :], tmp[:, 0, :], out_bank(ph, j),
                                          ALU.mult).then_inc(free_sem(ph, j), 1)
                return take

            def layer_norm(i):
                dve.wait_ge(S("ln_sum"), i + 1)

                def centre(k):
                    for j in range(4):
                        n = 4 * k + j
                        dve.scalar_tensor_tensor(out=H[:, n, :], in0=bank[2][:, 0:T], scalar=-1.0 / D, in1=H[:, n, :],
                                                 op0=ALU.mult, op1=ALU.add).then_inc(S("ln_centred"), 1)

                loop(dve, KT // 4, centre)
                dve.wait_ge(S("ln_std"), i + 1)
                dve.reciprocal(tmp[:, 0, :], tmp[:, 0, :]).then_inc(S("ln_rstd"), 1)
                dve.wait_ge(S("ln_rstd"), i + 1)

                def scale(k):
                    for j in range(4):
                        n = 4 * k + j
                        dve.tensor_tensor(H[:, n, :], H[:, n, :], tmp[:, 0, :], ALU.mult).then_inc(S("ln_scaled"), 1)

                loop(dve, KT // 4, scale)

            def take_conv(tile0):
                def take(ph, j, k, u):
                    n = j + k * u
                    dve.wait_ge(S("conv_begun"), tile0 + n + 1)
                    for tap in (2, 1, 0):
                        lag = 3 - tap
                        d = tmp[:, j % 2, :]
                        if lag > 1:
                            dve.wait_ge(S("conv_tap"), 2 * (tile0 + n) + lag - 1)
                        i = dve.scalar_tensor_tensor(out=d[:, lag:T], in0=out_bank(ph, j)[:, 0:T - lag],
                                                     scalar=param("conv_w", tap * 48 + tile0 + n), in1=d[:, lag:T],
                                                     op0=ALU.mult, op1=ALU.add)
                        i.then_inc(S("conv_tap") if tap else free_sem(ph, j), 1)
                return take

            def take_dt(ph, j, k, u):
                bias = par[0:HEADS, PARAM_AT["dt_bias"], :]
                out_wait(dve, ph, j, k, u)
                dve.wait_ge(S("dt_abs"), 1)
                dve.tensor_scalar(dtc[:, :], out_bank(ph, j), bias, 0.0, ALU.add, ALU.max).then_inc(free_sem(ph, j), 1)
                dve.wait_ge(free_sem(ph, j), freed(ph, j, k, u))
                dve.wait_ge(S("dt_ln"), 1)
                dve.tensor_tensor(dtc[:, :], dtc[:, :], dtb[:, :], ALU.add).then_inc(S("dt_step"), 1)
                dve.wait_ge(S("dt_rate"), 1)
                dve.wait_ge(S("dt_step"), 1)
                dve.tensor_scalar(dta[:, :], dtc[:, :], aneg[:, 0:1], -1.0, ALU.mult, ALU.mult).then_inc(S("dt_step"), 1)
                dve.wait_ge(S("dt_step"), 2)
                for c in range(2):
                    dve.tensor_tensor_scan(cs[:, P * c:P * c + P], ones[0:HEADS, :], dta[:, P * c:P * c + P], 0.0,
                                           ALU.mult, ALU.add).then_inc(S("dt_step"), 1)
                dve.wait_ge(S("dt_step"), 4)
                dve.tensor_copy(aneg[:, 1:2], cs[:, P - 1:P]).then_inc(S("dt_step"), 1)
                dve.wait_ge(S("dt_step"), 5)
                dve.tensor_scalar(cs[:, 0:P], cs[:, 0:P], aneg[:, 1:2], None, ALU.subtract).then_inc(S("cs_ready"), 1)

            def delta_rule():
                dve.wait_ge(S("mask_landed"), 80)
                for g in range(2):
                    dve.memset(SC[g][:, :, 0:1], 0.0).then_inc(S("scan_zeroed"), 1)
                dve.wait_ge(S("scan_zeroed"), 2)

                def bc(m, n):
                    return m.unsqueeze(1).broadcast_to([P, n, m.shape[-1]])

                def flat(x):
                    return x[:, :, :].rearrange("p a b -> p (a b)")

                def two(x):
                    return x.rearrange("p (a b) -> p a b", a=2)

                def four(x):
                    return x.rearrange("p (a b) -> p a b", a=4)

                def scaled_keys(m):
                    for g in range(2):
                        if beyond(m, 1):
                            dve.wait_ge(S("kka_ready"), 2 * m)
                            dve.wait_ge(S("a_tilde"), 2 * m)
                        dve.tensor_scalar(flat(KK[g]), K[:, 2 * m + g, :], param("k_k", 2 * m + g), None,
                                          ALU.mult).then_inc(S("key_scaled"), 1)

                def inverse_norms(m):
                    dve.wait_ge(S("norm_ready"), m + 1)
                    dve.tensor_scalar(NR[:, :], NR[:, :], 1e-12, None, ALU.max).then_inc(S("norm_floor"), 1)
                    dve.wait_ge(S("norm_floor"), m + 1)
                    dve.reciprocal(NR[:, :], NR[:, :]).then_inc(S("norm_inv"), 1)

                def scans(m):
                    for g in range(2):
                        dve.wait_ge(S("decay_gate"), 2 * m + g + 1)
                        if beyond(m, 1):
                            dve.wait_ge(S("decayed"), 8 * m)
                        for c in range(2):
                            dve.tensor_tensor_scan(SC[g][:, c, 1:P + 1], ones, SG[g][:, c, :], 0.0,
                                                   ALU.mult, ALU.add).then_inc(S("scanned"), 1)
                    for g in range(2):
                        dve.wait_ge(S("scanned"), 4 * m + 2 * g + 2)
                        for i, sign in enumerate((DECAY, -DECAY)):
                            dve.tensor_scalar(kb[:, g, i, :], SC[g][:, :, 64], sign, None, ALU.mult).then_inc(S("mid_ready"), 1)

                def normed_keys(m):
                    for g in range(2):
                        dve.wait_ge(S("norm_spread"), 2 * m + g + 1)
                        dve.wait_ge(S("key_scaled"), 2 * m + g + 1)
                        dve.tensor_tensor(flat(KK[g]), flat(KK[g]), bank[4 * g + 3][:, 0:T], ALU.mult).then_inc(S("kk_ready"), 1)

                def rate_factors(m):
                    for g in range(2):
                        dve.wait_ge(S("rate_gate"), 2 * m + g + 1)
                        dve.wait_ge(S("scanned"), 4 * m + 2 * g + 2)
                        dve.tensor_scalar(flat(SG[g]), AA[g][:, :], param("k_a", 2 * m + g), omka[:, 2 * m + g, :],
                                          ALU.mult, ALU.add).then_inc(S("rate_factor"), 1)

                def rates(m):
                    for g in range(2):
                        dve.wait_ge(S("decayed"), 8 * m + 4 * g + 4)
                        dve.wait_ge(S("kka_ready"), 2 * m + g + 1)
                        dve.tensor_tensor(BT[g][:, :, :], SQ[g][:, :, :], EI[g][:, :, 1:P + 1], ALU.mult).then_inc(S("b_tilde"), 1)
                    for g in range(2):
                        dve.wait_ge(S("key_ready"), 2 * m + g + 1)
                        dve.tensor_tensor(KW[g][:, :, :], SG[g][:, :, :], EI[g][:, :, 1:P + 1], ALU.mult).then_inc(S("k_tilde"), 1)

                def bonus_inputs(m):
                    for g in range(2):
                        dve.wait_ge(S("b_tilde"), 2 * m + g + 1)
                        dve.scalar_tensor_tensor(out=flat(SQ[g]), in0=R[:, 2 * m + g, :], scalar=param("r_k", 2 * m + g),
                                                 in1=flat(SG[g]), op0=ALU.mult, op1=ALU.mult).then_inc(S("bonus_in"), 1)

                def bonuses(m, side):
                    for g in range(2):
                        dve.wait_ge(S("bonus_mm"), 2 * m + g + 1)
                        dve.wait_ge(S(f"v_landed{g}"), 16 * m + 16)
                        if beyond(m, 2):
                            dve.wait_ge(S("y_bonus"), 2 * m - 2)
                        dve.tensor_tensor(BV[side][g][:, :], bank[4 * g + 2][:, T:2 * T], VS[g][:, :],
                                          ALU.mult).then_inc(S("bonus_ready"), 1)
                    for g in range(2):
                        dve.tensor_tensor(dsc[:, 2 * side + g, :], EE[g][:, 0, P:P + 1], EI[g][:, 1, 0:1],
                                          ALU.mult).then_inc(S("carry"), 1)
                        dve.scalar_tensor_tensor(out=AR[side][g][:, :, 0, :], in0=KK[g][:, :, :], scalar=-1.0,
                                                 in1=EE[g][:, :, 0:P], op0=ALU.mult, op1=ALU.mult).then_inc(S("a_tilde"), 1)

                def pair_products(m, k=None):
                    pairs = bc(pair_mask[:, :], 2)
                    for g in range(2):
                        dve.wait_ge(S("attn_b"), 2 * m + g + 1)
                        for h in range(2):
                            dve.tensor_tensor(LM1[g][:, 2 * h:2 * h + 2, :], two(bank[4 * g + h][:, :]), pairs,
                                              ALU.mult).then_inc(S("lm1_ready"), 1)
                        if k is not None:
                            centre(k, g)
                    for g in range(2):
                        dve.wait_ge(S("lm1_ready"), 4 * m + 2 * g + 2)
                        dve.tensor_tensor(UI[g][:, :, :], LM1[g][:, :, 0:P], bc(first_mask[:, :], 4), ALU.mult).then_inc(S("u_begun"), 1)
                        dve.wait_ge(S("u_begun"), 2 * m + g + 1)
                        dve.tensor_tensor(UI[g][:, :, :], UI[g][:, :, :], bc(ident, 4), ALU.add).then_inc(S("u_ready"), 1)
                    for g in range(2):
                        dve.wait_ge(S("attn_k"), 2 * m + g + 1)
                        for h in range(2):
                            dve.tensor_tensor(LM2[g][:, 2 * h:2 * h + 2, :], two(bank[4 * g + 2 + h][:, :]), pairs,
                                              ALU.mult).then_inc(S("lm2_ready"), 1)

                def centre(k, g):
                    dve.wait_ge(S("y_sum_mm"), 2 * k + g + 1)
                    if beyond(k, 1):
                        dve.wait_ge(S("y_low"), 2 * k)
                    dve.scalar_tensor_tensor(out=YC[g][:, :], in0=bank[4 * g + 3][:, 0:T], scalar=-1.0 / 64, in1=YY[g][:, :],
                                             op0=ALU.mult, op1=ALU.add).then_inc(S("y_centred"), 1)

                def inverse_deviations(k):
                    dve.wait_ge(S("y_std"), k + 1)
                    dve.reciprocal(YV[:, :], YV[:, :]).then_inc(S("y_rstd"), 1)

                def normed(k):
                    for g in range(2):
                        dve.wait_ge(S("y_spread"), 2 * k + g + 1)
                        dve.tensor_tensor(YC[g][:, :], YC[g][:, :], bank[4 * g + 3][:, 0:T], ALU.mult).then_inc(S("y_normed"), 1)

                def affine(k):
                    for g in range(2):
                        dve.wait_ge(S("y_normed"), 2 * k + g + 1)
                        dve.tensor_scalar(YC[g][:, :], YC[g][:, :], param("gn_g", 2 * k + g), param("gn_b", 2 * k + g),
                                          ALU.mult, ALU.add).then_inc(S("y_affine"), 1)

                def turn(k, side, post, pre):
                    m = k + 1
                    for lev in range(len(LEVELS)):
                        for g in range(2):
                            dve.wait_ge(S("x_mm"), 12 * k + 2 * lev + g + 1)
                            dve.tensor_tensor(XI[g][:, :, :], four(bank[4 * g][:, :]), bc(level_mask[:, lev, :], 4),
                                              ALU.mult).then_inc(S("x_ready"), 1)
                        if post and lev == 1:
                            normed(k - 1)
                        if post and lev == 2:
                            affine(k - 1)
                        if pre:
                            if lev == 0:
                                scaled_keys(m)
                            elif lev == 3:
                                normed_keys(m)
                            elif lev == 5:
                                bonus_inputs(m)
                        for g in range(2):
                            dve.wait_ge(S("u_mm"), 12 * k + 2 * lev + g + 1)
                            dve.tensor_tensor(UI[g][:, :, :], UI[g][:, :, :], four(bank[4 * g + 1][:, :]),
                                              ALU.add).then_inc(S("u_ready"), 1)
                        if post and lev == 0:
                            inverse_deviations(k - 1)
                        if pre:
                            if lev == 1:
                                inverse_norms(m)
                            elif lev == 2:
                                scans(m)
                            elif lev == 3:
                                rate_factors(m)
                            elif lev == 4:
                                rates(m)
                            elif lev == 5:
                                bonuses(m, 1 - side)
                    for g in range(2):
                        dve.wait_ge(S("state_mm"), 2 * k + g + 1)
                        dve.wait_ge(S("carry"), 2 * k + g + 1)
                        dve.tensor_scalar(S0[g][:, :], bank[4 * g + 2][:, 0:64], dsc[:, 2 * side + g, :], None,
                                          ALU.mult).then_inc(S("state_ready"), 1)
                    if pre:
                        pair_products(m, k)
                    else:
                        centre(k, 0)
                        centre(k, 1)
                        inverse_deviations(k)
                        normed(k)
                        affine(k)

                scaled_keys(0)
                inverse_norms(0)
                scans(0)
                normed_keys(0)
                rate_factors(0)
                rates(0)
                bonus_inputs(0)
                bonuses(0, 0)
                pair_products(0)
                pair_turns(dve, turn)

            def ssd():
                dve.wait_ge(S("smask_landed"), 16)
                dve.wait_ge(S("dt_tokens"), 2)

                def body(k):
                    dve.wait_ge(S("cb_mm"), k + 1)
                    dve.tensor_tensor(CBM[:, :], bank[0][:, 0:3 * P], smask[:, :], ALU.mult).then_inc(S("cbm_ready"), 1)
                    for c in range(2):
                        dve.wait_ge(S("x_turned"), 2 * k + c + 1)
                        dve.tensor_tensor(XDT[:, c, :, :], bank[1 + c][:, :].rearrange("p (h d) -> p h d", h=8),
                                          dtt[:, c, :, :].rearrange("p (g h) o -> p g h o", g=GROUPS)[:, k, :, :].broadcast_to([P, 8, 64]),
                                          ALU.mult).then_inc(S("xdt_ready"), 1)

                    def seg(h):
                        if h >= 2:
                            dve.wait_ge(S("ge_ready"), 8 * k + h - 1)
                        head = 8 * k + h
                        dve.tensor_scalar(SEG[h % 2][:, 0:T], CSB[:, h, :], ncs[:, 0, head, :], 0.0, ALU.add,
                                          ALU.min).then_inc(S("seg_ready"), 1)
                        dve.tensor_scalar(SEG[h % 2][:, T:T + P], CSB[:, h, P:T], ncs[:, 1, head, :], 0.0, ALU.add,
                                          ALU.min).then_inc(S("seg_ready"), 1)

                    dve.wait_ge(S("csb_landed"), 16 * k + 16)
                    dve.wait_ge(S("cbm_ready"), k + 1)
                    seg(0)
                    for h in range(8):
                        if h < 7:
                            seg(h + 1)
                        dve.wait_ge(S("ge_ready"), 8 * k + h + 1)
                        dve.tensor_tensor(GE[h % 2][:, :], GE[h % 2][:, :], CBM[:, :], ALU.mult).then_inc(S("g_ready"), 1)
                    for t in range(4):
                        n = 4 * k + t
                        dve.wait_ge(S("ssd_y_mm"), 8 * k + 2 * t + 2)
                        dve.wait_ge(S("xst_landed"), 16 * k + 16)
                        dve.wait_ge(S("ys_low"), 4 * k + CREDIT)
                        dve.scalar_tensor_tensor(out=YG[:, t, :], in0=XST[:, t, :], scalar=param("d_skip", n),
                                                 in1=bank[3 + t][:, 0:T], op0=ALU.mult, op1=ALU.add).then_inc(S("ys_skip"), 1)
                        dve.wait_ge(S("ys_skip"), n + 1)
                        dve.tensor_tensor(YG[:, t, :], YG[:, t, :], Z[:, n, :], ALU.mult).then_inc(S("ys_gated"), 1)
                    dve.wait_ge(S("ys_std"), k + 1)
                    dve.reciprocal(RST[:, :], RST[:, :]).then_inc(S("ys_rstd"), 1)
                    dve.wait_ge(S("ys_rstd"), k + 1)
                    for t in range(4):
                        n = 4 * k + t
                        dve.scalar_tensor_tensor(out=YG[:, t, :], in0=YG[:, t, :], scalar=param("norm_g", n), in1=RST[:, :],
                                                 op0=ALU.mult, op1=ALU.mult).then_inc(S("ys_normed"), 1)

                loop(dve, GROUPS, body)

            for i, e in enumerate((LN_EPS, GN_EPS, RMS_EPS, 1.0)):
                dve.memset(eps[:, i, :], e).then_inc(S("eps_set"), 1)
            dve.wait_ge(S("par_landed"), 16)
            for dst, name, n in ((omm, "mu", 6 * KT), (omka, "k_a", KT)):
                dve.tensor_scalar(dst[:, :, 0], par[:, PARAM_AT[name]:PARAM_AT[name] + n, 0], -1.0, 1.0, ALU.mult,
                                  ALU.add).then_inc(S("one_minus"), 1)
            dve.wait_ge(S("one_minus"), 2)
            dve.wait_ge(S("eps_set"), 4)
            dve.wait_ge(S("x_landed"), 16)
            dve.wait_ge(S("basic_landed"), 16)
            mix_all("r")
            prepare(by["r"], 0, 0, 0)
            prepare(by["r"], 1, 0, 0)
            for name, later, last in (("r", ["k", "w1"], "r"), ("w1", [], "r"), ("k", ["v"], "k"), ("v", ["a1"], "v")):
                dve.wait_ge(S("mix_low_" + last), KT + CREDIT)
                before, take = mixing(later)
                run_phase(dve, by[name], prepare, take, before)
            dve.wait_ge(S("mix_low_a1"), KT + CREDIT)
            mix_all("g1")
            run_phase(dve, by["a1"], prepare, nothing)
            run_phase(dve, by["g1"], prepare, nothing, until=by["wo"].slab0)
            delta_rule()
            prepare(by["wo"], by["wo"].slab0, 0, 0)
            dve.wait_ge(S("y_low"), KT)
            prepare(by["wo"], by["wo"].slab0 + 1, 0, 0)
            run_phase(dve, by["wo"], prepare, take_residual)
            layer_norm(0)
            run_phase(dve, by["up0"], prepare, take_up(0))
            run_phase(dve, by["down0"], prepare, take_residual)
            layer_norm(1)
            run_phase(dve, by["x"], prepare, take_conv(0))
            run_phase(dve, by["bc"], prepare, take_conv(NX))
            run_phase(dve, by["z"], prepare, nothing)
            run_phase(dve, by["dt"], prepare, take_dt)
            ssd()
            run_phase(dve, by["so"], prepare, take_residual)
            layer_norm(2)
            run_phase(dve, by["up1"], prepare, take_up(1))
            run_phase(dve, by["down1"], prepare, take_residual)
            layer_norm(3)

        @block.gpsimd
        def _(pool):
            def apart():
                pool.wait_ge(S("par_landed"), 16)

            def add_up(ph, i):
                pool.wait_ge(slab_done, ph.slab0)
                pool.memset(tmp[:, 0, :], 0.0).then_inc(S("acc_zeroed"), 1)
                pool.wait_ge(S("acc_zeroed"), i + 1)

                def body(k):
                    for j in range(2):
                        n = 2 * k + j
                        pool.wait_ge(free_sem(ph, j), freed(ph, j, k, 2))
                        pool.wait_ge(S("ln_acc"), KT * i + n + CREDIT)
                        apart()
                        pool.tensor_tensor(tmp[:, 0, :], tmp[:, 0, :], H[:, n, :], ALU.add).then_inc(S("ln_acc"), 1)

                loop(pool, KT // 2, body)

            def low_of_norm(i):
                def body(k):
                    pool.wait_ge(S("ln_high"), KT * i + k + 1)
                    apart()
                    pool.tensor_tensor(XS[:, 1, k, :], H[:, k, :], XS[:, 0, k, :].bitcast(F32),
                                       ALU.subtract).then_inc(S("ln_low"), 1)

                loop(pool, KT, body)

            def low_of_hidden(layer):
                def body(k):
                    for j in range(2):
                        n = 2 * k + j
                        pool.wait_ge(S("hid_high"), NF * layer + n + 1)
                        apart()
                        pool.tensor_tensor(HID[:, 1, n, :], tmp[:, 1 + j, :], HID[:, 0, n, :].bitcast(F32),
                                           ALU.subtract).then_inc(S("hid_low"), 1)

                loop(pool, NF // 2, body)

            def delta_rule():
                def flat(x):
                    return x[:, :, :].rearrange("p a b -> p (a b)")

                def rates(m):
                    for g in range(2):
                        pool.wait_ge(S("kk_ready"), 2 * m + g + 1)
                        pool.wait_ge(S("rate_gate"), 2 * m + g + 1)
                        pool.tensor_tensor(flat(SQ[g]), flat(KK[g]), AA[g][:, :], ALU.mult).then_inc(S("kka_ready"), 1)

                def keys(m, side):
                    for g in range(2):
                        pool.wait_ge(S("rate_factor"), 2 * m + g + 1)
                        apart()
                        pool.tensor_tensor(flat(SG[g]), K[:, 2 * m + g, :], flat(SG[g]), ALU.mult).then_inc(S("key_ready"), 1)
                    for g in range(2):
                        pool.wait_ge(S("decayed"), 8 * m + 4 * g + 4)
                        apart()
                        pool.tensor_tensor(AR[side][g][:, :, 1, :], R[:, 2 * m + g, :].rearrange("p (a b) -> p a b", a=2),
                                           EE[g][:, :, 1:P + 1], ALU.mult).then_inc(S("r_tilde"), 1)

                def gated(k, side):
                    for g in range(2):
                        pool.wait_ge(S("y_affine"), 2 * k + g + 1)
                        pool.wait_ge(S("bonus_ready"), 2 * k + g + 1)
                        pool.tensor_tensor(YC[g][:, :], YC[g][:, :], BV[side][g][:, :], ALU.add).then_inc(S("y_bonus"), 1)
                    for g in range(2):
                        pool.wait_ge(S("gate_ready"), 2 * k + g + 1)
                        pool.wait_ge(S("y_bonus"), 2 * k + g + 1)
                        pool.tensor_tensor(YC[g][:, :], YC[g][:, :], GG[side][g][:, :], ALU.mult).then_inc(S("y_gated"), 1)

                def low(k):
                    for g in range(2):
                        pool.wait_ge(S("y_high"), 2 * k + g + 1)
                        apart()
                        pool.tensor_tensor(YR[:, 1, 2 * k + g, :], YC[g][:, :], YR[:, 0, 2 * k + g, :].bitcast(F32),
                                           ALU.subtract).then_inc(S("y_low"), 1)

                def turn(k, side, post, pre):
                    if post:
                        gated(k - 1, 1 - side)
                    if pre:
                        rates(k + 1)
                    if post:
                        low(k - 1)
                    if pre:
                        keys(k + 1, 1 - side)

                rates(0)
                keys(0, 0)
                pair_turns(pool, turn)
                gated(PAIRS - 1, (PAIRS - 1) % 2)
                low(PAIRS - 1)

            def low_of_ssd():
                def body(k):
                    for t in range(4):
                        n = 4 * k + t
                        pool.wait_ge(S("ys_high"), n + 1)
                        apart()
                        pool.tensor_tensor(YS[:, 1, n, :], YG[:, t, :], YS[:, 0, n, :].bitcast(F32),
                                           ALU.subtract).then_inc(S("ys_low"), 1)

                loop(pool, GROUPS, body)

            mixes = ["mix_low_" + name for name in MU]
            for sem in (*bank_free, *map(S, ("ys_low", "ln_acc", "hid_low", *mixes))):
                pool.sem_inc(sem, CREDIT)
            delta_rule()
            add_up(by["wo"], 0)
            low_of_norm(0)
            low_of_hidden(0)
            add_up(by["down0"], 1)
            low_of_norm(1)
            low_of_ssd()
            add_up(by["so"], 2)
            low_of_norm(2)
            low_of_hidden(1)
            add_up(by["down1"], 3)


def kernel(**inputs):
    import numpy as np
    import concourse.bacc as bacc
    from concourse.bass_utils import run_bass_kernel_spmd as run

    a = {name: np.asarray(v) for name, v in inputs.items()}

    def slabs(w, per=1, width=P):
        rows, cols = w.shape
        tiles = rows // P // per
        v = w.reshape(per, tiles, P, cols // width, width)
        return np.ascontiguousarray(v.transpose(3, 0, 2, 1, 4)).reshape(-1, P, tiles * width)

    def cols(v):
        return v.reshape(-1, P).T

    def interleaved(w):
        half = w.shape[1] // 2 // P
        return w.reshape(D, 2, half, P).transpose(0, 2, 1, 3).reshape(D, -1)

    basic, chunk, ssd_mask, sel, sel_t = shape_constants()
    pad = np.zeros(P - HEADS, np.float32)
    lora2 = np.zeros((KT, P, 4, P), np.float32)
    lora2[:, :LORA, 0] = a["rwkv_w2"].reshape(LORA, KT, P).transpose(1, 0, 2)
    lora2[:, :LORA, 1] = a["rwkv_a2"].reshape(LORA, KT, P).transpose(1, 0, 2)
    lora2[:, :, 2:] = a["rwkv_g2"].reshape(2, P, KT, P).transpose(2, 1, 0, 3)
    params = np.concatenate([
        cols(a["rwkv_mu"]), cols(a["rwkv_w0"]), cols(a["rwkv_a0"]), cols(a["rwkv_k_k"]), cols(a["rwkv_k_a"]),
        cols(a["rwkv_r_k"]), cols(a["rwkv_ln_g"]), cols(a["rwkv_ln_b"]), cols(a["ssd_conv_w"]), cols(a["ssd_conv_b"]),
        cols(a["ssd_norm_g"]), cols(np.repeat(a["ssd_d"], 64)), cols(a["ln_g"]), cols(a["ln_b"]),
        cols(np.concatenate([a["ssd_dt_bias"], pad])), cols(np.concatenate([a["ssd_a_log"], pad]))], axis=1)
    w_ssd = a["ssd_w_in"]
    n_inner = NX * P
    arrays = {
        "x_cm": a["x"][0].T.reshape(KT, P, T).transpose(1, 0, 2),
        "params": params, "basic": basic, "pair_mask": chunk[:, :2 * P],
        "first_mask": chunk[:, 2 * P:3 * P], "level_mask": chunk[:, 3 * P:].reshape(P, -1, P),
        "sel": sel, "sel_t": sel_t,
        "ssd_mask": ssd_mask, "lora2": lora2,
        "w_r": slabs(a["rwkv_w_in"][0]), "w_k": slabs(a["rwkv_w_in"][1]), "w_v": slabs(a["rwkv_w_in"][2]),
        "w_w1": slabs(a["rwkv_w1"], width=LORA), "w_a1": slabs(a["rwkv_a1"], width=LORA), "w_g1": slabs(a["rwkv_g1"]),
        "w_ro": slabs(a["rwkv_w_out"]),
        "w_z": slabs(w_ssd[:, :n_inner]), "w_x": slabs(w_ssd[:, n_inner:2 * n_inner]),
        "w_bc": slabs(w_ssd[:, 2 * n_inner:-HEADS]), "w_dt": slabs(w_ssd[:, -HEADS:], width=HEADS),
        "w_so": slabs(a["ssd_w_out"], per=2),
    }
    for layer in range(DEPTH):
        arrays[f"w_up{layer}"] = slabs(interleaved(a["ffn_w_in"][layer]))
        arrays[f"w_down{layer}"] = slabs(a["ffn_w_out"][layer], per=4)
    arrays = {name: np.ascontiguousarray(v) for name, v in arrays.items()}

    nc = bacc.Bacc("TRN2", target_bir_lowering=False, num_devices=1)
    inp = {name: nc.dram_tensor(name, v.shape, F32, kind="ExternalInput").ap() for name, v in arrays.items()}
    out = nc.dram_tensor("out", (P, KT, T), F32, kind="ExternalOutput").ap()
    build(nc, inp, out)
    r = run(nc, [arrays], core_ids=[0])
    return r.results[0]["out"].transpose(1, 0, 2).reshape(D, T).T.reshape(1, T, D)
```

```python
import math
from contextlib import ExitStack

import concourse.bass as bass
from concourse import mybir

F32 = mybir.dt.float32
F32R = mybir.dt.float32r
ALU = mybir.AluOpType
ACT = mybir.ActivationFunctionType

P = 128
T = 256
D = 2048
KT = D // P
DEPTH = 2
ALPHA = (2 * DEPTH) ** 0.25
LN_EPS = 1e-5
GN_EPS = 64e-5
RMS_EPS = 1e-5
DECAY = math.exp(-0.5)
LORA = 96
NF = 44
NX = 32
HEADS = 64
GROUPS = 8
PAIRS = KT // 2
RAW, SPLIT = 4, 2

PARAM_TILES = [("mu", 6 * KT), ("w0", KT), ("a0", KT), ("k_k", KT), ("k_a", KT), ("r_k", KT), ("gn_g", KT),
               ("gn_b", KT), ("conv_w", 4 * 48), ("conv_b", 48), ("norm_g", NX), ("d_skip", NX), ("ln_g", 4 * KT),
               ("ln_b", 4 * KT), ("dt_bias", 1), ("a_log", 1)]
PARAM_AT = {}
NPARAM = 0
for _name, _n in PARAM_TILES:
    PARAM_AT[_name] = NPARAM
    NPARAM += _n

N_BASIC, N_SSD = 3 * P, 3 * P
CREDIT = 1
LEVELS = (2, 4, 8, 16, 32, 64)


def shape_constants():
    import numpy as np
    row, col = np.arange(P)[:, None], np.arange(P)[None, :]
    level = lambda m: ((row // m) % 2 == 1) & (col // m == row // m - 1)
    basic = [row == col, row // 64 == col // 64, row >= 0 * col]
    chunk = [row < col, row <= col, level(1).T] + [level(m) for m in LEVELS]
    ssd = [row <= col, row >= 0 * col, row <= col]
    wide = lambda parts: np.concatenate([np.broadcast_to(m, (P, P)).astype(np.float32) for m in parts], axis=1)
    sel = np.concatenate([np.arange(4)[None, :] == 2 * g + row // 64 for g in range(2)], axis=1).astype(np.float32)
    sel_t = np.concatenate([sel[:, 4 * g:4 * g + 4].T for g in range(2)], axis=1)
    return wide(basic), wide(chunk), wide(ssd), sel, sel_t


class Phase:

    def __init__(self, name, src, outs, per, tiles, width, unroll):
        self.name, self.src, self.outs, self.per, self.tiles, self.width, self.unroll = (
            name, src, outs, per, tiles, width, unroll)
        self.slabs = outs * per
        self.cols = tiles * width
        self.halves = ((0, (tiles + 1) // 2 * width), ((tiles + 1) // 2 * width, self.cols))
        self.slab0 = self.out0 = 0


def nothing(*_):
    pass


def loop(eng, n, body):
    if n == 1:
        body(0)
    elif n > 1:
        with eng.Fori(0, n) as k:
            body(k)


def beyond(m, n):
    return not isinstance(m, int) or m >= n


def pair_turns(eng, turn):
    turn(0, 0, False, True)

    def body(q):
        turn(2 * q + 1, 1, True, True)
        turn(2 * q + 2, 0, True, True)

    loop(eng, PAIRS // 2 - 1, body)
    turn(PAIRS - 1, 1, True, False)


def group_turns(eng, turn):
    turn(0, False, True)
    with eng.Fori(1, GROUPS - 1) as k:
        turn(k, True, True)
    turn(GROUPS - 1, True, False)


def build(nc, inp, out, debug=None):
    ctx = ExitStack()
    with ctx:
        sems = {}

        def S(name):
            if name not in sems:
                sems[name] = ctx.enter_context(nc.semaphore(name))
            return sems[name]

        KB = 1024
        at = [16512]

        def place(nbytes):
            here = at[0]
            at[0] += nbytes
            return here

        def sb(name, shape, dt, offset):
            return nc.alloc_sbuf_tensor_at(name, shape, dt, offset=offset)

        basic = sb("basic", [P, N_BASIC], F32, place(4 * N_BASIC))
        par = sb("par", [P, NPARAM, 1], F32, place((4 * NPARAM + 31) // 32 * 32))
        omm = sb("omm", [P, 6 * KT, 1], F32, place(4 * 6 * KT))
        omka = sb("omka", [P, KT, 1], F32, place(4 * KT))
        eps = sb("eps", [P, 4, 1], F32, place(32))
        raw = sb("raw", [P, RAW, D], F32, place(RAW * 8 * KB))
        wsp_at = place(SPLIT * 16 * KB)
        wsp = sb("wsp", [P, SPLIT, 2, D], F32R, wsp_at)
        H = sb("H", [P, KT, T], F32, place(16 * KB))
        xs_at = place(32 * KB)
        big_at = place(88 * KB)
        tmp_at = place(3 * KB)
        assert at[0] <= 229344, at
        XS = sb("XS", [P, 2, KT, T], F32R, xs_at)
        tmp = sb("tmp", [P, 3, T], F32, tmp_at)
        LSQ = sb("LSQ", [P, KT, T], F32, xs_at + 16 * KB)
        ident, bones, ones = (basic[:, i * P:(i + 1) * P] for i in range(3))

        def param(name, i):
            return par[:, PARAM_AT[name] + i, :]

        R = sb("R", [P, KT, T], F32, big_at)
        K = sb("K", [P, KT, T], F32, big_at + 16 * KB)
        V = sb("V", [P, KT, T], F32, big_at + 32 * KB)
        XS2 = sb("XS2", [P, 2, KT, T], F32R, big_at + 48 * KB)
        XS3 = sb("XS3", [P, 2, KT, T], F32R, big_at + 16 * KB)
        lo_w = sb("lo_w", [P, T], F32, big_at + 80 * KB)
        lo_a = sb("lo_a", [P, T], F32, big_at + 81 * KB)
        lo_g = sb("lo_g", [P, 2, T], F32, big_at + 82 * KB)
        mixb = sb("mixb", [P, 4, T], F32, big_at + 84 * KB)
        YR = sb("YR", [P, 2, KT, T], F32R, big_at)

        ct = [big_at + 48 * KB]

        def core(name, shape, dt=F32):
            n = 4
            for s in shape[1:]:
                n *= s
            here = ct[0]
            ct[0] += (n + 31) // 32 * 32
            return sb(name, shape, dt, here)

        LM1 = [core(f"LM1_{g}", [P, 4, 2 * P]) for g in range(2)]
        LM2 = [core(f"LM2_{g}", [P, 4, 2 * P]) for g in range(2)]
        XI = [core(f"XI_{g}", [P, 4, P]) for g in range(2)]
        TI = [core(f"TI_{g}", [P, 4, P]) for g in range(2)]
        UI = [core(f"UI_{g}", [P, 4, P]) for g in range(2)]
        S0 = [sb(f"S0_{g}", [P, 64], F32, tmp_at + 256 * (g + 1)) for g in range(2)]
        assert ct[0] <= big_at + 76 * KB, ct
        ct = [big_at + 84 * KB]
        RH = [core(f"RH_{g}", [P, 4, 64]) for g in range(2)]
        SA = [core(f"SA_{g}", [P, 4, 64]) for g in range(2)]
        assert ct[0] <= big_at + 88 * KB
        ct = [xs_at]
        LW = [core(f"LW_{g}", [P, 4, P]) for g in range(2)]
        SG, AA, SC, EE, EI, KK, VS, BT, KW, SQ = ([] for _ in range(10))
        for g in range(2):
            SG.append(core(f"SG_{g}", [P, 2, P]))
            AA.append(core(f"AA_{g}", [P, T]))
            SC.append(core(f"SC_{g}", [P, 2, P + 1]))
            EE.append(core(f"EE_{g}", [P, 2, P + 1]))
            EI.append(core(f"EI_{g}", [P, 2, P + 1]))
            KK.append(core(f"KK_{g}", [P, 2, P]))
            VS.append(core(f"VS_{g}", [P, T]))
            BT.append(core(f"BT_{g}", [P, 2, P]))
            KW.append(core(f"KW_{g}", [P, 2, P]))
            SQ.append(core(f"SQ_{g}", [P, 2, P]))
        AR, TOK, BV, GG = [[], []], [[], []], [[], []], [[], []]
        AR[0] = [core(f"AR_0{g}", [P, 2, 2, P]) for g in range(2)]
        GG[0] = [core(f"GG_0{g}", [P, T]) for g in range(2)]
        assert ct[0] <= xs_at + 32 * KB, ct
        ct = [wsp_at]
        AR[1] = [core(f"AR_1{g}", [P, 2, 2, P]) for g in range(2)]
        for side in range(2):
            TOK[side] = [core(f"TOK_{side}{g}", [P, 4, P]) for g in range(2)]
        assert ct[0] <= wsp_at + 16 * KB, ct
        ct = [wsp_at + 16 * KB]
        GG[1] = [core(f"GG_1{g}", [P, T]) for g in range(2)]
        for side in range(2):
            BV[side] = [core(f"BV_{side}{g}", [P, T]) for g in range(2)]
        YY = [core(f"YY_{g}", [P, T]) for g in range(2)]
        YC = [core(f"YC_{g}", [P, T]) for g in range(2)]
        SY = [core(f"SY_{g}", [P, T]) for g in range(2)]
        NR = core("NR", [4, T])
        YV = core("YV", [4, T])
        assert ct[0] <= wsp_at + 32 * KB, ct
        level_mask = sb("level_mask", [P, len(LEVELS), P], F32, big_at + 76 * KB)
        pair_mask = sb("pair_mask", [P, 2 * P], F32, tmp_at + KB)
        first_mask = sb("first_mask", [P, P], F32, tmp_at + 2 * KB)
        sel = sb("sel", [P, 8], F32, tmp_at + 3 * KB // 4)
        sel_t = sb("sel_t", [4, 2 * P], F32, big_at + 79 * KB)
        kb = sb("kb", [P, 2, 2, 2], F32, tmp_at)
        dsc = sb("dsc", [P, 4, 1], F32, tmp_at + 64)

        HID = sb("HID", [P, 2, NF, T], F32R, big_at)

        XC = sb("XC", [P, NX, T], F32, big_at)
        Z = sb("Z", [P, NX, T], F32, big_at + 32 * KB)
        BC = sb("BC", [P, 2 * GROUPS, T], F32, big_at + 64 * KB)
        YS = sb("YS", [P, 2, NX, T], F32R, big_at)
        dtt = sb("dtt", [P, 2, HEADS, 1], F32, big_at + 80 * KB)
        ncs = sb("ncs", [P, 2, HEADS, 1], F32, big_at + 80 * KB + 512)
        dtc = sb("dtc", [HEADS, T], F32, big_at + 81 * KB)
        cs = sb("cs", [HEADS, T], F32, big_at + 82 * KB)
        dta = sb("dta", [HEADS, T], F32, big_at + 83 * KB)
        dtb = sb("dtb", [HEADS, T], F32, big_at + 84 * KB)
        aneg = sb("aneg", [HEADS, 2], F32, big_at + 85 * KB)
        pcs = sb("pcs", [P, 2, HEADS, 1], F32, big_at + 85 * KB + 32)
        smask = sb("smask", [P, N_SSD], F32, big_at + 86 * KB)
        ct = [xs_at]
        CSB = core("CSB", [P, 8, T])
        XST = core("XST", [P, 4, T])
        BST = core("BST", [P, T])
        CBM = core("CBM", [P, 3 * P])
        XDT = core("XDT", [P, 2, 8, 64])
        GE = [core(f"GE_{i}", [P, 3 * P]) for i in range(4)]
        YN = core("YN", [P, 4, T])
        SQS = [core(f"SQS_{i}", [P, T]) for i in range(2)]
        RST = core("RST", [P, T])
        assert ct[0] <= xs_at + 32 * KB, (ct, xs_at)
        cs_dram = nc.dram_tensor("cs_scratch", (HEADS, T), F32, kind="Internal").ap()

        bank = [nc.alloc_psum_tensor(f"bank{i}", [P, 512], F32) for i in range(8)]
        phases = [
            Phase("r", inp["w_r"], 16, 1, 16, P, 4),
            Phase("w1", inp["w_w1"], 1, 1, 16, LORA, 4),
            Phase("k", inp["w_k"], 16, 1, 16, P, 4),
            Phase("v", inp["w_v"], 16, 1, 16, P, 4),
            Phase("a1", inp["w_a1"], 1, 1, 16, LORA, 4),
            Phase("g1", inp["w_g1"], 2, 1, 16, P, 4),
            Phase("wo", inp["w_ro"], 16, 1, 16, P, 4),
            Phase("up0", inp["w_up0"], 88, 1, 16, P, 4),
            Phase("down0", inp["w_down0"], 16, 4, 11, P, 2),
            Phase("x", inp["w_x"], NX, 1, 16, P, 4),
            Phase("bc", inp["w_bc"], 2 * GROUPS, 1, 16, P, 4),
            Phase("dt", inp["w_dt"], 1, 1, 16, HEADS, 4),
            Phase("z", inp["w_z"], 32, 1, 16, P, 4),
            Phase("so", inp["w_so"], 16, 2, 16, P, 4),
            Phase("up1", inp["w_up1"], 88, 1, 16, P, 4),
            Phase("down1", inp["w_down1"], 16, 4, 11, P, 2),
        ]
        by = {}
        s = o = 0
        for ph in phases:
            ph.slab0, ph.out0 = s, o
            s, o = s + ph.slabs, o + ph.outs
            by[ph.name] = ph
        n_slabs = s
        owner = [ph for ph in phases for _ in range(ph.slabs)]

        landed = [S(f"slab_landed{i}") for i in range(RAW)]
        high_ready, low_ready, slab_done = S("high_ready"), S("low_ready"), S("slab_done")
        bank_free = [S("bank0_free"), S("bank1_free")]

        def run_phase(eng, ph, prepare, take, before=None, after=None, peel=0, until=None):
            turn = ph.unroll * ph.per
            n = max(0, (ph.slabs - 2) // turn)

            def step(j, k, u, slab):
                if before:
                    before(ph, j, k, u)
                for q in range(ph.per):
                    if q == ph.per - 1:
                        take(ph, j, k, u)
                    slab(ph.slab0 + j * ph.per + q + 2, k)
                if after:
                    after(ph, j, k, u)

            def straight(s, k):
                if s < (until or n_slabs):
                    prepare(owner[s], s, 0, 0)

            def body(k):
                for i in range(ph.unroll):
                    step(peel * ph.unroll + i, k, ph.unroll, lambda s, k: prepare(ph, s, k, turn))

            for j in range(peel * ph.unroll):
                step(j, 0, 0, straight)
            loop(eng, n - peel, body)
            for j in range(n * ph.unroll, ph.outs):
                step(j, 0, 0, straight)

        def lands(s, k, turn):
            return landed[s % RAW], 16 * (s // RAW + 1) + k * (16 * turn // RAW)

        def out_wait(eng, ph, j, k, u):
            eng.wait_ge(slab_done, ph.slab0 + (j + 1) * ph.per + k * (u * ph.per))

        def out_bank(ph, j):
            return bank[(ph.out0 + j) % 2][:ph.width, 0:T]

        def free_sem(ph, j):
            return bank_free[(ph.out0 + j) % 2]

        def freed(ph, j, k, u):
            return (ph.out0 + j) // 2 + 1 + k * (u // 2) + CREDIT

        def shifted(i, k, j):
            return S("ln_odd" if j % 2 else "ln_even"), KT // 2 * i + 2 * k + j // 2 + 1

        def normed_split(i):
            def ready(n):
                if n % 4 == 3:
                    return S("ln_low_fourth"), KT // 4 * i + n // 4 + 1
                return S("ln_low"), KT // 4 * 3 * i + n // 4 * 3 + n % 4 + 1
            return ready

        def counted(name, base=0):
            return lambda n: (S(name), base + n + 1)

        block = ctx.enter_context(nc.Block())

        MU = {"r": 0, "w1": 1, "k": 2, "v": 3, "a1": 4, "g1": 5}
        HIDDEN = ("k", "w1", "v", "a1")
        MIXED = {"r": XS, "w1": XS3, "k": XS2, "v": XS, "a1": XS2, "g1": XS}

        @block.sync
        def _(sp):
            def load(ph, s, k, turn):
                if s >= RAW:
                    sp.wait_ge(low_ready, 2 * (s - RAW + 1) + k * (2 * turn))
                sem, _n = lands(s, k, turn)
                sp.dma_start(raw[:, s % RAW, 0:ph.cols], ph.src[s - ph.slab0 + k * turn]).then_inc(sem, 16)

            sp.dma_start(H[:, :, :], inp["x_cm"]).then_inc(S("x_landed"), 16)
            sp.dma_start(par[:, :, 0], inp["params"]).then_inc(S("par_landed"), 16)
            for s in range(RAW):
                load(owner[s], s, 0, 0)
            sp.dma_start(basic[:, :], inp["basic"]).then_inc(S("basic_landed"), 16)
            for ph in phases:
                first = ph.slab0 if ph.slab0 else RAW
                n = (ph.slab0 + ph.slabs - first) // 4

                def body(k):
                    for j in range(4):
                        load(ph, first + j, k, 4)

                loop(sp, n, body)
                for s in range(first + 4 * n, ph.slab0 + ph.slabs):
                    load(ph, s, 0, 0)
            for n in range(KT):
                sp.wait_ge(*shifted(3, n // 4, n % 4))
                sp.dma_start(out[:, n, :], H[:, n, :]).then_inc(S("out_stored"), 16)
            sp.wait_ge(S("out_stored"), 16 * KT)

        @block.scalar
        def _(act):
            def apart():
                act.wait_ge(S("par_landed"), 16)

            def prepare(ph, s, k, turn):
                act.wait_ge(*lands(s, k, turn))
                if s >= 2:
                    act.wait_ge(slab_done, s - 1 + k * turn)
                for a, b in ph.halves:
                    act.activation(wsp[:, s % 2, 0, a:b], raw[:, s % RAW, a:b], ACT.Copy).then_inc(high_ready, 1)

            def mix_high(name, n, mixed):
                act.wait_ge(S("mixed_" + name), n + 1)
                apart()
                act.activation(MIXED[name][:, 0, n, :], mixed, ACT.Copy).then_inc(S("mix_high_" + name), 1)

            def mix_all(name, between=nothing):
                mu = KT * MU[name]

                def four(k, first=False):
                    for j in range(4):
                        n = 4 * k + j
                        if not first:
                            act.wait_ge(S("mix_low_" + name), n - 3)
                        apart()
                        act.activation(mixb[:, j, :], H[:, n, :], ACT.Copy, scale=omm[:, mu + n, :]).then_inc(
                            S("mix_begun_" + name), 1)
                        if not (first and j == 0):
                            mix_high(name, n - 1, mixb[:, (j - 1) % 4, :])

                four(0, first=True)
                between()
                with act.Fori(1, KT // 4) as k:
                    four(k)
                mix_high(name, KT - 1, mixb[:, 3, :])

            def mixing(names):
                def after(ph, j, k, u):
                    for i, name in enumerate(names):
                        mix_high(name, j + k * u, tmp[:, i, :])
                return after

            def take_copy(dst, func=ACT.Copy):
                def take(ph, j, k, u):
                    out_wait(act, ph, j, k, u)
                    apart()
                    act.activation(dst(j + k * u), out_bank(ph, j), func).then_inc(free_sem(ph, j), 1)
                return take

            def take_up(ph, j, k, u):
                if j % 2 == 0:
                    out_wait(act, ph, j, k, u)
                    act.wait_ge(free_sem(ph, 1), (ph.out0 + 1) // 2 + j // 2 + k * (u // 2) + CREDIT)
                    act.activation(tmp[:, 0, :], out_bank(ph, j), ACT.Silu).then_inc(free_sem(ph, j), 1)

            def high_of_hidden(ph, j, k, u):
                if j % 2:
                    n = j // 2 + k * (u // 2)
                    act.wait_ge(free_sem(ph, 1), (ph.out0 + 1) // 2 + n + 1 + CREDIT)
                    apart()
                    act.activation(HID[:, 0, n, :], tmp[:, 1 + (j // 2) % 2, :], ACT.Copy).then_inc(S("hid_high"), 1)

            def layer_norm(i):
                def squares(k):
                    for j in range(4):
                        act.wait_ge(S("ln_centred"), KT * i + 4 * k + j + 1)
                        apart()
                        act.activation(LSQ[:, 4 * k + j, :], H[:, 4 * k + j, :], ACT.Square).then_inc(S("ln_sq"), 1)

                loop(act, KT // 4, squares)
                act.wait_ge(S("ln_sqsum"), KT * (i + 1))
                act.activation(tmp[:, 0, :], bank[3][:, 0:T], ACT.Sqrt, scale=1.0 / D,
                               bias=eps[:, 0, :]).then_inc(S("ln_std"), 1)

                def finish(k):
                    for j in (0, 2):
                        n = 4 * k + j
                        act.wait_ge(S("ln_scaled"), KT * i + n + 1)
                        apart()
                        act.activation(H[:, n, :], H[:, n, :], ACT.Identity, scale=param("ln_g", KT * i + n),
                                       bias=param("ln_b", KT * i + n)).then_inc(S("ln_even"), 1)
                    for j in (0, 1, 2, 3):
                        if i < 3:
                            act.wait_ge(*shifted(i, k, j))
                            apart()
                            act.activation(XS[:, 0, 4 * k + j, :], H[:, 4 * k + j, :], ACT.Copy).then_inc(S("ln_high"), 1)

                loop(act, KT // 4, finish)

            def take_conv(tile0, dst):
                def silu(ph, j, k, u):
                    act.wait_ge(free_sem(ph, j), freed(ph, j, k, u))
                    apart()
                    act.activation(dst(j + k * u), tmp[:, j % 2, :], ACT.Silu).then_inc(S("conv_done"), 1)

                def take(ph, j, k, u):
                    n = j + k * u
                    if j:
                        silu(ph, j - 1, k, u)
                    if tile0 + j >= 2:
                        act.wait_ge(S("conv_done"), tile0 + n - 1)
                    out_wait(act, ph, j, k, u)
                    apart()
                    act.activation(tmp[:, j % 2, :], out_bank(ph, j), ACT.Identity, scale=param("conv_w", 3 * 48 + tile0 + n),
                                   bias=param("conv_b", tile0 + n)).then_inc(S("conv_begun"), 1)

                def after(ph, j, k, u):
                    if j == ph.outs - 1:
                        silu(ph, j, k, u)
                return take, after

            def take_dt(ph, j, k, u):
                out_wait(act, ph, j, k, u)
                act.activation(dta[:, :], out_bank(ph, j), ACT.Abs,
                               bias=par[0:HEADS, PARAM_AT["dt_bias"], :]).then_inc(S("dt_abs"), 1)
                act.activation(aneg[:, 0:1], par[0:HEADS, PARAM_AT["a_log"], :], ACT.Exp).then_inc(S("dt_rate"), 1)
                act.wait_ge(S("dt_abs"), 1)
                act.activation(dtb[:, :], dta[:, :], ACT.Exp, scale=-1.0).then_inc(S("dt_exp"), 1)
                act.wait_ge(S("dt_exp"), 1)
                act.activation(dtb[:, :], dtb[:, :], ACT.Ln, bias=eps[0:HEADS, 3, :]).then_inc(S("dt_ln"), 1)

            def take_z(ph, j, k, u):
                out_wait(act, ph, j, k, u)
                apart()
                act.activation(Z[:, j + k * u, :], out_bank(ph, j), ACT.Silu).then_inc(free_sem(ph, j), 1)
                if j == ph.outs - 4:
                    act.wait_ge(S("cs_ready"), 1)
                    act.dma_start(cs_dram, cs[:, :]).then_inc(S("cs_stored"), 16)

            def delta_rule():
                act.wait_ge(slab_done, by["wo"].slab0)
                act.wait_ge(S("mix_low_g1"), KT)
                act.dma_start(level_mask[:, :, :], inp["level_mask"]).then_inc(S("mask_landed"), 16)
                act.dma_start(pair_mask[:, :], inp["pair_mask"]).then_inc(S("mask_landed"), 16)
                act.dma_start(first_mask[:, :], inp["first_mask"]).then_inc(S("mask_landed"), 16)
                act.dma_start(sel[:, :], inp["sel"]).then_inc(S("mask_landed"), 16)
                act.dma_start(sel_t[:, :], inp["sel_t"]).then_inc(S("mask_landed"), 16)

                def flat(x):
                    return x[:, :, :].rearrange("p a b -> p (a b)")

                def keys(m):
                    for g in range(2):
                        if beyond(m, 1):
                            act.wait_ge(S("bonus_ready"), 2 * m)
                        act.dma_start(LW[g][:, :, :], inp["lora2"][2 * m + g]).then_inc(S(f"lora_landed{g}"), 16)
                        act.dma_start(VS[g][:, :], V[:, 2 * m + g, :]).then_inc(S(f"v_landed{g}"), 16)
                    for g in range(2):
                        if beyond(m, 1):
                            act.wait_ge(S("bonus_mm"), 2 * m)
                        apart()
                        act.activation(flat(SQ[g]), K[:, 2 * m + g, :], ACT.Square,
                                       scale=param("k_k", 2 * m + g)).then_inc(S("key_sq"), 1)

                def norms(m):
                    act.wait_ge(S("norm_mm"), m + 1)
                    act.activation(NR[:, :], bank[3][0:4, 0:T], ACT.Sqrt).then_inc(S("norm_ready"), 1)

                def gates(m):
                    for g in range(2):
                        act.wait_ge(S("lora_mm"), 2 * m + g + 1)
                        apart()
                        act.activation(flat(SG[g]), bank[4 * g + 3][:, 0:T], ACT.Sigmoid,
                                       bias=param("w0", 2 * m + g)).then_inc(S("decay_gate"), 1)
                        apart()
                        act.activation(AA[g][:, :], bank[4 * g + 3][:, T:2 * T], ACT.Sigmoid,
                                       bias=param("a0", 2 * m + g)).then_inc(S("rate_gate"), 1)

                def decays(m, g):
                    act.wait_ge(S("mid_ready"), 4 * m + 2 * g + 2)
                    if beyond(m, 1):
                        act.wait_ge(S("a_tilde"), 2 * m)
                        act.wait_ge(S("r_tilde"), 2 * m)
                    for c in range(2):
                        act.activation(EE[g][:, c, :], SC[g][:, c, :], ACT.Exp, scale=-DECAY,
                                       bias=kb[:, g, 0, c:c + 1]).then_inc(S("decayed"), 1)
                        act.activation(EI[g][:, c, :], SC[g][:, c, :], ACT.Exp, scale=DECAY,
                                       bias=kb[:, g, 1, c:c + 1]).then_inc(S("decayed"), 1)

                def output_gate(m, side):
                    for g in range(2):
                        act.wait_ge(S("gate_mm"), 2 * m + g + 1)
                        act.activation(GG[side][g][:, :], bank[4 * g + 3][:, 0:T], ACT.Copy).then_inc(S("gate_ready"), 1)

                def token_major(m, side):
                    for g in range(2):
                        act.wait_ge(S("turned"), 2 * m + g + 1)
                        act.activation(flat(TOK[side][g]), bank[4 * g + 3][:, :], ACT.Copy).then_inc(S("token_major"), 1)

                def inverse_begun(m):
                    for g in range(2):
                        act.wait_ge(S("t_mm"), 12 * m + g + 1)
                        act.activation(flat(TI[g]), bank[4 * g + 1][:, :], ACT.Copy).then_inc(S("t_copied"), 1)

                def output(k):
                    for g in range(2):
                        act.wait_ge(S("y_mm"), 4 * k + g + 3)
                        act.activation(YY[g][:, :], bank[4 * g + 1][:, 0:T], ACT.Copy).then_inc(S("y_ready"), 1)
                    for g in range(2):
                        act.wait_ge(S("y_centred"), 2 * k + g + 1)
                        act.activation(SY[g][:, :], YC[g][:, :], ACT.Square).then_inc(S("y_sq"), 1)
                    act.wait_ge(S("y_var_mm"), 2 * k + 2)
                    act.activation(YV[:, :], bank[0][0:4, 0:T], ACT.Sqrt, scale=1.0 / 64,
                                   bias=eps[0:4, 1, :]).then_inc(S("y_std"), 1)

                def output_high(k):
                    for g in range(2):
                        act.wait_ge(S("y_gated"), 2 * k + g + 1)
                        apart()
                        act.activation(YR[:, 0, 2 * k + g, :], YC[g][:, :], ACT.Copy).then_inc(S("y_high"), 1)

                def turn(k, side, post, pre):
                    if pre:
                        keys(k + 1)
                    for lev in range(len(LEVELS)):
                        if lev < len(LEVELS) - 1:
                            for g in range(2):
                                act.wait_ge(S("t_mm"), 12 * k + 2 * lev + g + 3)
                                act.activation(flat(TI[g]), bank[4 * g + 2][:, :], ACT.Copy).then_inc(S("t_copied"), 1)
                        if lev == 3 and post:
                            output_high(k - 1)
                        if pre:
                            if lev == 0:
                                norms(k + 1)
                            elif lev == 1:
                                gates(k + 1)
                            elif lev == 2:
                                decays(k + 1, 0)
                            elif lev == 3:
                                decays(k + 1, 1)
                                output_gate(k + 1, 1 - side)
                            elif lev == 4:
                                token_major(k + 1, 1 - side)
                    for c in range(2):
                        for g in range(2):
                            act.wait_ge(S("rhs_mm"), 4 * k + 2 * c + g + 1)
                            if c == 0:
                                act.activation(RH[g][:, 0:2, :], bank[4 * g + 3][:, 0:P].rearrange(
                                    "p (a b) -> p a b", a=2), ACT.Copy).then_inc(S("rhs_ready"), 1)
                            else:
                                for h in range(2):
                                    act.activation(RH[g][:, 2 + h, :], bank[4 * g + 3 - h][:, P + 64 * h:P + 64 * h + 64],
                                                   ACT.Copy).then_inc(S("rhs_ready"), 1)
                        for g in range(2):
                            act.wait_ge(S("sa_mm"), 4 * k + 2 * c + g + 1)
                            act.activation(SA[g][:, 2 * c:2 * c + 2, :], bank[4 * g][:, 128 * c:128 * c + 128].rearrange(
                                "p (a b) -> p a b", a=2), ACT.Copy).then_inc(S("sa_ready"), 1)
                    output(k)
                    if pre:
                        inverse_begun(k + 1)

                keys(0)
                norms(0)
                gates(0)
                decays(0, 0)
                decays(0, 1)
                output_gate(0, 0)
                token_major(0, 0)
                inverse_begun(0)
                pair_turns(act, turn)
                output_high(PAIRS - 1)

            def ssd():
                act.wait_ge(slab_done, by["so"].slab0)
                act.wait_ge(S("cs_stored"), 16)

                def load_sums(k, half):
                    act.dma_start(CSB[:, 4 * half:4 * half + 4, :], cs_dram.rearrange("(g h) t -> g h t", h=4)[2 * k + half]
                                  .partition_broadcast(P)).then_inc(S(f"csb_landed{half}"), 16)

                def load_group(k):
                    act.dma_start(BST[:, :], BC[:, k, :]).then_inc(S("bst_landed"), 16)
                    groups = XC[:, :, :].rearrange("p (g a) t -> p g (a t)", g=GROUPS)
                    act.dma_start(XST[:, :, :].rearrange("p a b -> p (a b)"), groups[:, k, :]).then_inc(
                        S("xst_landed"), 16)

                def square(k, t, first=False):
                    n = 4 * k + t
                    if not first:
                        act.wait_ge(S("ys_sq_mm"), n - 1)
                    act.wait_ge(S("ys_gated"), n + 1)
                    apart()
                    act.activation(SQS[t % 2][:, :], Z[:, n, :], ACT.Square).then_inc(S("ys_sq"), 1)

                def deviations(k):
                    act.wait_ge(S("ys_sq_mm"), 4 * k + 4)
                    act.activation(RST[:, :], bank[7][:, 0:T], ACT.Sqrt, scale=1.0 / 512,
                                   bias=eps[:, 2, :]).then_inc(S("ys_std"), 1)

                def high(k):
                    for t in range(4):
                        act.wait_ge(S("ys_normed"), 4 * k + t + 1)
                        apart()
                        act.activation(YS[:, 0, 4 * k + t, :], YN[:, t, :], ACT.Copy).then_inc(S("ys_high"), 1)

                def turn(k, post, more):
                    for h in range(8):
                        if h % 2 == 0:
                            o = h + 1
                            act.wait_ge(S(f"csb_landed{o // 4}"), 16 * k + 16)
                            if post or o >= 4:
                                act.wait_ge(S("ssd_y_mm"), 8 * k + o - 3)
                            apart()
                            act.activation(GE[o % 4][:, 0:T], CSB[:, o, :], ACT.Relu, scale=-1.0,
                                           bias=pcs[:, 0, 8 * k + o, :]).then_inc(S("seg_odd"), 1)
                            apart()
                            act.activation(GE[o % 4][:, T:T + P], CSB[:, o, P:T], ACT.Relu, scale=-1.0,
                                           bias=pcs[:, 1, 8 * k + o, :]).then_inc(S("seg_odd"), 1)
                            act.wait_ge(S("seg_even"), 8 * k + h + 2)
                        else:
                            act.wait_ge(S("seg_odd"), 8 * k + h + 1)
                        act.activation(GE[h % 4][:, :], GE[h % 4][:, :], ACT.Exp,
                                       scale=-1.0 if h % 2 else 1.0).then_inc(S("ge_ready"), 1)
                        if more and h == 0:
                            act.wait_ge(S("cb_mm"), k + 1)
                            act.wait_ge(S("x_turned"), 2 * k + 2)
                            load_group(k + 1)
                        if post and h in (1, 2):
                            square(k - 1, h + 1)
                        if post and h == 3:
                            deviations(k - 1)
                        if more and h == 4:
                            act.wait_ge(S("ge_ready"), 8 * k + 4)
                            load_sums(k + 1, 0)
                        if h == 5:
                            square(k, 0, first=not post)
                        if h == 7:
                            square(k, 1, first=not post)
                    if more:
                        act.wait_ge(S("ge_ready"), 8 * k + 8)
                        load_sums(k + 1, 1)
                    if post:
                        high(k - 1)

                load_group(0)
                load_sums(0, 0)
                load_sums(0, 1)
                act.wait_ge(S("dt_turned"), 1)
                act.activation(dtt[:, :, :, 0], bank[2][:, 0:2 * HEADS].rearrange("p (c h) -> p c h", c=2),
                               ACT.Copy).then_inc(S("dt_tokens"), 1)
                act.activation(ncs[:, :, :, 0], bank[2][:, 2 * HEADS:4 * HEADS].rearrange("p (c h) -> p c h", c=2),
                               ACT.Copy, scale=-1.0).then_inc(S("dt_tokens"), 1)
                act.activation(pcs[:, :, :, 0], bank[2][:, 2 * HEADS:4 * HEADS].rearrange("p (c h) -> p c h", c=2),
                               ACT.Copy).then_inc(S("dt_tokens"), 1)
                act.wait_ge(S("dt_tokens"), 3)
                group_turns(act, turn)
                square(GROUPS - 1, 2)
                square(GROUPS - 1, 3)
                deviations(GROUPS - 1)
                high(GROUPS - 1)

            act.wait_ge(S("par_landed"), 16)
            act.wait_ge(S("x_landed"), 16)
            act.wait_ge(S("one_minus"), 2)
            mix_all("r", between=lambda: prepare(by["r"], 0, 0, 0))
            prepare(by["r"], 1, 0, 0)
            run_phase(act, by["r"], prepare, take_copy(lambda n: R[:, n, :]), after=mixing(["k", "w1"]))
            run_phase(act, by["w1"], prepare, take_copy(lambda n: lo_w[0:LORA, :], ACT.Tanh))
            run_phase(act, by["k"], prepare, take_copy(lambda n: K[:, n, :]), after=mixing(["v"]))
            run_phase(act, by["v"], prepare, take_copy(lambda n: V[:, n, :]), after=mixing(["a1"]))
            mix_all("g1")
            run_phase(act, by["a1"], prepare, take_copy(lambda n: lo_a[0:LORA, :]))
            run_phase(act, by["g1"], prepare, take_copy(lambda n: lo_g[:, n, :], ACT.Sigmoid), until=by["wo"].slab0)
            delta_rule()
            for i in range(SPLIT):
                prepare(by["wo"], by["wo"].slab0 + i, 0, 0)
            run_phase(act, by["wo"], prepare, nothing)
            layer_norm(0)
            run_phase(act, by["up0"], prepare, take_up, after=high_of_hidden)
            run_phase(act, by["down0"], prepare, nothing)
            layer_norm(1)
            act.dma_start(smask[:, :], inp["ssd_mask"]).then_inc(S("smask_landed"), 16)
            take, after = take_conv(0, lambda n: XC[:, n, :])
            run_phase(act, by["x"], prepare, take, after=after, peel=1)
            take, after = take_conv(NX, lambda n: BC[:, n, :])
            run_phase(act, by["bc"], prepare, take, after=after, peel=1)
            run_phase(act, by["dt"], prepare, take_dt)
            run_phase(act, by["z"], prepare, take_z)
            ssd()
            run_phase(act, by["so"], prepare, nothing)
            layer_norm(2)
            run_phase(act, by["up1"], prepare, take_up, after=high_of_hidden)
            run_phase(act, by["down1"], prepare, nothing)
            layer_norm(3)

        @block.tensor
        def _(pe):
            def product(ph, acts, ready):
                turn = ph.unroll * ph.per

                def output(j, k, u, ready=None):
                    o = ph.out0 + j
                    pe.wait_ge(bank_free[o % 2], o // 2 + k * (u // 2) + CREDIT)
                    for q in range(ph.per):
                        s = ph.slab0 + j * ph.per + q
                        w = wsp[:, s % 2, :, 0:ph.cols].rearrange("p a (t c) -> p a t c", t=ph.tiles)
                        for t in range(ph.tiles):
                            i = q * ph.tiles + t
                            first, last = i == 0, i == ph.per * ph.tiles - 1
                            if t in (0, (ph.tiles + 1) // 2):
                                pe.wait_ge(low_ready, 2 * s + (1 if t == 0 else 2) + k * (2 * u * ph.per))
                            if ready:
                                pe.wait_ge(*ready(i))
                            pe.matmul(out_bank(ph, j), w[:, 0, t, :], acts[:, 0, i, :], start=first, stop=False)
                            pe.matmul(out_bank(ph, j), w[:, 0, t, :], acts[:, 1, i, :], start=False, stop=False)
                            mm = pe.matmul(out_bank(ph, j), w[:, 1, t, :], acts[:, 0, i, :], start=False, stop=last)
                        mm.then_inc(slab_done, 1)

                output(0, 0, 0, ready)
                u = 2
                n = (ph.outs - 1) // u

                def body(k):
                    for j in range(u):
                        output(1 + j, k, u)

                loop(pe, n, body)
                for j in range(1 + n * u, ph.outs):
                    output(j, 0, 0)

            def layer_norm(i):
                pe.wait_ge(S("ln_acc"), KT * (i + 1) + CREDIT)
                pe.matmul(bank[2][:, 0:T], ones, tmp[:, 0, :], start=True, stop=True).then_inc(S("ln_sum"), 1)
                for n in range(KT):
                    pe.wait_ge(S("ln_sq"), KT * i + n + 1)
                    pe.matmul(bank[3][:, 0:T], ones, LSQ[:, n, :], start=n == 0,
                              stop=n == KT - 1).then_inc(S("ln_sqsum"), 1)

            def flat(x):
                return x[:, :, :].rearrange("p a b -> p (a b)")

            def delta_rule():
                pe.wait_ge(bank_free[0], (by["wo"].out0 + 1) // 2 + CREDIT)
                pe.wait_ge(bank_free[1], by["wo"].out0 // 2 + CREDIT)
                pe.wait_ge(S("mask_landed"), 80)

                def rows(x, h):
                    return x[64 * h:64 * h + 64]

                def norm_sums(m):
                    for g in range(2):
                        pe.wait_ge(S("key_sq"), 2 * m + g + 1)
                        mm = pe.matmul(bank[3][0:4, 0:T], sel[:, 4 * g:4 * g + 4], flat(SQ[g]), start=g == 0, stop=g == 1)
                    mm.then_inc(S("norm_mm"), 1)

                def lora(m):
                    pe.wait_ge(S("norm_ready"), m + 1)
                    for g in range(2):
                        pe.wait_ge(S(f"lora_landed{g}"), 16 * m + 16)
                        pe.matmul(bank[4 * g + 3][:, 0:T], LW[g][0:LORA, 0, :], lo_w[0:LORA, :], start=True, stop=True)
                        pe.matmul(bank[4 * g + 3][:, T:2 * T], LW[g][0:LORA, 1, :], lo_a[0:LORA, :], start=True,
                                  stop=True).then_inc(S("lora_mm"), 1)

                def norm_spread(m):
                    pe.wait_ge(S("norm_inv"), m + 1)
                    for g in range(2):
                        pe.wait_ge(S("rate_gate"), 2 * m + g + 1)
                        pe.matmul(bank[4 * g + 3][:, 0:T], sel_t[:, P * g:P * g + P], NR[:, :], start=True,
                                  stop=True).then_inc(S("norm_spread"), 1)

                def output_gate(m):
                    for g in range(2):
                        pe.wait_ge(S("kk_ready"), 2 * m + g + 1)
                        pe.matmul(bank[4 * g + 3][:, 0:T], LW[g][:, 2, :], lo_g[:, 0, :], start=True, stop=False)
                        pe.matmul(bank[4 * g + 3][:, 0:T], LW[g][:, 3, :], lo_g[:, 1, :], start=False,
                                  stop=True).then_inc(S("gate_mm"), 1)

                def token_major(m):
                    for g in range(2):
                        pe.wait_ge(S("gate_ready"), 2 * m + g + 1)
                        pe.wait_ge(S(f"v_landed{g}"), 16 * m + 16)
                        pe.transpose(bank[4 * g + 3][:, 0:P], VS[g][:, 0:P], ident)
                        pe.transpose(bank[4 * g + 3][:, P:2 * P], VS[g][:, P:2 * P], ident)
                        pe.wait_ge(S("b_tilde"), 2 * m + g + 1)
                        pe.transpose(bank[4 * g + 3][:, 2 * P:3 * P], BT[g][:, 0, :], ident)
                        pe.wait_ge(S("k_tilde"), 2 * m + g + 1)
                        pe.transpose(bank[4 * g + 3][:, 3 * P:4 * P], KW[g][:, 0, :], ident).then_inc(S("turned"), 1)

                def bonus(m):
                    for g in range(2):
                        pe.wait_ge(S("bonus_in"), 2 * m + g + 1)
                        pe.matmul(bank[4 * g + 2][:, T:2 * T], bones, flat(SQ[g]), start=True, stop=True).then_inc(S("bonus_mm"), 1)

                def mean(k, g):
                    pe.wait_ge(S("y_ready"), 2 * k + g + 1)
                    pe.matmul(bank[4 * g + 3][:, 0:T], bones, YY[g][:, :], start=True, stop=True).then_inc(S("y_sum_mm"), 1)

                def variance(k):
                    for g in range(2):
                        pe.wait_ge(S("y_sq"), 2 * k + g + 1)
                        pe.matmul(bank[0][0:4, 0:T], sel[:, 4 * g:4 * g + 4], SY[g][:, :], start=g == 0,
                                  stop=g == 1).then_inc(S("y_var_mm"), 1)

                def output_spread(k):
                    pe.wait_ge(S("y_rstd"), k + 1)
                    for g in range(2):
                        pe.matmul(bank[4 * g + 3][:, 0:T], sel_t[:, P * g:P * g + P], YV[:, :], start=True,
                                  stop=True).then_inc(S("y_spread"), 1)

                def pair_products(m, side, k=None):
                    for g in range(2):
                        if k is not None:
                            pe.wait_ge(S("y_ready"), 2 * k + g + 1)
                        pe.wait_ge(S("a_tilde"), 2 * m + g + 1)
                        pe.wait_ge(S("r_tilde"), 2 * m + g + 1)
                        for c in range(2):
                            for h in range(2):
                                mm = pe.matmul(bank[4 * g + h][:, T * c:T * c + T], rows(BT[g], h)[:, c, :],
                                               rows(AR[side][g], h)[:, c, :, :].rearrange("p a b -> p (a b)"),
                                               start=True, stop=True)
                        mm.then_inc(S("attn_b"), 1)
                        if k is not None:
                            mean(k, g)
                    for g in range(2):
                        pe.wait_ge(S("bonus_ready"), 2 * m + g + 1)
                        pe.wait_ge(S("token_major"), 2 * m + g + 1)
                        if k is not None:
                            pe.wait_ge(S("y_centred"), 2 * k + g + 1)
                        for c in range(2):
                            for h in range(2):
                                mm = pe.matmul(bank[4 * g + 2 + h][:, T * c:T * c + T], rows(KW[g], h)[:, c, :],
                                               rows(AR[side][g], h)[:, c, :, :].rearrange("p a b -> p (a b)"),
                                               start=True, stop=True)
                        mm.then_inc(S("attn_k"), 1)
                    if k is not None:
                        pe.wait_ge(S("lm1_ready"), 4 * m + 2)
                        variance(k)
                    for g in range(2):
                        pe.wait_ge(S("u_ready"), 14 * m + g + 1)
                        for p in range(4):
                            mm = pe.transpose(bank[4 * g + 1][:, P * p:P * p + P], UI[g][:, p, :], ident)
                        mm.then_inc(S("t_mm"), 1)

                def turn(k, side, post, pre):
                    m = k + 1
                    tok, ar = TOK[side], AR[side]
                    for lev in range(len(LEVELS)):
                        if lev == 0 and post:
                            pe.wait_ge(S("y_std"), k)
                        for g in range(2):
                            pe.wait_ge(S("t_copied"), 12 * k + 2 * lev + g + 1)
                            for p in range(4):
                                mm = pe.matmul(bank[4 * g][:, P * p:P * p + P], LM1[g][:, p, 0:P], TI[g][:, p, :],
                                               start=True, stop=True)
                            mm.then_inc(S("x_mm"), 1)
                        if lev == 1 and post:
                            if pre:
                                pe.wait_ge(S("norm_ready"), m + 1)
                            output_spread(k - 1)
                        if lev == 5 and pre:
                            token_major(m)
                        for g in range(2):
                            pe.wait_ge(S("x_ready"), 12 * k + 2 * lev + g + 1)
                            pe.wait_ge(S("u_ready"), 14 * k + 2 * lev + g + 1)
                            if lev == 0:
                                pe.wait_ge(S("lm2_ready"), 4 * k + 2 * g + 2)
                            for p in range(4):
                                mm = pe.matmul(bank[4 * g + 1][:, P * p:P * p + P], XI[g][:, p, :], UI[g][:, p, :],
                                               start=True, stop=True)
                            mm.then_inc(S("u_mm"), 1)
                        for g in range(2):
                            if lev < len(LEVELS) - 1:
                                pe.wait_ge(S("u_ready"), 14 * k + 2 * lev + g + 3)
                                for p in range(4):
                                    mm = pe.transpose(bank[4 * g + 2][:, P * p:P * p + P], UI[g][:, p, :], ident)
                                mm.then_inc(S("t_mm"), 1)
                        if pre:
                            if lev == 0:
                                norm_sums(m)
                            elif lev == 1:
                                if post:
                                    pe.wait_ge(S("y_normed"), 2 * k)
                                lora(m)
                            elif lev == 2:
                                norm_spread(m)
                            elif lev == 3:
                                output_gate(m)
                            elif lev == 5:
                                bonus(m)
                    for c in range(2):
                        for g in range(2):
                            if c:
                                pe.wait_ge(S("state_ready"), 2 * k + g + 1)
                            elif pre:
                                pe.wait_ge(S("token_major"), 2 * m + g + 1)
                            else:
                                pe.wait_ge(S("y_normed"), 2 * k)
                            for h in range(2):
                                to = bank[4 * g + 3 - c * h][:, P * c + 64 * h:P * c + 64 * h + 64]
                                if c:
                                    pe.matmul(to, rows(ar[g], h)[:, 1, 0, :], rows(S0[g], h)[:, :], start=True, stop=False)
                                mm = pe.matmul(to, LM2[g][:, 2 * h + c, 0:P], tok[g][:, c, 64 * h:64 * h + 64],
                                               start=c == 0, stop=True)
                            mm.then_inc(S("rhs_mm"), 1)
                        for g in range(2):
                            pe.wait_ge(S("rhs_ready"), 6 * k + (2 * g + 4 if c else g + 1))
                            pe.wait_ge(S("u_ready"), 14 * k + 2 * len(LEVELS) + g + 1)
                            for h in range(2):
                                mm = pe.matmul(bank[4 * g][:, P * c + 64 * h:P * c + 64 * h + 64], UI[g][:, 2 * h + c, :],
                                               RH[g][:, 2 * c + h, :], start=True, stop=True)
                            mm.then_inc(S("sa_mm"), 1)
                        if c == 0:
                            for g in range(2):
                                pe.wait_ge(S("sa_ready"), 4 * k + g + 1)
                                if pre:
                                    pe.wait_ge(S("bonus_ready"), 2 * m + g + 1)
                                for h in range(2):
                                    to = bank[4 * g + 2][64 * h:64 * h + 64, 0:64]
                                    pe.matmul(to, tok[g][:, 2, 64 * h:64 * h + 64], SA[g][:, h, :], start=True, stop=False)
                                    mm = pe.matmul(to, tok[g][:, 3, 64 * h:64 * h + 64], tok[g][:, 0, 64 * h:64 * h + 64],
                                                   start=False, stop=True)
                                mm.then_inc(S("state_mm"), 1)
                        for g in range(2):
                            pe.wait_ge(S("sa_ready"), 4 * k + 2 * c + g + 1)
                            for h in range(2):
                                to = bank[4 * g + 1][64 * h:64 * h + 64, P * c:P * c + P]
                                p = 2 * h + c
                                pe.matmul(to, SA[g][:, 2 * c + h, :], LM1[g][:, p, P:2 * P], start=True, stop=False)
                                mm = pe.matmul(to, tok[g][:, c, 64 * h:64 * h + 64], LM2[g][:, p, P:2 * P],
                                               start=False, stop=c == 0)
                                if c:
                                    mm = pe.matmul(to, rows(S0[g], h)[:, :], rows(ar[g], h)[:, 1, 1, :],
                                                   start=False, stop=True)
                            mm.then_inc(S("y_mm"), 1)
                    if pre:
                        pair_products(m, 1 - side, k)
                    else:
                        mean(k, 0)
                        mean(k, 1)
                        variance(k)
                        output_spread(k)

                norm_sums(0)
                lora(0)
                norm_spread(0)
                output_gate(0)
                token_major(0)
                bonus(0)
                pair_products(0, 0)
                pair_turns(pe, turn)

            def turn_dt():
                pe.wait_ge(S("cs_ready"), 1)
                half = ident[0:HEADS, 0:HEADS]
                for c in range(2):
                    pe.transpose(bank[2][:, HEADS * c:HEADS * c + HEADS], dtc[:, P * c:P * c + P], half)
                for c in range(2):
                    mm = pe.transpose(bank[2][:, HEADS * (2 + c):HEADS * (3 + c)], cs[:, P * c:P * c + P], half)
                mm.then_inc(S("dt_turned"), 1)

            def ssd():
                pe.wait_ge(bank_free[0], (by["so"].out0 + 1) // 2 + CREDIT)
                pe.wait_ge(bank_free[1], by["so"].out0 // 2 + CREDIT)
                pe.wait_ge(S("dt_tokens"), 3)

                def prepare_group(k, post):
                    pe.wait_ge(S("bst_landed"), 16 * k + 16)
                    if post:
                        pe.wait_ge(S("cbm_ready"), k)
                    pe.matmul(bank[0][:, 0:T], BST[:, 0:P], BC[:, GROUPS + k, :], start=True, stop=True)
                    pe.matmul(bank[0][:, T:T + P], BST[:, P:T], BC[:, GROUPS + k, P:T], start=True,
                              stop=True).then_inc(S("cb_mm"), 1)
                    pe.wait_ge(S("xst_landed"), 16 * k + 16)
                    if post:
                        pe.wait_ge(S("xdt_ready"), 2 * k)
                    for c in range(2):
                        for t in range(4):
                            mm = pe.transpose(bank[1 + c][:, P * t:P * t + P], XST[:, t, P * c:P * c + P], ident)
                        mm.then_inc(S("x_turned"), 1)

                def square_sum(k, t):
                    pe.wait_ge(S("ys_sq"), 4 * k + t + 1)
                    pe.matmul(bank[7][:, 0:T], ones, SQS[t % 2][:, :], start=t == 0, stop=t == 3).then_inc(S("ys_sq_mm"), 1)

                def turn(k, post, more):
                    pe.wait_ge(S("xdt_ready"), 2 * k + 2)
                    for h in range(8):
                        if post and h % 2 == 0:
                            pe.wait_ge(S("ys_skip"), 4 * k + h // 2 - 3)
                        pe.wait_ge(S("g_ready"), 8 * k + h + 1)
                        half = 64 * (h % 2)
                        to = bank[3 + h // 2]
                        pe.matmul(to[half:half + 64, 0:T], XDT[:, 0, h, :], GE[h % 4][:, 0:T], start=True, stop=False)
                        pe.matmul(to[half:half + 64, P:T], XDT[:, 1, h, :], GE[h % 4][:, T:T + P], start=False,
                                  stop=True).then_inc(S("ssd_y_mm"), 1)
                        if post and h in (0, 1):
                            square_sum(k - 1, h + 2)
                        if more and h == 3:
                            prepare_group(k + 1, True)
                    square_sum(k, 0)
                    square_sum(k, 1)

                prepare_group(0, False)
                group_turns(pe, turn)
                square_sum(GROUPS - 1, 2)
                square_sum(GROUPS - 1, 3)

            pe.wait_ge(S("basic_landed"), 16)
            for name in ("r", "w1", "k", "v", "a1", "g1"):
                product(by[name], MIXED[name], counted("mix_low_" + name, CREDIT * (name in HIDDEN)))
            delta_rule()
            pe.wait_ge(S("y_normed"), KT)
            product(by["wo"], YR, counted("y_low"))
            layer_norm(0)
            product(by["up0"], XS, normed_split(0))
            product(by["down0"], HID, counted("hid_low", CREDIT))
            layer_norm(1)
            for name in ("x", "bc", "dt", "z"):
                product(by[name], XS, normed_split(1) if name == "x" else None)
            turn_dt()
            ssd()
            product(by["so"], YS, counted("ys_low", CREDIT))
            layer_norm(2)
            product(by["up1"], XS, normed_split(2))
            product(by["down1"], HID, counted("hid_low", NF + CREDIT))
            layer_norm(3)

        @block.vector
        def _(dve):
            def prepare(ph, s, k, turn):
                for i, (a, b) in enumerate(ph.halves):
                    dve.wait_ge(high_ready, 2 * s + i + 1 + k * (2 * turn))
                    dve.tensor_tensor(wsp[:, s % 2, 1, a:b], raw[:, s % RAW, a:b],
                                      wsp[:, s % 2, 0, a:b].bitcast(F32), ALU.subtract).then_inc(low_ready, 1)

            def mix(name, n, buf, after=None):
                mu = KT * MU[name] + n
                if after is not None:
                    dve.wait_ge(S("mix_low_" + name), after)
                dve.tensor_scalar(tmp[:, buf, :], H[:, n, :], omm[:, mu, :], None, ALU.mult).then_inc(S("mix_begun_" + name), 1)
                dve.wait_ge(S("mix_begun_" + name), n + 1)
                dve.scalar_tensor_tensor(out=tmp[:, buf, 1:T], in0=H[:, n, 0:T - 1], scalar=param("mu", mu),
                                         in1=tmp[:, buf, 1:T], op0=ALU.mult, op1=ALU.add).then_inc(S("mixed_" + name), 1)

            def mix_low(name, n, buf):
                dve.wait_ge(S("mix_high_" + name), n + 1)
                dve.tensor_tensor(MIXED[name][:, 1, n, :], tmp[:, buf, :], MIXED[name][:, 0, n, :].bitcast(F32),
                                  ALU.subtract).then_inc(S("mix_low_" + name), 1)

            def mix_all(name, between=nothing):
                mu = KT * MU[name]

                def low(n, j):
                    dve.wait_ge(S("mix_high_" + name), n + 1)
                    dve.tensor_tensor(MIXED[name][:, 1, n, :], mixb[:, j, :], MIXED[name][:, 0, n, :].bitcast(F32),
                                      ALU.subtract).then_inc(S("mix_low_" + name), 1)

                def four(k, first=False):
                    for j in range(4):
                        n = 4 * k + j
                        dve.wait_ge(S("mix_begun_" + name), n + 1)
                        dve.scalar_tensor_tensor(out=mixb[:, j, 1:T], in0=H[:, n, 0:T - 1], scalar=param("mu", mu + n),
                                                 in1=mixb[:, j, 1:T], op0=ALU.mult, op1=ALU.add).then_inc(S("mixed_" + name), 1)
                        if not (first and j == 0):
                            low(n - 1, (j - 1) % 4)

                four(0, first=True)
                between()
                with dve.Fori(1, KT // 4) as k:
                    four(k)
                low(KT - 1, 3)

            def mixing(names):
                def before(ph, j, k, u):
                    for i, name in enumerate(names):
                        mix(name, j + k * u, i, after=j + k * u + CREDIT)

                def after(ph, j, k, u):
                    for i, name in enumerate(names):
                        mix_low(name, j + k * u, i)
                return before, after

            def take_residual(ph, j, k, u):
                n = j + k * u
                out_wait(dve, ph, j, k, u)
                dve.scalar_tensor_tensor(out=H[:, n, :], in0=H[:, n, :], scalar=ALPHA, in1=out_bank(ph, j),
                                         op0=ALU.mult, op1=ALU.add).then_inc(free_sem(ph, j), 1)

            def take_up(layer):
                def take(ph, j, k, u):
                    if j % 2:
                        n = j // 2 + k * (u // 2)
                        out_wait(dve, ph, j, k, u)
                        dve.wait_ge(free_sem(ph, j - 1), freed(ph, j - 1, k, u))
                        dve.wait_ge(S("hid_low"), NF * layer + n + CREDIT)
                        dve.tensor_tensor(tmp[:, 1 + (j // 2) % 2, :], tmp[:, 0, :], out_bank(ph, j),
                                          ALU.mult).then_inc(free_sem(ph, j), 1)
                return take

            def layer_norm(i):
                dve.wait_ge(S("ln_sum"), i + 1)

                def centre(k):
                    for j in range(4):
                        n = 4 * k + j
                        dve.scalar_tensor_tensor(out=H[:, n, :], in0=bank[2][:, 0:T], scalar=-1.0 / D, in1=H[:, n, :],
                                                 op0=ALU.mult, op1=ALU.add).then_inc(S("ln_centred"), 1)

                loop(dve, KT // 4, centre)
                dve.wait_ge(S("ln_std"), i + 1)
                dve.reciprocal(tmp[:, 0, :], tmp[:, 0, :]).then_inc(S("ln_rstd"), 1)
                dve.wait_ge(S("ln_rstd"), i + 1)

                def low(k):
                    if i < 3:
                        n = 4 * k + 3
                        dve.wait_ge(S("ln_high"), KT * i + n + 1)
                        dve.tensor_tensor(XS[:, 1, n, :], H[:, n, :], XS[:, 0, n, :].bitcast(F32),
                                          ALU.subtract).then_inc(S("ln_low_fourth"), 1)

                def four(k, first=False):
                    for j in range(4):
                        n = 4 * k + j
                        dve.tensor_tensor(H[:, n, :], H[:, n, :], tmp[:, 0, :], ALU.mult).then_inc(S("ln_scaled"), 1)
                    for j in (1, 3):
                        n = 4 * k + j
                        dve.wait_ge(S("ln_scaled"), KT * i + n + 1)
                        dve.tensor_scalar(H[:, n, :], H[:, n, :], param("ln_g", KT * i + n), param("ln_b", KT * i + n),
                                          ALU.mult, ALU.add).then_inc(S("ln_odd"), 1)
                    if not first:
                        low(k - 1)

                four(0, first=True)
                with dve.Fori(1, KT // 4) as k:
                    four(k)
                low(KT // 4 - 1)

            def take_conv(tile0):
                def take(ph, j, k, u):
                    n = j + k * u
                    dve.wait_ge(S("conv_begun"), tile0 + n + 1)
                    for tap in (2, 1, 0):
                        lag = 3 - tap
                        d = tmp[:, j % 2, :]
                        if lag > 1:
                            dve.wait_ge(S("conv_tap"), 2 * (tile0 + n) + lag - 1)
                        i = dve.scalar_tensor_tensor(out=d[:, lag:T], in0=out_bank(ph, j)[:, 0:T - lag],
                                                     scalar=param("conv_w", tap * 48 + tile0 + n), in1=d[:, lag:T],
                                                     op0=ALU.mult, op1=ALU.add)
                        i.then_inc(S("conv_tap") if tap else free_sem(ph, j), 1)
                return take

            def take_dt(ph, j, k, u):
                bias = par[0:HEADS, PARAM_AT["dt_bias"], :]
                out_wait(dve, ph, j, k, u)
                dve.wait_ge(S("dt_abs"), 1)
                dve.tensor_scalar(dtc[:, :], out_bank(ph, j), bias, 0.0, ALU.add, ALU.max).then_inc(free_sem(ph, j), 1)
                dve.wait_ge(free_sem(ph, j), freed(ph, j, k, u))
                dve.wait_ge(S("dt_ln"), 1)
                dve.tensor_tensor(dtc[:, :], dtc[:, :], dtb[:, :], ALU.add).then_inc(S("dt_step"), 1)
                dve.wait_ge(S("dt_rate"), 1)
                dve.wait_ge(S("dt_step"), 1)
                dve.tensor_scalar(dta[:, :], dtc[:, :], aneg[:, 0:1], -1.0, ALU.mult, ALU.mult).then_inc(S("dt_step"), 1)
                dve.wait_ge(S("dt_step"), 2)
                for c in range(2):
                    dve.tensor_tensor_scan(cs[:, P * c:P * c + P], ones[0:HEADS, :], dta[:, P * c:P * c + P], 0.0,
                                           ALU.mult, ALU.add).then_inc(S("dt_step"), 1)
                dve.wait_ge(S("dt_step"), 4)
                dve.tensor_copy(aneg[:, 1:2], cs[:, P - 1:P]).then_inc(S("dt_step"), 1)
                dve.wait_ge(S("dt_step"), 5)
                dve.tensor_scalar(cs[:, 0:P], cs[:, 0:P], aneg[:, 1:2], None, ALU.subtract).then_inc(S("cs_ready"), 1)

            def delta_rule():
                dve.wait_ge(S("mask_landed"), 80)
                dve.wait_ge(S("basic_landed"), 16)
                for g in range(2):
                    dve.memset(SC[g][:, :, 0:1], 0.0).then_inc(S("scan_zeroed"), 1)
                dve.wait_ge(S("scan_zeroed"), 2)

                def bc(m, n):
                    return m.unsqueeze(1).broadcast_to([P, n, m.shape[-1]])

                def flat(x):
                    return x[:, :, :].rearrange("p a b -> p (a b)")

                def two(x):
                    return x.rearrange("p (a b) -> p a b", a=2)

                def four(x):
                    return x.rearrange("p (a b) -> p a b", a=4)

                def scaled_keys(m):
                    for g in range(2):
                        if beyond(m, 1):
                            dve.wait_ge(S("kka_ready"), 2 * m)
                            dve.wait_ge(S("a_tilde"), 2 * m)
                        dve.tensor_scalar(flat(KK[g]), K[:, 2 * m + g, :], param("k_k", 2 * m + g), None,
                                          ALU.mult).then_inc(S("key_scaled"), 1)

                def inverse_norms(m):
                    dve.wait_ge(S("norm_ready"), m + 1)
                    dve.tensor_scalar(NR[:, :], NR[:, :], 1e-12, None, ALU.max).then_inc(S("norm_floor"), 1)
                    dve.wait_ge(S("norm_floor"), m + 1)
                    dve.reciprocal(NR[:, :], NR[:, :]).then_inc(S("norm_inv"), 1)

                def scans(m):
                    for g in range(2):
                        dve.wait_ge(S("decay_gate"), 2 * m + g + 1)
                        if beyond(m, 1):
                            dve.wait_ge(S("decayed"), 8 * m)
                        for c in range(2):
                            dve.tensor_tensor_scan(SC[g][:, c, 1:P + 1], ones, SG[g][:, c, :], 0.0,
                                                   ALU.mult, ALU.add).then_inc(S("scanned"), 1)
                    for g in range(2):
                        dve.wait_ge(S("scanned"), 4 * m + 2 * g + 2)
                        for i, sign in enumerate((DECAY, -DECAY)):
                            dve.tensor_scalar(kb[:, g, i, :], SC[g][:, :, 64], sign, None, ALU.mult).then_inc(S("mid_ready"), 1)

                def normed_keys(m):
                    for g in range(2):
                        dve.wait_ge(S("norm_spread"), 2 * m + g + 1)
                        dve.wait_ge(S("key_scaled"), 2 * m + g + 1)
                        dve.tensor_tensor(flat(KK[g]), flat(KK[g]), bank[4 * g + 3][:, 0:T], ALU.mult).then_inc(S("kk_ready"), 1)

                def rate_factors(m):
                    for g in range(2):
                        dve.wait_ge(S("rate_gate"), 2 * m + g + 1)
                        dve.wait_ge(S("scanned"), 4 * m + 2 * g + 2)
                        dve.tensor_scalar(flat(SG[g]), AA[g][:, :], param("k_a", 2 * m + g), omka[:, 2 * m + g, :],
                                          ALU.mult, ALU.add).then_inc(S("rate_factor"), 1)

                def rates(m):
                    for g in range(2):
                        dve.wait_ge(S("decayed"), 8 * m + 4 * g + 4)
                        dve.wait_ge(S("kka_ready"), 2 * m + g + 1)
                        dve.tensor_tensor(BT[g][:, :, :], SQ[g][:, :, :], EI[g][:, :, 1:P + 1], ALU.mult).then_inc(S("b_tilde"), 1)
                    for g in range(2):
                        dve.wait_ge(S("key_ready"), 2 * m + g + 1)
                        dve.tensor_tensor(KW[g][:, :, :], SG[g][:, :, :], EI[g][:, :, 1:P + 1], ALU.mult).then_inc(S("k_tilde"), 1)

                def bonus_inputs(m):
                    for g in range(2):
                        dve.wait_ge(S("b_tilde"), 2 * m + g + 1)
                        dve.scalar_tensor_tensor(out=flat(SQ[g]), in0=R[:, 2 * m + g, :], scalar=param("r_k", 2 * m + g),
                                                 in1=flat(SG[g]), op0=ALU.mult, op1=ALU.mult).then_inc(S("bonus_in"), 1)

                def bonuses(m, side):
                    for g in range(2):
                        dve.wait_ge(S("bonus_mm"), 2 * m + g + 1)
                        dve.wait_ge(S(f"v_landed{g}"), 16 * m + 16)
                        if beyond(m, 2):
                            dve.wait_ge(S("y_bonus"), 2 * m - 2)
                        dve.tensor_tensor(BV[side][g][:, :], bank[4 * g + 2][:, T:2 * T], VS[g][:, :],
                                          ALU.mult).then_inc(S("bonus_ready"), 1)
                    for g in range(2):
                        dve.tensor_tensor(dsc[:, 2 * side + g, :], EE[g][:, 0, P:P + 1], EI[g][:, 1, 0:1],
                                          ALU.mult).then_inc(S("carry"), 1)
                        dve.scalar_tensor_tensor(out=AR[side][g][:, :, 0, :], in0=KK[g][:, :, :], scalar=-1.0,
                                                 in1=EE[g][:, :, 0:P], op0=ALU.mult, op1=ALU.mult).then_inc(S("a_tilde"), 1)

                def pair_products(m, k=None):
                    pairs = bc(pair_mask[:, :], 2)
                    for g in range(2):
                        dve.wait_ge(S("attn_b"), 2 * m + g + 1)
                        for h in range(2):
                            dve.tensor_tensor(LM1[g][:, 2 * h:2 * h + 2, :], two(bank[4 * g + h][:, :]), pairs,
                                              ALU.mult).then_inc(S("lm1_ready"), 1)
                        if k is not None:
                            centre(k, g)
                    for g in range(2):
                        dve.wait_ge(S("lm1_ready"), 4 * m + 2 * g + 2)
                        dve.tensor_tensor(UI[g][:, :, :], LM1[g][:, :, 0:P], bc(first_mask[:, :], 4), ALU.mult).then_inc(S("u_begun"), 1)
                        dve.wait_ge(S("u_begun"), 2 * m + g + 1)
                        dve.tensor_tensor(UI[g][:, :, :], UI[g][:, :, :], bc(ident, 4), ALU.add).then_inc(S("u_ready"), 1)
                    for g in range(2):
                        dve.wait_ge(S("attn_k"), 2 * m + g + 1)
                        for h in range(2):
                            dve.tensor_tensor(LM2[g][:, 2 * h:2 * h + 2, :], two(bank[4 * g + 2 + h][:, :]), pairs,
                                              ALU.mult).then_inc(S("lm2_ready"), 1)

                def centre(k, g):
                    dve.wait_ge(S("y_sum_mm"), 2 * k + g + 1)
                    if beyond(k, 1):
                        dve.wait_ge(S("y_low"), 2 * k)
                    dve.scalar_tensor_tensor(out=YC[g][:, :], in0=bank[4 * g + 3][:, 0:T], scalar=-1.0 / 64, in1=YY[g][:, :],
                                             op0=ALU.mult, op1=ALU.add).then_inc(S("y_centred"), 1)

                def inverse_deviations(k):
                    dve.wait_ge(S("y_std"), k + 1)
                    dve.reciprocal(YV[:, :], YV[:, :]).then_inc(S("y_rstd"), 1)

                def normed(k):
                    for g in range(2):
                        dve.wait_ge(S("y_spread"), 2 * k + g + 1)
                        dve.tensor_tensor(YC[g][:, :], YC[g][:, :], bank[4 * g + 3][:, 0:T], ALU.mult).then_inc(S("y_normed"), 1)

                def affine(k):
                    for g in range(2):
                        dve.wait_ge(S("y_normed"), 2 * k + g + 1)
                        dve.tensor_scalar(YC[g][:, :], YC[g][:, :], param("gn_g", 2 * k + g), param("gn_b", 2 * k + g),
                                          ALU.mult, ALU.add).then_inc(S("y_affine"), 1)

                def turn(k, side, post, pre):
                    m = k + 1
                    for lev in range(len(LEVELS)):
                        for g in range(2):
                            dve.wait_ge(S("x_mm"), 12 * k + 2 * lev + g + 1)
                            dve.tensor_tensor(XI[g][:, :, :], four(bank[4 * g][:, :]), bc(level_mask[:, lev, :], 4),
                                              ALU.mult).then_inc(S("x_ready"), 1)
                        if post and lev == 1:
                            normed(k - 1)
                        if post and lev == 2:
                            affine(k - 1)
                        if pre:
                            if lev == 0:
                                scaled_keys(m)
                            elif lev == 3:
                                normed_keys(m)
                            elif lev == 5:
                                bonus_inputs(m)
                        for g in range(2):
                            dve.wait_ge(S("u_mm"), 12 * k + 2 * lev + g + 1)
                            dve.tensor_tensor(UI[g][:, :, :], UI[g][:, :, :], four(bank[4 * g + 1][:, :]),
                                              ALU.add).then_inc(S("u_ready"), 1)
                        if post and lev == 0:
                            inverse_deviations(k - 1)
                        if pre:
                            if lev == 1:
                                inverse_norms(m)
                            elif lev == 2:
                                scans(m)
                            elif lev == 3:
                                rate_factors(m)
                            elif lev == 4:
                                rates(m)
                            elif lev == 5:
                                bonuses(m, 1 - side)
                    for g in range(2):
                        dve.wait_ge(S("state_mm"), 2 * k + g + 1)
                        dve.wait_ge(S("carry"), 2 * k + g + 1)
                        dve.tensor_scalar(S0[g][:, :], bank[4 * g + 2][:, 0:64], dsc[:, 2 * side + g, :], None,
                                          ALU.mult).then_inc(S("state_ready"), 1)
                    if pre:
                        pair_products(m, k)
                    else:
                        centre(k, 0)
                        centre(k, 1)
                        inverse_deviations(k)
                        normed(k)
                        affine(k)

                scaled_keys(0)
                inverse_norms(0)
                scans(0)
                normed_keys(0)
                rate_factors(0)
                rates(0)
                bonus_inputs(0)
                bonuses(0, 0)
                pair_products(0)
                pair_turns(dve, turn)

            def ssd():
                dve.wait_ge(S("smask_landed"), 16)
                dve.wait_ge(S("dt_tokens"), 3)

                def skip(k, t, first=False):
                    n = 4 * k + t
                    if not first:
                        dve.wait_ge(S("ys_gated"), n - 1)
                    dve.wait_ge(S("ssd_y_mm"), 8 * k + 2 * t + 2)
                    dve.scalar_tensor_tensor(out=tmp[:, t % 2, :], in0=XC[:, n, :], scalar=param("d_skip", n),
                                             in1=bank[3 + t][:, 0:T], op0=ALU.mult, op1=ALU.add).then_inc(S("ys_skip"), 1)

                def seg(k, h, wait):
                    dve.wait_ge(S(f"csb_landed{h // 4}"), 16 * k + 16)
                    if wait:
                        dve.wait_ge(S("ssd_y_mm"), 8 * k + h - 3)
                    dve.tensor_scalar(GE[h % 4][:, 0:T], CSB[:, h, :], ncs[:, 0, 8 * k + h, :], 0.0, ALU.add,
                                      ALU.min).then_inc(S("seg_even"), 1)
                    dve.tensor_scalar(GE[h % 4][:, T:T + P], CSB[:, h, P:T], ncs[:, 1, 8 * k + h, :], 0.0, ALU.add,
                                      ALU.min).then_inc(S("seg_even"), 1)

                def inverse(k):
                    dve.wait_ge(S("ys_std"), k + 1)
                    dve.reciprocal(RST[:, :], RST[:, :]).then_inc(S("ys_rstd"), 1)

                def normed(k, t):
                    n = 4 * k + t
                    dve.wait_ge(S("ys_rstd"), k + 1)
                    dve.scalar_tensor_tensor(out=YN[:, t, :], in0=Z[:, n, :], scalar=param("norm_g", n), in1=RST[:, :],
                                             op0=ALU.mult, op1=ALU.mult).then_inc(S("ys_normed"), 1)

                def turn(k, post, more):
                    seg(k, 0, post)
                    seg(k, 2, post)
                    if post:
                        dve.wait_ge(S("g_ready"), 8 * k)
                    dve.wait_ge(S("cb_mm"), k + 1)
                    dve.tensor_tensor(CBM[:, :], bank[0][:, 0:3 * P], smask[:, :], ALU.mult).then_inc(S("cbm_ready"), 1)
                    if post:
                        skip(k - 1, 3)
                    for c in range(2):
                        dve.wait_ge(S("x_turned"), 2 * k + c + 1)
                        dve.tensor_tensor(XDT[:, c, :, :], bank[1 + c][:, :].rearrange("p (h d) -> p h d", h=8),
                                          dtt[:, c, :, :].rearrange("p (g h) o -> p g h o", g=GROUPS)[:, k, :, :].broadcast_to([P, 8, 64]),
                                          ALU.mult).then_inc(S("xdt_ready"), 1)
                    dve.wait_ge(S("cbm_ready"), k + 1)
                    for h in range(8):
                        dve.wait_ge(S("ge_ready"), 8 * k + h + 1)
                        dve.tensor_tensor(GE[h % 4][:, :], GE[h % 4][:, :], CBM[:, :], ALU.mult).then_inc(S("g_ready"), 1)
                        if h in (1, 3):
                            seg(k, h + 3, True)
                        if h in (3, 5, 7):
                            skip(k, (h - 3) // 2, first=not post and h < 7)
                        if post and h == 4:
                            inverse(k - 1)
                        if post and h >= 5:
                            if h == 5:
                                dve.wait_ge(S("ys_low"), 4 * k - 4 + CREDIT)
                                normed(k - 1, 0)
                            normed(k - 1, h - 4)

                group_turns(dve, turn)
                skip(GROUPS - 1, 3)
                inverse(GROUPS - 1)
                dve.wait_ge(S("ys_low"), 4 * GROUPS - 4 + CREDIT)
                for t in range(4):
                    normed(GROUPS - 1, t)

            for i, e in enumerate((LN_EPS, GN_EPS, RMS_EPS, 1.0)):
                dve.memset(eps[:, i, :], e).then_inc(S("eps_set"), 1)
            dve.wait_ge(S("par_landed"), 16)
            for dst, name, n in ((omm, "mu", 6 * KT), (omka, "k_a", KT)):
                dve.tensor_scalar(dst[:, :, 0], par[:, PARAM_AT[name]:PARAM_AT[name] + n, 0], -1.0, 1.0, ALU.mult,
                                  ALU.add).then_inc(S("one_minus"), 1)
            dve.wait_ge(S("one_minus"), 2)
            dve.wait_ge(S("eps_set"), 4)
            dve.wait_ge(S("x_landed"), 16)
            mix_all("r", between=lambda: prepare(by["r"], 0, 0, 0))
            prepare(by["r"], 1, 0, 0)
            for name, later in (("r", ["k", "w1"]), ("w1", []), ("k", ["v"]), ("v", ["a1"])):
                if later and name != "r":
                    dve.wait_ge(S("mix_low_" + name), KT + CREDIT)
                before, after = mixing(later)
                run_phase(dve, by[name], prepare, nothing, before, after)
            dve.wait_ge(S("mix_low_a1"), KT + CREDIT)
            mix_all("g1")
            run_phase(dve, by["a1"], prepare, nothing)
            run_phase(dve, by["g1"], prepare, nothing, until=by["wo"].slab0)
            delta_rule()
            prepare(by["wo"], by["wo"].slab0, 0, 0)
            dve.wait_ge(S("y_low"), KT)
            prepare(by["wo"], by["wo"].slab0 + 1, 0, 0)
            run_phase(dve, by["wo"], prepare, take_residual)
            layer_norm(0)
            run_phase(dve, by["up0"], prepare, take_up(0))
            run_phase(dve, by["down0"], prepare, take_residual)
            layer_norm(1)
            run_phase(dve, by["x"], prepare, take_conv(0))
            run_phase(dve, by["bc"], prepare, take_conv(NX))
            run_phase(dve, by["dt"], prepare, take_dt)
            run_phase(dve, by["z"], prepare, nothing)
            ssd()
            run_phase(dve, by["so"], prepare, take_residual)
            layer_norm(2)
            run_phase(dve, by["up1"], prepare, take_up(1))
            run_phase(dve, by["down1"], prepare, take_residual)
            layer_norm(3)

        @block.gpsimd
        def _(pool):
            def apart():
                pool.wait_ge(S("par_landed"), 16)

            def add_up(ph, i):
                pool.wait_ge(slab_done, ph.slab0)
                pool.memset(tmp[:, 0, :], 0.0).then_inc(S("acc_zeroed"), 1)
                pool.wait_ge(S("acc_zeroed"), i + 1)

                def body(k):
                    for j in range(2):
                        n = 2 * k + j
                        pool.wait_ge(free_sem(ph, j), freed(ph, j, k, 2))
                        pool.wait_ge(S("ln_acc"), KT * i + n + CREDIT)
                        apart()
                        pool.tensor_tensor(tmp[:, 0, :], tmp[:, 0, :], H[:, n, :], ALU.add).then_inc(S("ln_acc"), 1)

                loop(pool, KT // 2, body)

            def low_of_norm(i):
                def body(k):
                    for j in range(3):
                        n = 4 * k + j
                        pool.wait_ge(S("ln_high"), KT * i + n + 1)
                        apart()
                        pool.tensor_tensor(XS[:, 1, n, :], H[:, n, :], XS[:, 0, n, :].bitcast(F32),
                                           ALU.subtract).then_inc(S("ln_low"), 1)

                loop(pool, KT // 4, body)

            def low_of_hidden(layer):
                def body(k):
                    for j in range(2):
                        n = 2 * k + j
                        pool.wait_ge(S("hid_high"), NF * layer + n + 1)
                        apart()
                        pool.tensor_tensor(HID[:, 1, n, :], tmp[:, 1 + j, :], HID[:, 0, n, :].bitcast(F32),
                                           ALU.subtract).then_inc(S("hid_low"), 1)

                loop(pool, NF // 2, body)

            def delta_rule():
                def flat(x):
                    return x[:, :, :].rearrange("p a b -> p (a b)")

                def rates(m):
                    for g in range(2):
                        pool.wait_ge(S("kk_ready"), 2 * m + g + 1)
                        pool.wait_ge(S("rate_gate"), 2 * m + g + 1)
                        pool.tensor_tensor(flat(SQ[g]), flat(KK[g]), AA[g][:, :], ALU.mult).then_inc(S("kka_ready"), 1)

                def keys(m, side):
                    for g in range(2):
                        pool.wait_ge(S("rate_factor"), 2 * m + g + 1)
                        apart()
                        pool.tensor_tensor(flat(SG[g]), K[:, 2 * m + g, :], flat(SG[g]), ALU.mult).then_inc(S("key_ready"), 1)
                    for g in range(2):
                        pool.wait_ge(S("decayed"), 8 * m + 4 * g + 4)
                        apart()
                        pool.tensor_tensor(AR[side][g][:, :, 1, :], R[:, 2 * m + g, :].rearrange("p (a b) -> p a b", a=2),
                                           EE[g][:, :, 1:P + 1], ALU.mult).then_inc(S("r_tilde"), 1)

                def gated(k, side):
                    for g in range(2):
                        pool.wait_ge(S("y_affine"), 2 * k + g + 1)
                        pool.wait_ge(S("bonus_ready"), 2 * k + g + 1)
                        pool.tensor_tensor(YC[g][:, :], YC[g][:, :], BV[side][g][:, :], ALU.add).then_inc(S("y_bonus"), 1)
                    for g in range(2):
                        pool.wait_ge(S("gate_ready"), 2 * k + g + 1)
                        pool.wait_ge(S("y_bonus"), 2 * k + g + 1)
                        pool.tensor_tensor(YC[g][:, :], YC[g][:, :], GG[side][g][:, :], ALU.mult).then_inc(S("y_gated"), 1)

                def low(k):
                    for g in range(2):
                        pool.wait_ge(S("y_high"), 2 * k + g + 1)
                        apart()
                        pool.tensor_tensor(YR[:, 1, 2 * k + g, :], YC[g][:, :], YR[:, 0, 2 * k + g, :].bitcast(F32),
                                           ALU.subtract).then_inc(S("y_low"), 1)

                def turn(k, side, post, pre):
                    if post:
                        gated(k - 1, 1 - side)
                    if pre:
                        rates(k + 1)
                    if post:
                        low(k - 1)
                    if pre:
                        keys(k + 1, 1 - side)

                rates(0)
                keys(0, 0)
                pair_turns(pool, turn)
                gated(PAIRS - 1, (PAIRS - 1) % 2)
                low(PAIRS - 1)

            def ssd():
                def gated(k, t):
                    n = 4 * k + t
                    pool.wait_ge(S("ys_skip"), n + 1)
                    apart()
                    pool.tensor_tensor(Z[:, n, :], tmp[:, t % 2, :], Z[:, n, :], ALU.mult).then_inc(S("ys_gated"), 1)

                def low(k):
                    for t in range(4):
                        n = 4 * k + t
                        pool.wait_ge(S("ys_high"), n + 1)
                        apart()
                        pool.tensor_tensor(YS[:, 1, n, :], YN[:, t, :], YS[:, 0, n, :].bitcast(F32),
                                           ALU.subtract).then_inc(S("ys_low"), 1)

                def turn(k, post, more):
                    if post:
                        gated(k - 1, 3)
                    for t in range(3):
                        gated(k, t)
                    if post:
                        low(k - 1)

                group_turns(pool, turn)
                gated(GROUPS - 1, 3)
                low(GROUPS - 1)

            mixes = ["mix_low_" + name for name in HIDDEN]
            for sem in (*bank_free, *map(S, ("ys_low", "ln_acc", "hid_low", *mixes))):
                pool.sem_inc(sem, CREDIT)
            delta_rule()
            add_up(by["wo"], 0)
            low_of_norm(0)
            low_of_hidden(0)
            add_up(by["down0"], 1)
            low_of_norm(1)
            ssd()
            pool.wait_ge(S("ys_gated"), NX)
            add_up(by["so"], 2)
            low_of_norm(2)
            low_of_hidden(1)
            add_up(by["down1"], 3)


def kernel(**inputs):
    import numpy as np
    import concourse.bacc as bacc
    from concourse.bass_utils import run_bass_kernel_spmd as run

    a = {name: np.asarray(v) for name, v in inputs.items()}

    def slabs(w, per=1, width=P):
        rows, cols = w.shape
        tiles = rows // P // per
        v = w.reshape(per, tiles, P, cols // width, width)
        return np.ascontiguousarray(v.transpose(3, 0, 2, 1, 4)).reshape(-1, P, tiles * width)

    def cols(v):
        return v.reshape(-1, P).T

    def interleaved(w):
        half = w.shape[1] // 2 // P
        return w.reshape(D, 2, half, P).transpose(0, 2, 1, 3).reshape(D, -1)

    basic, chunk, ssd_mask, sel, sel_t = shape_constants()
    pad = np.zeros(P - HEADS, np.float32)
    lora2 = np.zeros((KT, P, 4, P), np.float32)
    lora2[:, :LORA, 0] = a["rwkv_w2"].reshape(LORA, KT, P).transpose(1, 0, 2)
    lora2[:, :LORA, 1] = a["rwkv_a2"].reshape(LORA, KT, P).transpose(1, 0, 2)
    lora2[:, :, 2:] = a["rwkv_g2"].reshape(2, P, KT, P).transpose(2, 1, 0, 3)
    params = np.concatenate([
        cols(a["rwkv_mu"]), cols(a["rwkv_w0"]), cols(a["rwkv_a0"]), cols(a["rwkv_k_k"]), cols(a["rwkv_k_a"]),
        cols(a["rwkv_r_k"]), cols(a["rwkv_ln_g"]), cols(a["rwkv_ln_b"]), cols(a["ssd_conv_w"]), cols(a["ssd_conv_b"]),
        cols(a["ssd_norm_g"]), cols(np.repeat(a["ssd_d"], 64)), cols(a["ln_g"]), cols(a["ln_b"]),
        cols(np.concatenate([a["ssd_dt_bias"], pad])), cols(np.concatenate([a["ssd_a_log"], pad]))], axis=1)
    w_ssd = a["ssd_w_in"]
    n_inner = NX * P
    arrays = {
        "x_cm": a["x"][0].T.reshape(KT, P, T).transpose(1, 0, 2),
        "params": params, "basic": basic, "pair_mask": chunk[:, :2 * P],
        "first_mask": chunk[:, 2 * P:3 * P], "level_mask": chunk[:, 3 * P:].reshape(P, -1, P),
        "sel": sel, "sel_t": sel_t,
        "ssd_mask": ssd_mask, "lora2": lora2,
        "w_r": slabs(a["rwkv_w_in"][0]), "w_k": slabs(a["rwkv_w_in"][1]), "w_v": slabs(a["rwkv_w_in"][2]),
        "w_w1": slabs(a["rwkv_w1"], width=LORA), "w_a1": slabs(a["rwkv_a1"], width=LORA), "w_g1": slabs(a["rwkv_g1"]),
        "w_ro": slabs(a["rwkv_w_out"]),
        "w_z": slabs(w_ssd[:, :n_inner]), "w_x": slabs(w_ssd[:, n_inner:2 * n_inner]),
        "w_bc": slabs(w_ssd[:, 2 * n_inner:-HEADS]), "w_dt": slabs(w_ssd[:, -HEADS:], width=HEADS),
        "w_so": slabs(a["ssd_w_out"], per=2),
    }
    for layer in range(DEPTH):
        arrays[f"w_up{layer}"] = slabs(interleaved(a["ffn_w_in"][layer]))
        arrays[f"w_down{layer}"] = slabs(a["ffn_w_out"][layer], per=4)
    arrays = {name: np.ascontiguousarray(v) for name, v in arrays.items()}

    nc = bacc.Bacc("TRN2", target_bir_lowering=False, num_devices=1)
    inp = {name: nc.dram_tensor(name, v.shape, F32, kind="ExternalInput").ap() for name, v in arrays.items()}
    out = nc.dram_tensor("out", (P, KT, T), F32, kind="ExternalOutput").ap()
    build(nc, inp, out)
    r = run(nc, [arrays], core_ids=[0])
    return r.results[0]["out"].transpose(1, 0, 2).reshape(D, T).T.reshape(1, T, D)
```
